# Optimizing a Trainium2 kernel written in Bass

```python
import math
import jax, jax.numpy as jnp
from jax import lax
import numpy as np

D_MODEL = 1024
BATCH = 1
SEQ = 256
DEPTH = 1

MOBA_HEADS = 8
MOBA_HEAD_DIM = 128
MOBA_BLOCK = 256
MOBA_TOPK = 3
MOBA_Q_CHUNK = 64
DN_HEADS = 8
DN_HEAD_DIM = 128
DN_CONV = 4
DN_CHUNK = 64
MEM_LEN = 256
MEM_HEADS = 4
MEM_HEAD_DIM = 256
N_BRANCHES = 3
BRANCH_W = 1024
PEER_HEADS = 8
PEER_N_KEYS = 128
PEER_N_EXPERTS = PEER_N_KEYS * PEER_N_KEYS
PEER_QUERY_DIM = 256
PEER_TOPK = 16
PEER_TOKEN_CHUNK = 128

ROPE_THETA = 10000.0
EPS = 1e-6

MOBA_W = MOBA_HEADS * MOBA_HEAD_DIM
DN_W = DN_HEADS * DN_HEAD_DIM
MEM_W = MEM_HEADS * MEM_HEAD_DIM
IN_SIZES = (3 * MOBA_W, 3 * DN_W, DN_HEADS, DN_HEADS, DN_W, MEM_W, N_BRANCHES * D_MODEL)
IN_WIDTH = 3 * MOBA_W + 3 * DN_W + 2 * DN_HEADS + DN_W + MEM_W + N_BRANCHES * D_MODEL

kernel_name = "hybrid_moba_deltanet_mem_peer"

def rms_norm(x, g):
    xf = x.astype(jnp.float32)
    y = xf * lax.rsqrt(jnp.mean(xf * xf, axis=-1, keepdims=True) + EPS)
    return (y * g.astype(jnp.float32)).astype(x.dtype)

def l2_norm(x):
    xf = x.astype(jnp.float32)
    return xf * lax.rsqrt(jnp.sum(xf * xf, axis=-1, keepdims=True) + EPS)

def rope(x, pos):
    hd = x.shape[-1]
    inv = 1.0 / (ROPE_THETA ** (jnp.arange(0, hd, 2, dtype=jnp.float32) / hd))
    ang = pos.astype(jnp.float32)[:, None] * inv[None, :]
    cos, sin = jnp.cos(ang), jnp.sin(ang)
    xf = x.astype(jnp.float32)
    x1, x2 = xf[..., : hd // 2], xf[..., hd // 2:]
    return jnp.concatenate([x1 * cos - x2 * sin, x2 * cos + x1 * sin], axis=-1).astype(x.dtype)

def split_heads(t, n_heads):
    B, S, _ = t.shape
    return t.reshape(B, S, n_heads, -1).transpose(0, 2, 1, 3)

def merge_heads(t):
    B, H, S, hd = t.shape
    return t.transpose(0, 2, 1, 3).reshape(B, S, H * hd)

def causal_depthwise_conv(x, w):
    K, C = w.shape
    return lax.conv_general_dilated(x, w[:, None, :], window_strides=(1,), padding=[(K - 1, 0)],
                                    dimension_numbers=('NWC', 'WIO', 'NWC'), feature_group_count=C)

def moba_attention(q, k, v):
    B, H, S, hd = q.shape
    L = MOBA_BLOCK
    nb = -(-S // L)
    k_sel = min(MOBA_TOPK, nb)
    pad = ((0, 0), (0, 0), (0, nb * L - S), (0, 0))
    kb = jnp.pad(k, pad).reshape(B, H, nb, L, hd)
    vb = jnp.pad(v, pad).reshape(B, H, nb, L, hd)
    scale = hd ** -0.5
    pos = jnp.arange(S)
    q_blk = pos // L
    k_mean = jnp.mean(kb.astype(jnp.float32), axis=3)
    gate = jnp.einsum('bhsd,bhnd->bhsn', q.astype(jnp.float32), k_mean)
    fully_past = jnp.arange(nb)[None, :] < q_blk[:, None]
    gate = jnp.where(fully_past, gate, -jnp.inf)
    _, sel = lax.top_k(gate, k_sel)
    valid = jnp.arange(k_sel)[None, :] < q_blk[:, None]

    C = MOBA_Q_CHUNK
    nc = S // C
    bi = jnp.arange(B)[:, None, None]
    hi = jnp.arange(H)[None, :, None]

    def to_chunks(a):
        a = a.reshape(B, H, nc, C, *a.shape[3:])
        return jnp.moveaxis(a, 2, 0)

    def one_chunk(args):
        q_c, sel_c, valid_c, c = args
        t = c * C + jnp.arange(C)
        own = (c * C) // L
        k_own = lax.dynamic_index_in_dim(kb, own, axis=2, keepdims=False)
        v_own = lax.dynamic_index_in_dim(vb, own, axis=2, keepdims=False)
        key_pos = own * L + jnp.arange(L)
        s_own = jnp.einsum('bhcd,bhld->bhcl', q_c, k_own).astype(jnp.float32) * scale
        s_own = jnp.where(key_pos[None, :] <= t[:, None], s_own, -jnp.inf)
        scores = []
        for j in range(k_sel):
            k_j = kb[bi, hi, sel_c[..., j]]
            s_j = jnp.einsum('bhcd,bhcld->bhcl', q_c, k_j).astype(jnp.float32) * scale
            scores.append(jnp.where(valid_c[:, j][:, None], s_j, -jnp.inf))
        p = jax.nn.softmax(jnp.concatenate(scores + [s_own], axis=-1), axis=-1).astype(v.dtype)
        p = p.reshape(B, H, C, k_sel + 1, L)
        out = jnp.einsum('bhcl,bhld->bhcd', p[..., k_sel, :], v_own)
        for j in range(k_sel):
            v_j = vb[bi, hi, sel_c[..., j]]
            out = out + jnp.einsum('bhcl,bhcld->bhcd', p[..., j, :], v_j)
        return out

    out = lax.map(one_chunk, (to_chunks(q), to_chunks(sel), valid.reshape(nc, C, k_sel), jnp.arange(nc)))
    return jnp.moveaxis(out, 0, 2).reshape(B, H, S, hd)

def gated_delta_rule(q, k, v, g, beta):
    B, H, S, dk = q.shape
    dv = v.shape[-1]
    C = DN_CHUNK
    n = S // C
    f32 = jnp.float32
    q = q.astype(f32).reshape(B, H, n, C, dk)
    k = k.astype(f32).reshape(B, H, n, C, dk)
    v = v.astype(f32).reshape(B, H, n, C, dv)
    g = jnp.cumsum(g.astype(f32).reshape(B, H, n, C), axis=-1)
    beta = beta.astype(f32).reshape(B, H, n, C)
    incl = jnp.tril(jnp.ones((C, C), dtype=bool))
    strict = jnp.tril(jnp.ones((C, C), dtype=bool), k=-1)
    gdiff = g[..., :, None] - g[..., None, :]
    decay = jnp.where(incl, jnp.exp(jnp.where(incl, gdiff, 0.0)), 0.0)
    k_beta = k * beta[..., None]
    v_beta = v * beta[..., None]
    lower = jnp.where(strict, jnp.einsum('bhncd,bhnmd->bhncm', k_beta, k) * decay, 0.0)
    a_mat = lower + jnp.eye(C, dtype=f32)
    rhs = jnp.concatenate([v_beta, k_beta * jnp.exp(g)[..., None]], axis=-1)
    sol = lax.linalg.triangular_solve(a_mat, rhs, left_side=True, lower=True, unit_diagonal=True)
    u = sol[..., :dv]
    w = sol[..., dv:]
    attn_intra = jnp.where(incl, jnp.einsum('bhncd,bhnmd->bhncm', q, k) * decay, 0.0)

    def step(state, xs):
        q_i, k_i, u_i, w_i, g_i, a_i = xs
        v_new = u_i - jnp.einsum('bhcd,bhde->bhce', w_i, state)
        o = (jnp.einsum('bhcd,bhde->bhce', q_i * jnp.exp(g_i)[..., None], state)
             + jnp.einsum('bhcm,bhme->bhce', a_i, v_new))
        g_last = g_i[..., -1]
        state = (state * jnp.exp(g_last)[..., None, None]
                 + jnp.einsum('bhcd,bhce->bhde', k_i * jnp.exp(g_last[..., None] - g_i)[..., None], v_new))
        return state, o

    xs = tuple(jnp.moveaxis(a, 2, 0) for a in (q, k, u, w, g, attn_intra))
    _, o = lax.scan(step, jnp.zeros((B, H, dk, dv), f32), xs)
    return jnp.moveaxis(o, 0, 2).reshape(B, H, S, dv)

def peer_ffn(h, w_q, keys1, keys2, u, v):
    B, S, D = h.shape
    T = B * S
    Hh, K = PEER_HEADS, PEER_TOPK
    hf = h.reshape(T, D)
    q = (hf @ w_q).astype(jnp.float32).reshape(T, Hh, 2, PEER_QUERY_DIM // 2)
    s1 = jnp.einsum('thd,nd->thn', q[:, :, 0], keys1.astype(jnp.float32))
    s2 = jnp.einsum('thd,nd->thn', q[:, :, 1], keys2.astype(jnp.float32))
    v1, i1 = lax.top_k(s1, K)
    v2, i2 = lax.top_k(s2, K)
    cand = (v1[..., :, None] + v2[..., None, :]).reshape(T, Hh, K * K)
    sc, ci = lax.top_k(cand, K)
    experts = (jnp.take_along_axis(i1, ci // K, axis=-1) * PEER_N_KEYS
               + jnp.take_along_axis(i2, ci % K, axis=-1))
    wts = jax.nn.softmax(sc, axis=-1)
    C = PEER_TOKEN_CHUNK
    nc = T // C

    def one_chunk(args):
        h_c, e_c, w_c = args
        act = jax.nn.gelu(jnp.einsum('td,thkd->thk', h_c, u[e_c]).astype(jnp.float32))
        return jnp.einsum('thk,thkd->td', (w_c * act).astype(v.dtype), v[e_c])

    out = lax.map(one_chunk, (hf.reshape(nc, C, D), experts.reshape(nc, C, Hh, K), wts.reshape(nc, C, Hh, K)))
    return out.reshape(B, S, D)

def hybrid_layer(x, mem, attn_norm_g, mem_norm_g, ffn_norm_g, w_in, moba_q_norm_g, moba_k_norm_g,
                 dn_conv_w, dn_a_log, dn_dt_bias, dn_out_norm_g, w_mem_kv, mem_q_norm_g, mem_k_norm_g,
                 w_branch, w_out, peer_w_q, peer_keys1, peer_keys2, peer_u, peer_v):
    B, S, D = x.shape
    pos = jnp.arange(S)
    h = rms_norm(x, attn_norm_g)
    proj = h @ w_in
    offsets = [int(o) for o in np.cumsum(IN_SIZES)[:-1]]
    moba_qkv, dn_qkv, b_raw, a_raw, z, mem_q, gate_raw = jnp.split(proj, offsets, axis=-1)

    mq, mk, mv = jnp.split(moba_qkv, 3, axis=-1)
    mq = rope(rms_norm(split_heads(mq, MOBA_HEADS), moba_q_norm_g), pos)
    mk = rope(rms_norm(split_heads(mk, MOBA_HEADS), moba_k_norm_g), pos)
    mv = split_heads(mv, MOBA_HEADS)
    moba_out = merge_heads(moba_attention(mq, mk, mv))

    dn_qkv = jax.nn.silu(causal_depthwise_conv(dn_qkv, dn_conv_w))
    dq, dk, dv = jnp.split(dn_qkv, 3, axis=-1)
    dq = l2_norm(split_heads(dq, DN_HEADS)) * (DN_HEAD_DIM ** -0.5)
    dk = l2_norm(split_heads(dk, DN_HEADS))
    dv = split_heads(dv, DN_HEADS)
    beta = jax.nn.sigmoid(b_raw.astype(jnp.float32)).transpose(0, 2, 1)
    g = (-jnp.exp(dn_a_log.astype(jnp.float32))[:, None]
         * jax.nn.softplus(a_raw.astype(jnp.float32).transpose(0, 2, 1) + dn_dt_bias.astype(jnp.float32)[:, None]))
    o = gated_delta_rule(dq, dk, dv, g, beta).transpose(0, 2, 1, 3)
    o = rms_norm(o, dn_out_norm_g) * jax.nn.silu(z.astype(jnp.float32).reshape(B, S, DN_HEADS, DN_HEAD_DIM))
    dn_out = o.reshape(B, S, DN_W).astype(x.dtype)

    mem_h = rms_norm(mem, mem_norm_g)
    mem_k, mem_v = jnp.split(mem_h @ w_mem_kv, 2, axis=-1)
    cq = rms_norm(split_heads(mem_q, MEM_HEADS), mem_q_norm_g)
    ck = rms_norm(split_heads(mem_k, MEM_HEADS), mem_k_norm_g)
    cv = split_heads(mem_v, MEM_HEADS)
    cs = jnp.einsum('bhsd,bhmd->bhsm', cq, ck).astype(jnp.float32) * (MEM_HEAD_DIM ** -0.5)
    cp = jax.nn.softmax(cs, axis=-1).astype(cv.dtype)
    mem_out = merge_heads(jnp.einsum('bhsm,bhmd->bhsd', cp, cv))

    branches = jnp.stack([moba_out, dn_out, mem_out], axis=2)
    branch_proj = jnp.einsum('bsnw,nwd->bsnd', branches, w_branch)
    gates = jax.nn.sigmoid(gate_raw.reshape(B, S, N_BRANCHES, D))
    mixed = jnp.sum(gates * branch_proj, axis=2)
    x = x + mixed @ w_out

    h2 = rms_norm(x, ffn_norm_g)
    x = x + peer_ffn(h2, peer_w_q, peer_keys1, peer_keys2, peer_u, peer_v)
    return x

def setup_inputs(seed: int = 0) -> dict:
    key = jax.random.key(seed)
    ks = jax.random.split(key, 24)
    f32 = jnp.float32

    def nrm(k, shape, scale):
        return jax.random.normal(k, shape, f32) * scale

    def gain(k, n):
        return 1.0 + 0.02 * jax.random.normal(k, (DEPTH, n), f32)

    x = nrm(ks[0], (BATCH, SEQ, D_MODEL), 1.0)
    mem = nrm(ks[1], (BATCH, MEM_LEN, D_MODEL), 1.0)
    attn_norm_g = gain(ks[2], D_MODEL)
    mem_norm_g = gain(ks[3], D_MODEL)
    ffn_norm_g = gain(ks[4], D_MODEL)
    w_in = nrm(ks[5], (DEPTH, D_MODEL, IN_WIDTH), D_MODEL ** -0.5)
    moba_q_norm_g = gain(ks[6], MOBA_HEAD_DIM)
    moba_k_norm_g = gain(ks[7], MOBA_HEAD_DIM)
    dn_conv_w = nrm(ks[8], (DEPTH, DN_CONV, 3 * DN_W), DN_CONV ** -0.5)
    dn_a_log = jnp.log(jax.random.uniform(ks[9], (DEPTH, DN_HEADS), f32, 1.0, 16.0))
    dt = jnp.exp(jax.random.uniform(ks[10], (DEPTH, DN_HEADS), f32, math.log(1e-3), math.log(1e-1)))
    dn_dt_bias = dt + jnp.log(-jnp.expm1(-dt))
    dn_out_norm_g = gain(ks[11], DN_HEAD_DIM)
    w_mem_kv = nrm(ks[12], (DEPTH, D_MODEL, 2 * MEM_W), D_MODEL ** -0.5)
    mem_q_norm_g = gain(ks[13], MEM_HEAD_DIM)
    mem_k_norm_g = gain(ks[14], MEM_HEAD_DIM)
    w_branch = nrm(ks[15], (DEPTH, N_BRANCHES, BRANCH_W, D_MODEL), BRANCH_W ** -0.5)
    w_out = nrm(ks[16], (DEPTH, D_MODEL, D_MODEL), D_MODEL ** -0.5)
    peer_w_q = nrm(ks[17], (DEPTH, D_MODEL, PEER_HEADS * PEER_QUERY_DIM), D_MODEL ** -0.5)
    peer_keys1 = nrm(ks[18], (DEPTH, PEER_N_KEYS, PEER_QUERY_DIM // 2), (PEER_QUERY_DIM // 2) ** -0.5)
    peer_keys2 = nrm(ks[19], (DEPTH, PEER_N_KEYS, PEER_QUERY_DIM // 2), (PEER_QUERY_DIM // 2) ** -0.5)
    peer_u = nrm(ks[20], (DEPTH, PEER_N_EXPERTS, D_MODEL), D_MODEL ** -0.5)
    peer_v = nrm(ks[21], (DEPTH, PEER_N_EXPERTS, D_MODEL), D_MODEL ** -0.5)
    return {"x": x, "mem": mem, "attn_norm_g": attn_norm_g, "mem_norm_g": mem_norm_g,
            "ffn_norm_g": ffn_norm_g, "w_in": w_in, "moba_q_norm_g": moba_q_norm_g,
            "moba_k_norm_g": moba_k_norm_g, "dn_conv_w": dn_conv_w, "dn_a_log": dn_a_log,
            "dn_dt_bias": dn_dt_bias, "dn_out_norm_g": dn_out_norm_g, "w_mem_kv": w_mem_kv,
            "mem_q_norm_g": mem_q_norm_g, "mem_k_norm_g": mem_k_norm_g, "w_branch": w_branch,
            "w_out": w_out, "peer_w_q": peer_w_q, "peer_keys1": peer_keys1, "peer_keys2": peer_keys2,
            "peer_u": peer_u, "peer_v": peer_v}

def reference(x, mem, attn_norm_g, mem_norm_g, ffn_norm_g, w_in, moba_q_norm_g, moba_k_norm_g,
              dn_conv_w, dn_a_log, dn_dt_bias, dn_out_norm_g, w_mem_kv, mem_q_norm_g, mem_k_norm_g,
              w_branch, w_out, peer_w_q, peer_keys1, peer_keys2, peer_u, peer_v):
    for l in range(DEPTH):
        x = hybrid_layer(x, mem, attn_norm_g[l], mem_norm_g[l], ffn_norm_g[l], w_in[l],
                         moba_q_norm_g[l], moba_k_norm_g[l], dn_conv_w[l], dn_a_log[l], dn_dt_bias[l],
                         dn_out_norm_g[l], w_mem_kv[l], mem_q_norm_g[l], mem_k_norm_g[l], w_branch[l],
                         w_out[l], peer_w_q[l], peer_keys1[l], peer_keys2[l], peer_u[l], peer_v[l])
    return x


_drawn_inputs = setup_inputs


def setup_inputs(seed=0):
    import zlib

    import numpy as np

    out = dict(_drawn_inputs(seed))
    spreads = {}
    factors = {'attn_norm_g': 5.094,
     'mem_norm_g': 8.0,
     'ffn_norm_g': 8.0,
     'moba_q_norm_g': 8.0,
     'moba_k_norm_g': 8.0,
     'dn_out_norm_g': 8.0,
     'mem_q_norm_g': 8.0,
     'mem_k_norm_g': 8.0,
     'peer_w_q': 3.999,
     'peer_keys1': 4.055,
     'peer_keys2': 4.067,
     'peer_u': 4.434,
     'peer_v': 4.011}
    for name, (base, spread) in spreads.items():
        noise = np.random.default_rng([zlib.crc32(name.encode()), seed]).standard_normal(out[name].shape)
        drawn = base * np.exp(spread * noise) if base else spread * noise
        out[name] = __import__('jax').numpy.asarray(drawn.astype(out[name].dtype))
    for name, factor in factors.items():
        out[name] = (out[name] * factor).astype(out[name].dtype)
    return out
```

```python
from contextlib import ExitStack

import numpy as np

import concourse.bass as bass
from concourse import mybir

F32 = mybir.dt.float32
U32 = mybir.dt.uint32
ALU = mybir.AluOpType
ACT = mybir.ActivationFunctionType
AX = mybir.AxisListType

P = 128
T = 256
NC = T // P
D = 1024
KT = D // P
HEADS = 8
HD = 128
MEM_HEADS = 4
EPS = 1e-6
LEVELS = 7

C_MQ, C_MK, C_MV = 0, 1024, 2048
C_DQ, C_DK, C_DV = 3072, 4096, 5120
C_BA = 6144
C_Z = 6160
C_CQ = 7184
C_G = 8208
IN_W = 11280

NEXP = 16384
NKEY = 128
TOPK = 16
PHEADS = 8

R_CONV = 0
R_ATTN = 96
R_MEM = 104
R_MQ, R_MK, R_DN = 112, 113, 114
R_CQ, R_CK = 115, 117
NROWS = 119

NEG = -1.0e30


def constants():
    i = np.arange(P)
    ident = np.eye(P, dtype=np.float32)
    after = (i[:, None] > i[None, :]).astype(np.float32)
    upto = (i[:, None] <= i[None, :]).astype(np.float32)
    ones = np.ones((P, P), np.float32)
    causal = np.where(i[None, :] <= i[:, None], 0.0, NEG).astype(np.float32)
    zeros = np.zeros((P, P), np.float32)
    swap = np.zeros((P, P), np.float32)
    half = HD // 2
    for d in range(half):
        swap[d + half, d] = -1.0
        swap[d, d + half] = 1.0
    inv = (1.0 / (np.float32(10000.0) ** (np.arange(0, HD, 2, dtype=np.float32) / np.float32(HD)))).astype(np.float32)
    ang = (np.arange(T, dtype=np.float32)[:, None] * inv[None, :]).astype(np.float32)
    cos = np.cos(ang.astype(np.float64)).astype(np.float32).T
    sin = np.sin(ang.astype(np.float64)).astype(np.float32).T
    cos, sin = np.concatenate([cos, cos]), np.concatenate([sin, sin])
    levels = []
    for n in range(LEVELS):
        s = 1 << n
        same = i[:, None] // (2 * s) == i[None, :] // (2 * s)
        low = (i[None, :] % (2 * s) >= s) & (i[:, None] % (2 * s) < s)
        levels.append((same & low).astype(np.float32))
    eps = np.full((P, 1), EPS, np.float32)
    iota = np.tile(np.arange(TOPK, dtype=np.float32), (P, 1))
    parts = {
        "ident": ident, "after": after, "ones": ones, "swap": swap,
        "upto": np.concatenate([upto, ones, upto], 1),
        "mask": np.concatenate([causal, zeros, causal], 1),
        "cos": cos, "sin": sin, "levels": np.concatenate(levels, 1), "eps": eps, "iota": iota,
    }
    at, where = 0, {}
    for k, v in parts.items():
        where[k] = (at, v.shape[1])
        at += v.shape[1]
    return np.ascontiguousarray(np.concatenate(list(parts.values()), 1), dtype=np.float32), where


class Event:

    def __init__(self, sem, primed=0):
        self.sem, self.primed = sem, primed

    def now(self, it):
        return it + (1 + self.primed)

    def before(self, it):
        assert self.primed
        return it + 1


def hybrid_layer(nc, cst_d, where, x_d, mem_d, rows, w_in, a_log, dt_bias, ffn_g, w_kv, w_branch, w_out,
                 w_q, keys1, keys2, peer_u, peer_v, out_d):
    with ExitStack() as ctx:
        def sb(name, shape, dt=F32):
            return ctx.enter_context(nc.sbuf_tensor(name, shape, dt))

        def sem(name):
            return ctx.enter_context(nc.semaphore(name))

        PH1 = 41472
        arena = sb("arena", [P, PH1])
        cst = sb("cst", [P, cst_d.shape[1]])
        x1 = sb("x1", [P, NC, D])
        h2 = sb("h2", [P, NC, D])
        small = sb("small", [P, 512])
        ps = ctx.enter_context(nc.psum_tensor("ps", [P, 8, 512], F32))

        def const(name):
            a, n = where[name]
            return cst[:, a:a + n]

        ident, after, ones, swap = const("ident"), const("after"), const("ones"), const("swap")
        upto, mask, cos, sin = const("upto"), const("mask"), const("cos"), const("sin")
        levels = const("levels").rearrange("p (s j) -> p s j", s=LEVELS)
        eps, iota = const("eps"), const("iota")

        taken = [0]

        def carve(words):
            a = taken[0]
            taken[0] += words
            assert taken[0] <= PH1, taken[0]
            return arena[:, a:a + words]

        ring = arena[:, 0:32 * D].rearrange("p (s n) -> p s n", s=32)
        gates = carve(3 * KT * T).rearrange("p (k t) -> p k t", t=T)
        branch = carve(3 * KT * T).rearrange("p (k t) -> p k t", t=T)
        zT = carve(KT * T).rearrange("p (k t) -> p k t", t=T)
        WS = 9
        wring = carve(WS * D)
        wslot = [wring[:, D * s:D * (s + 1)].rearrange("p (k j) -> p k j", k=KT) for s in range(WS)]
        hT = carve(KT * T).rearrange("p (k t) -> p k t", t=T)
        memhT = carve(KT * T).rearrange("p (k t) -> p k t", t=T)
        stage0 = taken[0]

        cols = small[:, 0:NROWS]
        gtok = small[:, 120:136].rearrange("p (c h) -> p c h", c=NC)
        btok = small[:, 136:152].rearrange("p (c h) -> p c h", c=NC)
        ss4 = small[:, 152:156]
        rstd4 = small[:, 156:160]
        var4 = small[:, 160:164]
        arow = small[:, 164:172]
        dtrow = small[:, 172:180]
        ba = small[:, 180:212].rearrange("p (c n) -> p c n", c=NC)
        ya = small[:, 212:228].rearrange("p (c n) -> p c n", c=NC)
        yb = small[:, 228:244].rearrange("p (c n) -> p c n", c=NC)
        yc = small[:, 244:260].rearrange("p (c n) -> p c n", c=NC)
        gfull = sb("gfull", [P, D])
        keysT = sb("keysT", [P, 2 * P])
        sq2, std2, rstd2 = small[:, 260:262], small[:, 262:264], small[:, 264:266]
        wba_t = sb("wba", [P, KT, 16])

        xin = carve(2 * NC * D).rearrange("p (s n) -> p s n", s=2 * NC)
        junk = carve(D)
        rows_sb = carve(P)
        taken[0] = stage0

        s_cst, s_rows, s_x, s_mem, s_ba, s_rowb = (sem(n) for n in ("s_cst", "s_rows", "s_x", "s_mem", "s_ba", "s_rowb"))
        a_sq, d_var, a_std, d_rstd, d_xn = (sem(n) for n in ("a_sq", "d_var", "a_std", "d_rstd", "d_xn"))
        p_cols, d_cols, p_tr, d_hT, p_ba, s_gate = (sem(n) for n in ("p_cols", "d_cols", "p_tr", "d_hT", "p_ba", "s_gate"))

        HT = 2 * T
        qg = carve(HT)
        sqm = carve(HT)
        rp1 = carve(HT)
        rp2 = carve(HT)
        qk = carve(HT)
        sm = carve(384)
        pr = carve(384)
        pT = carve(384)
        vtok = carve(T)
        cv = carve(3 * T).rearrange("p (i t) -> p i t", i=3)
        sl = carve(3 * T).rearrange("p (i t) -> p i t", i=3)
        kq = carve(HT)
        Gm = carve(384)
        Dm = carve(384)
        LT = carve(384)
        AT = carve(384)
        BT = carve(LEVELS * T).rearrange("p (s n) -> p s n", s=LEVELS)
        X = carve(T)
        XT = carve(T)
        Y = carve(T)
        dv = carve(T)
        vp = carve(T)
        vn = carve(T)
        w1 = carve(P)
        mx = carve(8)
        sqd = carve(HT)
        assert taken[0] <= PH1
        taken[0] = stage0

        mqk = carve(2 * HT)
        mqk4 = mqk.rearrange("p (a i t) -> p a i t", a=2, i=2)
        msq = carve(2 * HT)
        mstd = carve(HT)
        mv = carve(HT)
        mpr = carve(HT)
        mpT = carve(HT)
        zs = carve(HT)
        dstd = carve(HT)
        taken[0] = stage0

        mixT = hT
        prod = memhT[:, 0:3, :]
        mixs = memhT[:, 3, :]
        wo_late = carve(5 * D).rearrange("p (k n) -> p k n", k=5)
        assert taken[0] == 32 * D

        wq = carve(2 * D).rearrange("p (i k j) -> p i k j", i=2, k=KT)
        h2T = carve(KT * T).rearrange("p (k t) -> p k t", t=T)
        keys = carve(2 * P).rearrange("p (i d) -> p i d", i=2)
        pq = carve(HT)
        sc0 = carve(HT).rearrange("p (r n) -> p r n", r=4)
        cd0 = carve(HT).rearrange("p (c n) -> p c n", c=2)
        hot = carve(2 * HT)
        sc1 = hot[:, 0:HT].rearrange("p (r n) -> p r n", r=4)
        cd1 = hot[:, HT:2 * HT].rearrange("p (c n) -> p c n", c=2)
        rv = carve(64).rearrange("p (r k) -> p r k", r=4)
        ri = carve(64).bitcast(U32).rearrange("p (r k) -> p r k", r=4)
        rf = carve(64).rearrange("p (r k) -> p r k", r=4)
        sv = carve(32).rearrange("p (c k) -> p c k", c=2)
        ci = carve(32).bitcast(U32).rearrange("p (c k) -> p c k", c=2)
        ab = carve(64).bitcast(U32).rearrange("p (c i k) -> p c i k", c=2, i=2)
        ef = carve(64).rearrange("p (c i k) -> p c i k", c=2, i=2)
        idx2 = [carve(32).bitcast(U32) for _ in range(2)]
        ex = carve(32).rearrange("p (c k) -> p c k", c=2)
        wts2 = [carve(32).rearrange("p (c k) -> p c k", c=2) for _ in range(2)]
        neg = carve(8)
        acts = carve(32).rearrange("p (c k) -> p c k", c=2)
        gelu = carve(32).rearrange("p (c k) -> p c k", c=2)
        coef = carve(32).rearrange("p (c k) -> p c k", c=2)
        diag = carve(8 * P).rearrange("p (s j) -> p s j", s=8)
        assert taken[0] <= PH1, taken[0]
        s_wo, s_wq, s_keys, s_x1, s_out = (sem(n) for n in ("s_wo", "s_wq", "s_keys", "s_x1", "s_out"))
        s_u = [sem(f"s_u{i}") for i in range(TOPK // 2)]
        s_v = [sem(f"s_v{i}") for i in range(TOPK // 2)]
        t_route = sem("t_route")
        t_sp = sem("t_sp")
        t_pool = sem("t_pool")
        r_step, t_h2, t_tr, p_end = sem("r_step"), sem("t_h2"), sem("t_tr"), sem("p_end")
        RSTEPS = 14

        s_w = [sem(f"s_w{i}") for i in range(WS)]
        names = {}

        def ev(name, primed=0):
            if name not in names:
                names[name] = Event(sem(name), primed)
            return names[name]

        def on(eng, name, it):
            e = names[name]
            eng.wait_ge(e.sem, e.now(it))

        def on_before(eng, name, it):
            e = names[name]
            eng.wait_ge(e.sem, e.before(it))

        for i in range(WS):
            ev(f"tile{i}")
        for n in ("att_sq", "att_gain", "att_ss", "moba_rot", "att_std", "rope_cos", "rope_sin", "rope_sum",
                  "att_rstd", "att_qk", "scores", "masked", "maxes", "negmax", "probs", "psums", "z_silu", "dn_scaled", "br_sum", "br_mix", "sig", "x1_ready", "x1_done", "gdots",
                  "pnorm", "p_turned", "pT_ready",
                  "conv0", "conv1", "conv2", "conv3", "silu", "dn_sq", "dn_ss", "dn_std", "dn_rstd", "dn_kq",
                  "Gm_ready", "gdiff", "decay", "decay_masked", "dv_turned", "kq_dots0", "kq_dots1",
                  "LT_ready", "AT_ready", "BT_ready", "B_first", "X_first", "lvlY", "lvlYc", "lvlZ", "lvlX",
                  "att_out", "dn_out", "dv_kept", "sol0", "vp0", "cross", "w1_ready", "sol1", "vp1", "vn_ready"):
            ev(n)
        for n in ("gate0", "gate1", "z_kept", "att_kept", "dn_kept"):
            ev(n, 1)
        ev("br_prod", 2)
        for n in ("p_q", "p_qk", "p_s", "p_sk", "idx_ready", "wts_ready", "negs", "exps",
                  "acts", "gelu", "coef", "wq_used", "vmm_end"):
            ev(n)
        ev("dot", TOPK)
        ev("vrow", TOPK)
        ev("diag")

        block = ctx.enter_context(nc.Block())

        def w_cols(src, col):
            return src[:, bass.ds(col, P)].rearrange("(k p) j -> p k j", p=P)

        @block.sync
        def _(sp):
            sp.dma_start(cst[:, :], cst_d).then_inc(s_cst, 16)
            for first, src in rows:
                sp.dma_start(rows_sb[first:first + src.shape[0], :], src).then_inc(s_rows, 16)
            for c in range(NC):
                sp.dma_start(xin[:, c, :], x_d[c * P:(c + 1) * P, :]).then_inc(s_x, 16)
            for c in range(NC):
                sp.dma_start(xin[:, NC + c, :], mem_d[c * P:(c + 1) * P, :]).then_inc(s_mem, 16)
            sp.dma_start(wba_t[:, :, :], w_in[:, C_BA:C_BA + 16].rearrange("(k p) n -> p k n", p=P)).then_inc(s_ba, 16)
            sp.dma_start(gfull[:, :], ffn_g.partition_broadcast(P)).then_inc(s_x1, 16)
            for c in range(NC):
                sp.dma_start(x1[:, c, :], x_d[c * P:(c + 1) * P, :]).then_inc(s_x1, 16)
            sp.dma_start(arow, a_log.partition_broadcast(P)).then_inc(s_rowb, 16)
            sp.dma_start(dtrow, dt_bias.partition_broadcast(P)).then_inc(s_rowb, 16)

            def load(it, h, wait):
                starts = [C_MQ + h * P, C_MK + h * P, C_DK + h * P, C_DQ + h * P, C_DV + h * P, C_MV + h * P,
                          C_Z + h * P, C_G + h * (2 * P), C_G + h * (2 * P) + P]
                for i, at in enumerate(starts):
                    if wait:
                        sp.wait_ge(names[f"tile{i}"].sem, it)
                    sp.dma_start(wslot[i], w_cols(w_in, at)).then_inc(s_w[i], 16)

            load(0, 0, False)
            with sp.Fori(1, HEADS) as it:
                load(it, it, True)
            with sp.Fori(0, MEM_HEADS) as mh:
                sources = [(w_in, C_CQ), (w_in, C_CQ + P), (w_kv, 0), (w_kv, P), (w_kv, D), (w_kv, D + P),
                           (w_in, C_G + 16 * P), (w_in, C_G + 17 * P)]
                for i, (src, at) in enumerate(sources):
                    sp.wait_ge(names[f"tile{i}"].sem, mh + HEADS)
                    sp.sem_inc(t_sp, 1)
                    sp.dma_start(wslot[i], w_cols(src, mh * (2 * P) + at)).then_inc(s_w[i], 16)
            with sp.Fori(0, KT // 2) as m:
                for i in range(6):
                    sp.wait_ge(names[f"tile{i}"].sem, m + (HEADS + MEM_HEADS))
                    sp.sem_inc(t_sp, 1)
                    sp.dma_start(wslot[i], w_cols(w_branch[i % 3], m * (2 * P) + (i // 3) * P)).then_inc(s_w[i], 16)
                
            for i in (6, 7):
                sp.wait_ge(names[f"tile{i}"].sem, HEADS + MEM_HEADS)
            sp.wait_ge(names["tile8"].sem, HEADS)
            sp.wait_ge(names["att_kept"].sem, 1 + HEADS + MEM_HEADS)
            sp.wait_ge(names["dn_scaled"].sem, MEM_HEADS)
            sp.dma_start(wring[:, 6 * D:9 * D].rearrange("p (k n) -> p k n", k=3),
                         w_out[0:3 * P, :].rearrange("(k p) n -> p k n", p=P)).then_inc(s_wo, 16)
            sp.dma_start(wo_late, w_out[3 * P:D, :].rearrange("(k p) n -> p k n", p=P)).then_inc(s_wo, 16)
            for i, k in enumerate((keys1, keys2)):
                sp.dma_start(keys[:, i, :], k).then_inc(s_keys, 16)

            def load_wq(h):
                sp.dma_start(wq[:, 0, :, :], w_cols(w_q, h * (2 * P))).then_inc(s_wq, 16)
                sp.dma_start(wq[:, 1, :, :], w_cols(w_q, h * (2 * P) + P)).then_inc(s_wq, 16)

            load_wq(0)
            with sp.Fori(1, PHEADS) as h:
                sp.wait_ge(names["wq_used"].sem, h)
                load_wq(h)
            for c in range(NC):
                sp.wait_ge(p_end, c + 1)
                sp.dma_start(out_d[c * P:(c + 1) * P, :], x1[:, c, :]).then_inc(s_out, 16)
            sp.wait_ge(s_out, 16 * NC)

        @block.scalar
        def _(act):
            for s in range(2 * NC):
                act.wait_ge(s_x if s < NC else s_mem, 16 * NC)
                if s:
                    act.wait_ge(a_sq, s)
                act.activation(junk, xin[:, s, :], ACT.Square, accum_out=ss4[:, s:s + 1]).then_inc(a_sq, 1)
            act.wait_ge(d_var, 1)
            act.activation(var4, var4, ACT.Sqrt).then_inc(a_std, 1)
            act.wait_ge(p_ba, 1)
            act.activation(yb, ps[:, 0, 0:32].rearrange("p (c n) -> p c n", c=NC)[:, :, 0:8], ACT.Exp, scale=-1.0).then_inc(s_gate, 1)
            act.wait_ge(s_rowb, 32)
            act.activation(arow, arow, ACT.Exp).then_inc(s_gate, 1)
            act.wait_ge(s_gate, 6)
            act.activation(yc, ya, ACT.Abs).then_inc(s_gate, 1)
            act.wait_ge(s_gate, 7)
            act.activation(yc, yc, ACT.Exp, scale=-1.0).then_inc(s_gate, 1)
            act.wait_ge(s_gate, 8)
            act.activation(yc, yc, ACT.Ln, bias=1.0).then_inc(s_gate, 1)

            act.wait_ge(s_rows, 16 * len(rows))
            act.wait_ge(d_cols, 1)
            for n in ("gate0", "gate1", "z_kept", "att_kept", "dn_kept"):
                act.sem_inc(names[n].sem, 1)
            with act.Fori(0, HEADS) as h:
                on(act, "tile1", h)
                act.activation(sqm, ps[:, 0, :], ACT.Square).then_inc(names["att_sq"].sem, 1)
                act.activation(qg[:, 0:T], ps[:, 0, 0:T], ACT.Copy, scale=cols[:, R_MQ:R_MQ + 1])
                act.activation(qg[:, T:HT], ps[:, 0, T:HT], ACT.Copy, scale=cols[:, R_MK:R_MK + 1]).then_inc(names["att_gain"].sem, 1)
                on(act, "tile3", h)
                for i, tile in ((0, 8), (1, 0)):
                    tap = small[:, bass.ds(h + (R_CONV + 3 * 24 + tile), 1)]
                    ins = act.activation(cv[:, i, :], ps[:, 1, i * T:(i + 1) * T], ACT.Copy, scale=tap)
                on(act, "tile5", h)
                act.activation(vtok, ps[:, 2, T:HT], ACT.Copy)
                tap = small[:, bass.ds(h + (R_CONV + 3 * 24 + 16), 1)]
                act.activation(cv[:, 2, :], ps[:, 2, 0:T], ACT.Copy, scale=tap).then_inc(names["conv0"].sem, 1)
                on(act, "conv3", h)
                act.activation(sl[:, :, :], cv[:, :, :], ACT.Silu).then_inc(names["silu"].sem, 1)
                on(act, "silu", h)
                act.activation(sqd, sl[:, 0:2, :].rearrange("p i t -> p (i t)"), ACT.Square).then_inc(names["dn_sq"].sem, 1)
                on(act, "att_ss", h)
                act.activation(rp1, ps[:, 3, :], ACT.Sqrt, bias=eps, scale=1.0 / HD).then_inc(names["att_std"].sem, 1)
                on(act, "dn_ss", h)
                act.activation(kq, ps[:, 3, :], ACT.Sqrt, bias=eps, scale=1.0).then_inc(names["dn_std"].sem, 1)
                on(act, "gdiff", h)
                act.activation(Dm, ps[:, 5, 0:384], ACT.Exp).then_inc(names["decay"].sem, 1)
                on(act, "dv_turned", h)
                act.activation(dv, ps[:, 5, 0:T], ACT.Copy).then_inc(names["dv_kept"].sem, 1)
                on(act, "negmax", h)
                act.activation(pr[:, 0:P], sm[:, 0:P], ACT.Exp, bias=mx[:, 2:3], scale=float(HD) ** -0.5, accum_out=mx[:, 4:5])
                act.activation(pr[:, P:384], sm[:, P:384], ACT.Exp, bias=mx[:, 3:4], scale=float(HD) ** -0.5,
                               accum_out=mx[:, 5:6]).then_inc(names["probs"].sem, 1)
                on(act, "p_turned", h)
                act.activation(pT, ps[:, 5, 0:384], ACT.Copy).then_inc(names["pT_ready"].sem, 1)
                on(act, "att_out", h)
                act.activation(branch[:, bass.ds(h, 1), :], ps[:, 6, 0:T].rearrange("p (o t) -> p o t", o=1), ACT.Copy).then_inc(names["att_kept"].sem, 1)
                on(act, "tile7", h)
                act.activation(zT[:, bass.ds(h, 1), :], ps[:, 7, 0:T].rearrange("p (o t) -> p o t", o=1), ACT.Copy).then_inc(names["z_kept"].sem, 1)
                act.activation(gates[:, bass.ds(h * 2, 1), :], ps[:, 7, T:HT].rearrange("p (o t) -> p o t", o=1), ACT.Copy).then_inc(names["gate0"].sem, 1)
                on(act, "tile8", h)
                act.activation(gates[:, bass.ds(h * 2 + 1, 1), :], ps[:, 0, 0:T].rearrange("p (o t) -> p o t", o=1), ACT.Copy).then_inc(names["gate1"].sem, 1)
                on(act, "dn_out", h)
                act.activation(branch[:, bass.ds(h + 8, 1), :], ps[:, 4, 0:T].rearrange("p (o t) -> p o t", o=1), ACT.Copy).then_inc(names["dn_kept"].sem, 1)

            with act.Fori(HEADS, HEADS + MEM_HEADS) as it:
                two = lambda a: a.rearrange("p (i t) -> p i t", i=2)
                heads = branch[:, bass.ds((it - HEADS) * 2 + 8, 2), :]
                act.activation(two(sqd), heads, ACT.Square).then_inc(names["dn_sq"].sem, 1)
                on(act, "tile1", it)
                act.activation(msq[:, 0:HT], ps[:, 0, :], ACT.Square)
                for i in range(2):
                    ins = act.activation(mqk4[:, 0, i, :], ps[:, 0, i * T:(i + 1) * T], ACT.Copy, scale=cols[:, R_CQ + i:R_CQ + i + 1])
                on(act, "tile3", it)
                act.activation(msq[:, HT:2 * HT], ps[:, 1, :], ACT.Square).then_inc(names["att_sq"].sem, 1)
                for i in range(2):
                    ins = act.activation(mqk4[:, 1, i, :], ps[:, 1, i * T:(i + 1) * T], ACT.Copy, scale=cols[:, R_CK + i:R_CK + i + 1])
                ins.then_inc(names["att_gain"].sem, 1)
                on(act, "tile5", it)
                act.activation(mv, ps[:, 2, :], ACT.Copy).then_inc(names["dv_kept"].sem, 1)
                on(act, "dn_ss", it)
                act.activation(dstd, ps[:, 6, :], ACT.Sqrt, bias=eps, scale=1.0 / HD).then_inc(names["dn_std"].sem, 1)
                on(act, "att_ss", it)
                act.activation(mstd, ps[:, 3, :], ACT.Sqrt, bias=eps, scale=1.0 / (2 * HD)).then_inc(names["att_std"].sem, 1)
                act.activation(two(zs), zT[:, bass.ds((it - HEADS) * 2, 2), :], ACT.Silu).then_inc(names["z_silu"].sem, 1)
                on(act, "negmax", it)
                for c in range(NC):
                    ins = act.activation(mpr[:, c * T:(c + 1) * T], ps[:, 4, c * T:(c + 1) * T], ACT.Exp, bias=mx[:, 2 + c:3 + c],
                                         scale=float(2 * HD) ** -0.5, accum_out=mx[:, 4 + c:5 + c])
                ins.then_inc(names["probs"].sem, 1)
                on(act, "p_turned", it)
                act.activation(mpT, ps[:, 5, :], ACT.Copy).then_inc(names["pT_ready"].sem, 1)
                on(act, "tile7", it)
                act.activation(gates[:, bass.ds((it - HEADS) * 2 + 16, 2), :], two(ps[:, 7, :]), ACT.Copy).then_inc(names["gate0"].sem, 1)
                on(act, "att_out", it)
                act.activation(branch[:, bass.ds((it - HEADS) * 2 + 16, 2), :], two(ps[:, 6, :]), ACT.Copy).then_inc(names["att_kept"].sem, 1)
            act.wait_ge(names["gate0"].sem, 1 + HEADS + MEM_HEADS)
            for n in range(3):
                act.activation(gates[:, 8 * n:8 * n + 8, :], gates[:, 8 * n:8 * n + 8, :], ACT.Sigmoid).then_inc(names["sig"].sem, 1)
            act.wait_ge(names["x1_ready"].sem, 2 * NC)
            for c in range(NC):
                if c:
                    act.wait_ge(names["x1_done"].sem, c)
                act.activation(h2[:, 0, :], x1[:, c, :], ACT.Square, accum_out=sq2[:, c:c + 1]).then_inc(names["x1_done"].sem, 1)
            act.wait_ge(t_h2, 1)
            act.activation(std2, std2, ACT.Sqrt).then_inc(t_h2, 1)

            def route_act(h):
                on(act, "p_q", h)
                act.activation(pq, ps[:, 4, :], ACT.Copy).then_inc(names["p_qk"].sem, 1)
                on(act, "p_s", h)
                act.activation(sc0.rearrange("p r n -> p (r n)"), ps[:, 5, :], ACT.Copy).then_inc(names["p_sk"].sem, 1)

            def weights_act(h):
                on(act, "negs", h)
                for c in range(NC):
                    ins = act.activation(ex[:, c, :], sv[:, c, :], ACT.Exp, bias=neg[:, c:c + 1], accum_out=neg[:, 4 + c:5 + c])
                ins.then_inc(names["exps"].sem, 1)

            def chunk_act(h, c):
                n = h * NC + c
                on(act, "acts", n)
                act.activation(gelu[:, c, :], acts[:, c, :], ACT.Gelu_apprx_tanh).then_inc(names["gelu"].sem, 1)
                on(act, "coef", n)
                for k in range(TOPK):
                    row = n * TOPK + k
                    act.wait_ge(names["vrow"].sem, row + 9)
                    act.activation(diag[:, k % 8, :], ident, ACT.Copy, scale=coef[:, c, k:k + 1]).then_inc(names["diag"].sem, 1)

            route_act(0)
            weights_act(0)

            def head_act(h, route=True):
                chunk_act(h, 0)
                if route:
                    route_act(h + 1)
                chunk_act(h, 1)
                if route:
                    weights_act(h + 1)

            with act.Fori(0, PHEADS // 2 - 1) as pair:
                head_act(pair * 2)
                head_act(pair * 2 + 1)
            head_act(PHEADS - 2)
            head_act(PHEADS - 1, False)

        @block.gpsimd
        def _(pool):
            with pool.Fori(0, HEADS) as h:
                on(pool, "decay", h)
                pool.tensor_tensor(Dm, Dm, upto, ALU.mult).then_inc(names["decay_masked"].sem, 1)
                on(pool, "LT_ready", h)
                for s in range(LEVELS):
                    for c in range(NC):
                        ins = pool.tensor_tensor(BT[:, s, c * P:(c + 1) * P], LT[:, c * T:c * T + P], levels[:, s, :], ALU.mult)
                    if s == 0:
                        ins.then_inc(names["B_first"].sem, 1)
                ins.then_inc(names["BT_ready"].sem, 1)

            pool.sem_inc(names["dot"].sem, TOPK)
            with pool.Fori(0, PHEADS // 2) as pair:
                for odd in range(2):
                    h, idx = pair * 2 + odd, idx2[odd]
                    on(pool, "idx_ready", h)
                    pool.sem_inc(t_pool, 1)
                    for c in range(NC):
                        for k in range(TOPK):
                            at = c * TOPK + k
                            pool.wait_ge(names["dot"].sem, (h * NC + c) * TOPK + (k + 1))
                            pool.sem_inc(t_pool, 1)
                            pool.indirect_dma_start(ring[:, k, :], None, peer_u, bass.IndirectOffsetOnAxis(ap=idx[:, at:at + 1], axis=0)).then_inc(s_u[k // 2], 16)
                        for k in range(TOPK):
                            at = c * TOPK + k
                            pool.wait_ge(names["vrow"].sem, (h * NC + c) * TOPK + (k + 1))
                            pool.sem_inc(t_pool, 1)
                            pool.indirect_dma_start(ring[:, TOPK + k, :], None, peer_v, bass.IndirectOffsetOnAxis(ap=idx[:, at:at + 1], axis=0)).then_inc(s_v[k // 2], 16)

        @block.vector
        def _(dve):
            def done(name):
                return names[name].sem

            dve.wait_ge(p_cols, 1)
            dve.tensor_copy(cols, ps[:, 7, 0:NROWS]).then_inc(d_cols, 1)
            dve.wait_ge(a_sq, 2 * NC)
            dve.tensor_scalar(var4, ss4, 1.0 / D, EPS, ALU.mult, ALU.add).then_inc(d_var, 1)
            dve.wait_ge(a_std, 1)
            dve.reciprocal(rstd4, var4).then_inc(d_rstd, 1)
            dve.wait_ge(d_rstd, 1)
            for s in range(2 * NC):
                dve.tensor_scalar(xin[:, s, :], xin[:, s, :], rstd4[:, s:s + 1], None, ALU.mult).then_inc(d_xn, 1)
            dve.wait_ge(d_cols, 1)
            for b in range(8):
                s, half = b // 2, b % 2
                c = s % NC
                gain = (R_ATTN if s < NC else R_MEM) + 4 * half
                dst = (hT if s < NC else memhT)[:, 4 * half:4 * half + 4, c * P:(c + 1) * P]
                dve.wait_ge(p_tr, b + 1)
                dve.tensor_tensor(dst, ps[:, b, :].rearrange("p (k t) -> p k t", k=4),
                                  cols[:, gain:gain + 4, None].to_broadcast([P, 4, P]), ALU.mult).then_inc(d_hT, 1)
            dve.wait_ge(s_gate, 2)
            dve.tensor_scalar(yb, yb, 1.0, None, ALU.add).then_inc(s_gate, 1)
            dve.wait_ge(s_gate, 3)
            dve.reciprocal(btok, yb).then_inc(s_gate, 1)
            dve.tensor_tensor(ya, ps[:, 0, 0:32].rearrange("p (c n) -> p c n", c=NC)[:, :, 8:16],
                              dtrow[:, None, :].to_broadcast([P, NC, 8]), ALU.add).then_inc(s_gate, 1)
            dve.wait_ge(s_gate, 5)
            dve.tensor_scalar(yb, ya, 0.0, None, ALU.max).then_inc(s_gate, 1)
            dve.wait_ge(s_gate, 9)
            dve.tensor_tensor(yb, yb, yc, ALU.add).then_inc(s_gate, 1)
            dve.wait_ge(s_gate, 10)
            dve.scalar_tensor_tensor(out=gtok, in0=yb, scalar=-1.0, in1=arow[:, None, :].to_broadcast([P, NC, 8]),
                                     op0=ALU.mult, op1=ALU.mult).then_inc(s_gate, 1)
            dve.wait_ge(s_gate, 11)
            dve.wait_ge(s_cst, 16)

            with dve.Fori(0, HEADS) as h:
                g0, g1 = (small[:, bass.ds(h + (120 + 8 * c), 1)] for c in range(NC))
                b0, b1 = (small[:, bass.ds(h + (136 + 8 * c), 1)] for c in range(NC))
                dve.tensor_scalar(Gm[:, 0:T], upto[:, 0:T], g0, None, ALU.mult)
                dve.tensor_scalar(Gm[:, T:384], upto[:, T:384], g1, None, ALU.mult).then_inc(done("Gm_ready"), 1)
                on(dve, "conv0", h)
                for back in (1, 2, 3):
                    if back > 1:
                        on(dve, f"conv{back - 1}", h)
                    for i, tile in ((0, 8), (1, 0), (2, 16)):
                        src = ps[:, 1, i * T:(i + 1) * T] if i < 2 else ps[:, 2, 0:T]
                        tap = small[:, bass.ds(h + (R_CONV + (3 - back) * 24 + tile), 1)]
                        ins = dve.scalar_tensor_tensor(out=cv[:, i, back:T], in0=src[:, 0:T - back], scalar=tap,
                                                       in1=cv[:, i, back:T], op0=ALU.mult, op1=ALU.add)
                    ins.then_inc(done(f"conv{back}"), 1)
                on(dve, "att_gain", h)
                on(dve, "att_std", h)
                dve.reciprocal(rp1, rp1).then_inc(done("att_rstd"), 1)
                on(dve, "moba_rot", h)
                both = lambda a: a.rearrange("p (i t) -> p i t", i=2)
                dve.tensor_tensor(both(rp2), both(ps[:, 4, :]), sin[:, None, :].to_broadcast([P, 2, T]), ALU.mult).then_inc(done("rope_sin"), 1)
                dve.tensor_tensor(both(qk), both(qg), cos[:, None, :].to_broadcast([P, 2, T]), ALU.mult).then_inc(done("rope_cos"), 1)
                on(dve, "rope_cos", h)
                dve.tensor_tensor(qk, qk, rp2, ALU.add).then_inc(done("rope_sum"), 1)
                on(dve, "rope_sum", h)
                dve.tensor_tensor(qk, qk, rp1, ALU.mult).then_inc(done("att_qk"), 1)
                on(dve, "dn_std", h)
                dve.reciprocal(kq, kq).then_inc(done("dn_rstd"), 1)
                on(dve, "dn_rstd", h)
                dve.tensor_tensor(kq, kq, sl[:, 0:2, :].rearrange("p i t -> p (i t)"), ALU.mult).then_inc(done("dn_kq"), 1)
                on(dve, "scores", h)
                dve.tensor_tensor(sm, ps[:, 6, 0:384], mask, ALU.add).then_inc(done("masked"), 1)
                on(dve, "masked", h)
                dve.tensor_reduce(mx[:, 0:1], sm[:, 0:P], AX.X, ALU.max)
                dve.tensor_reduce(mx[:, 1:2], sm[:, P:384], AX.X, ALU.max).then_inc(done("maxes"), 1)
                on(dve, "maxes", h)
                dve.tensor_scalar(mx[:, 2:4], mx[:, 0:2], -float(HD) ** -0.5, None, ALU.mult).then_inc(done("negmax"), 1)
                on(dve, "decay_masked", h)
                on(dve, "kq_dots0", h)
                dve.scalar_tensor_tensor(out=LT[:, 0:T], in0=ps[:, 4, 0:T], scalar=b0, in1=Dm[:, 0:T], op0=ALU.mult, op1=ALU.mult)
                on(dve, "kq_dots1", h)
                dve.scalar_tensor_tensor(out=LT[:, T:384], in0=ps[:, 5, 0:P], scalar=b1, in1=Dm[:, T:384],
                                         op0=ALU.mult, op1=ALU.mult).then_inc(done("LT_ready"), 1)
                dve.scalar_tensor_tensor(out=AT[:, 0:T], in0=ps[:, 4, T:HT], scalar=float(HD) ** -0.5, in1=Dm[:, 0:T],
                                         op0=ALU.mult, op1=ALU.mult)
                dve.scalar_tensor_tensor(out=AT[:, T:384], in0=ps[:, 5, P:T], scalar=float(HD) ** -0.5, in1=Dm[:, T:384],
                                         op0=ALU.mult, op1=ALU.mult).then_inc(done("AT_ready"), 1)
                two = lambda a: a.rearrange("p (c j) -> p c j", c=NC)
                idb = ident[:, None, :].to_broadcast([P, NC, P])
                on(dve, "B_first", h)
                dve.tensor_tensor(two(XT), idb, BT[:, 0, :].rearrange("p (c j) -> p c j", c=NC), ALU.subtract)
                on(dve, "lvlZ", h * LEVELS)
                dve.tensor_tensor(two(X), idb, two(ps[:, 2, 0:T]), ALU.subtract).then_inc(done("lvlX"), 1)
                on(dve, "probs", h)
                dve.reciprocal(mx[:, 6:8], mx[:, 4:6]).then_inc(done("psums"), 1)
                on(dve, "psums", h)
                dve.tensor_scalar(pr[:, 0:P], pr[:, 0:P], mx[:, 6:7], None, ALU.mult)
                dve.tensor_scalar(pr[:, P:384], pr[:, P:384], mx[:, 7:8], None, ALU.mult).then_inc(done("pnorm"), 1)
                for s in range(1, LEVELS):
                    on(dve, "lvlY", h * (LEVELS - 1) + (s - 1))
                    dve.tensor_copy(Y, ps[:, 1, 0:T]).then_inc(done("lvlYc"), 1)
                    on(dve, "lvlZ", h * LEVELS + s)
                    if s < LEVELS - 1:
                        dve.tensor_tensor(X, X, ps[:, 2, 0:T], ALU.subtract)
                    dve.tensor_tensor(XT, XT, ps[:, 2, T:HT], ALU.subtract).then_inc(done("lvlX"), 1)
                on(dve, "sol0", h)
                dve.tensor_copy(vp[:, 0:P], ps[:, 1, 0:P]).then_inc(done("vp0"), 1)
                on(dve, "cross", h)
                dve.tensor_tensor(w1, dv[:, P:T], ps[:, 2, 0:P], ALU.subtract).then_inc(done("w1_ready"), 1)
                dve.tensor_scalar(vn[:, 0:P], vp[:, 0:P], b0, None, ALU.mult)
                on(dve, "sol1", h)
                dve.tensor_scalar(vn[:, P:T], ps[:, 1, 0:P], b1, None, ALU.mult).then_inc(done("vn_ready"), 1)

            with dve.Fori(HEADS, HEADS + MEM_HEADS) as it:
                two = lambda a: a.rearrange("p (i t) -> p i t", i=2)
                heads = branch[:, bass.ds((it - HEADS) * 2 + 8, 2), :]
                on(dve, "dn_std", it)
                dve.reciprocal(dstd, dstd).then_inc(done("dn_rstd"), 1)
                on(dve, "att_std", it)
                dve.reciprocal(mstd, mstd).then_inc(done("att_rstd"), 1)
                on(dve, "att_rstd", it)
                on(dve, "att_gain", it)
                dve.tensor_tensor(mqk4, mqk4, two(mstd)[:, :, None, :].to_broadcast([P, 2, 2, T]), ALU.mult).then_inc(done("att_qk"), 1)
                on(dve, "dn_rstd", it)
                on(dve, "z_silu", it - HEADS)
                dve.scalar_tensor_tensor(out=dstd, in0=dstd, scalar=cols[:, R_DN:R_DN + 1], in1=zs, op0=ALU.mult,
                                         op1=ALU.mult).then_inc(done("dn_kq"), 1)
                on(dve, "dn_kq", it)
                dve.tensor_tensor(heads, heads, two(dstd), ALU.mult).then_inc(done("dn_scaled"), 1)
                on(dve, "scores", it)
                dve.tensor_reduce(mx[:, 0:2], two(ps[:, 4, :]), AX.X, ALU.max).then_inc(done("maxes"), 1)
                on(dve, "maxes", it)
                dve.tensor_scalar(mx[:, 2:4], mx[:, 0:2], -float(2 * HD) ** -0.5, None, ALU.mult).then_inc(done("negmax"), 1)
                on(dve, "probs", it)
                dve.reciprocal(mx[:, 6:8], mx[:, 4:6]).then_inc(done("psums"), 1)
                on(dve, "psums", it)
                dve.tensor_tensor(two(mpr), two(mpr), mx[:, 6:8, None].to_broadcast([P, 2, T]), ALU.mult).then_inc(done("pnorm"), 1)
            dve.wait_ge(done("sig"), 3)
            g4 = gates.rearrange("p (n m) t -> p n m t", n=3)
            with dve.Fori(0, KT // 2) as mp:
                for j in range(2):
                    m = mp * 2 + j
                    on(dve, f"tile{3 * j + 2}", mp + (HEADS + MEM_HEADS))
                    dve.tensor_tensor(prod, ps[:, 3 * j:3 * j + 3, 0:T], g4[:, :, bass.ds(m, 1), :].rearrange("p n o t -> p n (o t)"),
                                      ALU.mult).then_inc(done("br_prod"), 1)
                    on(dve, "br_prod", m)
                    dve.tensor_tensor(mixs, prod[:, 0, :], prod[:, 1, :], ALU.add).then_inc(done("br_sum"), 1)
                    on(dve, "br_sum", m)
                    dve.tensor_tensor(mixT[:, bass.ds(m, 1), :], mixs[:, None, :], prod[:, 2:3, :], ALU.add).then_inc(done("br_mix"), 1)
                    on(dve, "br_mix", m)
            dve.wait_ge(s_x1, 16 * (NC + 1))
            for c in range(NC):
                for n in range(2):
                    b = 2 * c + n
                    dve.wait_ge(done("gdots"), b + 1)
                    dve.tensor_tensor(x1[:, c, n * 512:(n + 1) * 512], x1[:, c, n * 512:(n + 1) * 512], ps[:, b, :],
                                      ALU.add).then_inc(done("x1_ready"), 1)
            dve.wait_ge(done("x1_done"), NC)
            dve.tensor_scalar(std2, sq2, 1.0 / D, EPS, ALU.mult, ALU.add).then_inc(t_h2, 1)
            dve.wait_ge(t_h2, 2)
            dve.reciprocal(rstd2, std2).then_inc(t_h2, 1)
            dve.wait_ge(t_h2, 3)
            for c in range(NC):
                dve.scalar_tensor_tensor(out=h2[:, c, :], in0=x1[:, c, :], scalar=rstd2[:, c:c + 1], in1=gfull[:, :],
                                         op0=ALU.mult, op1=ALU.mult).then_inc(t_h2, 1)
            for b in range(4):
                dve.wait_ge(t_tr, 1 + b)
                dve.tensor_copy(h2T[:, 4 * (b % 2):4 * (b % 2) + 4, (b // 2) * P:(b // 2 + 1) * P],
                                ps[:, b, :].rearrange("p (k t) -> p k t", k=4)).then_inc(s_gate, 1)
            dve.wait_ge(t_tr, 5)
            dve.tensor_copy(keysT[:, :], ps[:, 6, 0:2 * P]).then_inc(s_gate, 1)

            def route_dve(h, odd):
                step = [0]

                def link(ins):
                    ins.then_inc(r_step, 1)
                    step[0] += 1
                    dve.wait_ge(r_step, h * RSTEPS + step[0])
                    dve.sem_inc(t_route, 1)

                def best(values, where_, rows_, scratch):
                    link([dve.max(v[:, 0:8], a) for v, a in zip(values, rows_)][-1])
                    for v, i, a, b in zip(values, where_, rows_, scratch):
                        dve.max_index(i[:, 0:8], v[:, 0:8], a)
                        ins = dve.match_replace(b, v[:, 0:8], a, -3.0e38)
                    link(ins)
                    link([dve.max(v[:, 8:16], b) for v, b in zip(values, scratch)][-1])
                    link([dve.max_index(i[:, 8:16], v[:, 8:16], b) for v, i, b in zip(values, where_, scratch)][-1])

                on(dve, "p_sk", h)
                dve.sem_inc(t_route, 1)
                best([rv[:, r, :] for r in range(4)], [ri[:, r, :] for r in range(4)],
                     [sc0[:, r, :] for r in range(4)], [sc1[:, r, :] for r in range(4)])
                dve.tensor_copy(rf, ri)
                for c in range(NC):
                    ins = dve.tensor_tensor(cd0[:, c, :].rearrange("p (a b) -> p a b", a=TOPK),
                                            rv[:, 2 * c, :, None].to_broadcast([P, TOPK, TOPK]),
                                            rv[:, 2 * c + 1, None, :].to_broadcast([P, TOPK, TOPK]), ALU.add)
                link(ins)
                best([sv[:, c, :] for c in range(NC)], [ci[:, c, :] for c in range(NC)],
                     [cd0[:, c, :] for c in range(NC)], [cd1[:, c, :] for c in range(NC)])
                dve.tensor_scalar(neg[:, 0:2], sv[:, :, 0:1].rearrange("p c o -> p (c o)"), -1.0, None, ALU.mult).then_inc(done("negs"), 1)
                dve.tensor_scalar(ab[:, :, 0, :], ci, 4, None, ALU.logical_shift_right)
                link(dve.tensor_scalar(ab[:, :, 1, :], ci, 15, None, ALU.bitwise_and))
                h3 = hot.rearrange("p (r a) -> p r a", a=TOPK)
                link(dve.tensor_tensor(h3, ab.rearrange("p c i k -> p (c i k)")[:, :, None].to_broadcast([P, 64, TOPK]),
                                       iota[:, None, :].to_broadcast([P, 64, TOPK]), ALU.is_equal))
                h4 = hot.rearrange("p (r k a) -> p r k a", r=4, k=TOPK)
                link(dve.tensor_tensor(h4, h4, rf[:, :, None, :].to_broadcast([P, 4, TOPK, TOPK]), ALU.mult))
                link(dve.tensor_reduce(ef.rearrange("p c i k -> p (c i k)"), h3, AX.X, ALU.add))
                dve.wait_ge(done("vrow"), TOPK if isinstance(h, int) and h < 2 else (h - 1) * (NC * TOPK) + TOPK)
                dve.scalar_tensor_tensor(out=idx2[odd].rearrange("p (c k) -> p c k", c=2), in0=ef[:, :, 0, :], scalar=float(NKEY),
                                         in1=ef[:, :, 1, :], op0=ALU.mult, op1=ALU.add).then_inc(done("idx_ready"), 1)
                on(dve, "exps", h)
                link(dve.reciprocal(neg[:, 6:8], neg[:, 4:6]))
                dve.tensor_tensor(wts2[odd], ex, neg[:, 6:8, None].to_broadcast([P, NC, TOPK]), ALU.mult).then_inc(done("wts_ready"), 1)
                assert step[0] == RSTEPS

            def chunk_dve(h, odd, c):
                n = h * NC + c
                for k in range(TOPK):
                    if k % 2 == 0:
                        dve.wait_ge(s_u[k // 2], (n + 1) * 32)
                    dve.tensor_tensor_reduce(out=ring[:, k, :], in0=ring[:, k, :], in1=h2[:, c, :], scale=1.0, scalar=0.0,
                                             op0=ALU.mult, op1=ALU.add, accum_out=acts[:, c, k:k + 1]).then_inc(done("dot"), 1)
                dve.wait_ge(done("dot"), n * TOPK + 2 * TOPK)
                dve.sem_inc(done("acts"), 1)
                on(dve, "gelu", n)
                dve.tensor_tensor(coef[:, c, :], gelu[:, c, :], wts2[odd][:, c, :], ALU.mult).then_inc(done("coef"), 1)

            dve.memset(neg[:, :], 0.0).then_inc(s_gate, 1)
            dve.wait_ge(s_gate, 17)
            route_dve(0, 0)

            def head_dve(h, odd, route=True):
                on(dve, "wts_ready", h)
                chunk_dve(h, odd, 0)
                chunk_dve(h, odd, 1)
                if route:
                    route_dve(h + 1, 1 - odd)

            with dve.Fori(0, PHEADS // 2 - 1) as pair:
                head_dve(pair * 2, 0)
                head_dve(pair * 2 + 1, 1)
            head_dve(PHEADS - 2, 0)
            head_dve(PHEADS - 1, 1, False)
            dve.wait_ge(done("vmm_end"), 1)
            for c in range(NC):
                dve.tensor_tensor(x1[:, c, :], x1[:, c, :], ps[:, 2 * c:2 * c + 2, :].rearrange("p b n -> p (b n)"),
                                  ALU.add).then_inc(p_end, 1)

        @block.tensor
        def _(pe):
            def done(name):
                return names[name].sem

            pe.wait_ge(s_cst, 16)
            pe.wait_ge(s_rows, 16 * len(rows))
            pe.transpose(ps[:, 7, 0:NROWS], rows_sb[0:NROWS, :], ident[0:NROWS, 0:NROWS]).then_inc(p_cols, 1)
            for b in range(8):
                s, half = b // 2, b % 2
                pe.wait_ge(d_xn, s + 1)
                if b == 7:
                    pe.wait_ge(d_cols, 1)
                for k in range(4):
                    at = (4 * half + k) * P
                    ins = pe.transpose(ps[:, b, k * P:(k + 1) * P], xin[:, s, at:at + P], ident)
                ins.then_inc(p_tr, 1)
            pe.wait_ge(d_hT, 4)
            pe.wait_ge(s_ba, 16)
            for c in range(NC):
                for k in range(KT):
                    ins = pe.matmul(ps[:, 0, 16 * c:16 * c + 16], hT[:, k, c * P:(c + 1) * P], wba_t[:, k, :],
                                    start=(k == 0), stop=(k == KT - 1))
            ins.then_inc(p_ba, 1)
            pe.wait_ge(d_hT, 8)
            pe.sem_inc(done("br_prod"), 2)
            pe.wait_ge(s_gate, 5)

            def project(it, i, dst):
                pe.wait_ge(s_w[i], 16 * (it + 1))
                for k in range(KT):
                    ins = pe.matmul(dst, wslot[i][:, k, :], hT[:, k, :], start=(k == 0), stop=(k == KT - 1))
                    yield ins
                ins.then_inc(names[f"tile{i}"].sem, 1)

            def whole(steps):
                for _ in steps:
                    pass

            with pe.Fori(0, HEADS) as h:
                on_before(pe, "gate1", h)
                whole(project(h, 0, ps[:, 0, 0:T]))
                whole(project(h, 1, ps[:, 0, T:HT]))
                whole(project(h, 2, ps[:, 1, 0:T]))
                whole(project(h, 3, ps[:, 1, T:HT]))
                whole(project(h, 4, ps[:, 2, 0:T]))
                pe.wait_ge(s_w[5], 16 * (h + 1))
                for c in range(NC):
                    for k in range(KT):
                        ins = pe.matmul(ps[:, 2, T + c * P:T + (c + 1) * P], hT[:, k, c * P:(c + 1) * P], wslot[5][:, k, :],
                                        start=(k == 0), stop=(k == KT - 1))
                ins.then_inc(names["tile5"].sem, 1)
                on(pe, "att_sq", h)
                pe.matmul(ps[:, 3, :], ones, sqm, start=True, stop=True).then_inc(done("att_ss"), 1)
                on_before(pe, "dn_kept", h)
                on(pe, "att_gain", h)
                pe.matmul(ps[:, 4, :], swap, qg, start=True, stop=True).then_inc(done("moba_rot"), 1)

                def fillers():
                    on_before(pe, "z_kept", h)
                    on_before(pe, "gate0", h)
                    yield from project(h, 6, ps[:, 7, 0:T])
                    yield from project(h, 7, ps[:, 7, T:HT])
                    yield from project(h, 8, ps[:, 0, 0:T])

                filler = fillers()

                def fill(n):
                    for _ in range(n):
                        next(filler, None)

                on(pe, "Gm_ready", h)
                pe.matmul(ps[:, 5, 0:T], after, Gm[:, 0:T], start=True, stop=False, skip_group_check=True)
                pe.matmul(ps[:, 5, P:T], ones, Gm[:, T:384], start=False, stop=True, skip_group_check=True)
                pe.matmul(ps[:, 5, T:384], after, Gm[:, T:384], start=True, stop=True, skip_group_check=True).then_inc(done("gdiff"), 1)
                on(pe, "dn_sq", h)
                on(pe, "att_std", h)
                pe.matmul(ps[:, 3, :], ones, sqd, start=True, stop=True).then_inc(done("dn_ss"), 1)
                on(pe, "silu", h)
                on(pe, "decay", h)
                for c in range(NC):
                    ins = pe.transpose(ps[:, 5, c * P:(c + 1) * P], sl[:, 2, c * P:(c + 1) * P], ident)
                ins.then_inc(done("dv_turned"), 1)
                fill(2)
                on(pe, "att_qk", h)
                on_before(pe, "att_kept", h)
                pe.matmul(ps[:, 6, 0:P], qk[:, 0:P], qk[:, T:T + P], start=True, stop=True)
                pe.matmul(ps[:, 6, P:384], qk[:, P:T], qk[:, T:HT], start=True, stop=True).then_inc(done("scores"), 1)
                fill(2)
                on(pe, "dn_kq", h)
                pe.matmul(ps[:, 4, :], kq[:, 0:P], kq, start=True, stop=True).then_inc(done("kq_dots0"), 1)
                on(pe, "dv_kept", h)
                pe.matmul(ps[:, 5, 0:T].rearrange("p (i j) -> p i j", i=2), kq[:, P:T],
                          kq.rearrange("p (i t) -> p i t", i=2)[:, :, P:T], start=True, stop=True).then_inc(done("kq_dots1"), 1)
                fill(4)
                on(pe, "B_first", h)
                for c in range(NC):
                    ins = pe.transpose(ps[:, 2, c * P:(c + 1) * P], BT[:, 0, c * P:(c + 1) * P], ident)
                ins.then_inc(done("lvlZ"), 1)
                fill(2)
                on(pe, "BT_ready", h)
                for s in range(1, LEVELS):
                    on(pe, "lvlX", h * LEVELS + (s - 1))
                    for c in range(NC):
                        a, b = c * P, (c + 1) * P
                        ins = pe.matmul(ps[:, 1, a:b], BT[:, s, a:b], X[:, a:b], start=True, stop=True)
                    ins.then_inc(done("lvlY"), 1)
                    if s == 2:
                        on(pe, "pnorm", h)
                        on(pe, "AT_ready", h)
                        pe.transpose(ps[:, 5, 0:P], pr[:, 0:P], ident)
                        pe.transpose(ps[:, 5, P:T], pr[:, P:T], ident)
                        pe.transpose(ps[:, 5, T:384], pr[:, T:384], ident).then_inc(done("p_turned"), 1)
                    if s == 4:
                        on(pe, "pT_ready", h)
                        pe.matmul(ps[:, 6, 0:T], vtok[:, 0:P], pT[:, 0:T], start=True, stop=False, skip_group_check=True)
                        pe.matmul(ps[:, 6, P:T], vtok[:, P:T], pT[:, T:384], start=False, stop=True,
                                  skip_group_check=True).then_inc(done("att_out"), 1)
                    fill(1)
                    on(pe, "lvlYc", h * (LEVELS - 1) + (s - 1))
                    for c in range(NC):
                        a, b = c * P, (c + 1) * P
                        if s < LEVELS - 1:
                            pe.matmul(ps[:, 2, a:b], XT[:, a:b], Y[:, a:b], start=True, stop=True)
                        ins = pe.matmul(ps[:, 2, T + a:T + b], Y[:, a:b], XT[:, a:b], start=True, stop=True)
                    ins.then_inc(done("lvlZ"), 1)
                    fill(1)
                on(pe, "lvlX", h * LEVELS + (LEVELS - 1))
                on(pe, "dv_kept", h)
                pe.matmul(ps[:, 1, 0:P], XT[:, 0:P], dv[:, 0:P], start=True, stop=True).then_inc(done("sol0"), 1)
                fill(1)
                on(pe, "vp0", h)
                pe.matmul(ps[:, 2, 0:P], LT[:, P:T], vp[:, 0:P], start=True, stop=True).then_inc(done("cross"), 1)
                fill(1)
                on(pe, "w1_ready", h)
                pe.matmul(ps[:, 1, 0:P], XT[:, P:T], w1, start=True, stop=True).then_inc(done("sol1"), 1)
                fill(24)
                on(pe, "vn_ready", h)
                on(pe, "AT_ready", h)
                pe.matmul(ps[:, 4, 0:T], vn[:, 0:P], AT[:, 0:T], start=True, stop=False, skip_group_check=True)
                pe.matmul(ps[:, 4, P:T], vn[:, P:T], AT[:, T:384], start=False, stop=True,
                          skip_group_check=True).then_inc(done("dn_out"), 1)

            with pe.Fori(HEADS, HEADS + MEM_HEADS) as it:
                def product(i, dst, rhs):
                    pe.wait_ge(s_w[i], 16 * (it + 1))
                    for k in range(KT):
                        ins = pe.matmul(dst, wslot[i][:, k, :], rhs[:, k, :], start=(k == 0), stop=(k == KT - 1))
                        yield ins
                    ins.then_inc(done(f"tile{i}"), 1)

                on_before(pe, "gate1", HEADS)
                for i in range(2):
                    whole(product(i, ps[:, 0, i * T:(i + 1) * T], hT))
                for i in range(2):
                    whole(product(2 + i, ps[:, 1, i * T:(i + 1) * T], memhT))
                on(pe, "dn_sq", it)
                on_before(pe, "att_kept", it)
                pe.matmul(ps[:, 6, :], ones, sqd, start=True, stop=True).then_inc(done("dn_ss"), 1)
                for i in range(2):
                    pe.wait_ge(s_w[4 + i], 16 * (it + 1))
                    for c in range(NC):
                        for k in range(KT):
                            ins = pe.matmul(ps[:, 2, c * T + i * P:c * T + (i + 1) * P], memhT[:, k, c * P:(c + 1) * P],
                                            wslot[4 + i][:, k, :], start=(k == 0), stop=(k == KT - 1))
                    ins.then_inc(done(f"tile{4 + i}"), 1)
                on(pe, "att_sq", it)
                for a in range(2):
                    for i in range(2):
                        ins = pe.matmul(ps[:, 3, a * T:(a + 1) * T], ones, msq[:, (2 * a + i) * T:(2 * a + i + 1) * T],
                                        start=(i == 0), stop=(i == 1))
                ins.then_inc(done("att_ss"), 1)

                def fillers():
                    on_before(pe, "gate0", it)
                    yield from product(6, ps[:, 7, 0:T], hT)
                    yield from product(7, ps[:, 7, T:HT], hT)

                filler = fillers()

                def fill(n):
                    for _ in range(n):
                        next(filler, None)

                fill(6)
                on(pe, "att_qk", it)
                for c in range(NC):
                    for i in range(2):
                        ins = pe.matmul(ps[:, 4, c * T:(c + 1) * T], mqk4[:, 0, i, c * P:(c + 1) * P], mqk4[:, 1, i, :],
                                        start=(i == 0), stop=(i == 1))
                ins.then_inc(done("scores"), 1)
                fill(8)
                on(pe, "pnorm", it)
                for m in range(NC):
                    for c in range(NC):
                        ins = pe.transpose(ps[:, 5, m * T + c * P:m * T + (c + 1) * P], mpr[:, c * T + m * P:c * T + (m + 1) * P], ident)
                ins.then_inc(done("p_turned"), 1)
                fill(8)
                on(pe, "pT_ready", it)
                on(pe, "dv_kept", it)
                on(pe, "dn_std", it)
                for i in range(2):
                    for m in range(NC):
                        ins = pe.matmul(ps[:, 6, i * T:(i + 1) * T], mv[:, m * T + i * P:m * T + (i + 1) * P],
                                        mpT[:, m * T:(m + 1) * T], start=(m == 0), stop=(m == NC - 1))
                ins.then_inc(done("att_out"), 1)

            pe.wait_ge(done("att_kept"), 1 + HEADS + MEM_HEADS)
            pe.wait_ge(done("dn_scaled"), MEM_HEADS)
            with pe.Fori(0, KT // 2) as mp:
                for j in range(2):
                    m = mp * 2 + j
                    pe.wait_ge(done("br_prod"), m + 1)
                    for n in range(3):
                        i = 3 * j + n
                        pe.wait_ge(s_w[i], (mp + (HEADS + MEM_HEADS + 1)) * 16)
                        for k in range(KT):
                            ins = pe.matmul(ps[:, i, 0:T], wslot[i][:, k, :], branch[:, 8 * n + k, :], start=(k == 0), stop=(k == KT - 1))
                        ins.then_inc(done(f"tile{i}"), 1)
            pe.wait_ge(done("br_mix"), KT)
            pe.wait_ge(s_wo, 32)
            for c in range(NC):
                for n in range(2):
                    for k in range(KT):
                        w = wring[:, (6 + k) * D:(7 + k) * D] if k < 3 else wo_late[:, k - 3, :]
                        ins = pe.matmul(ps[:, 2 * c + n, :], mixT[:, k, c * P:(c + 1) * P], w[:, n * 512:(n + 1) * 512],
                                        start=(k == 0), stop=(k == KT - 1))
                    ins.then_inc(done("gdots"), 1)
            pe.wait_ge(done("x1_ready"), 4)
            for b in range(4):
                pe.wait_ge(t_h2, 4 + b // 2)
                for k in range(4):
                    at = (4 * (b % 2) + k) * P
                    ins = pe.transpose(ps[:, b, k * P:(k + 1) * P], h2[:, b // 2, at:at + P], ident)
                ins.then_inc(t_tr, 1)
            pe.wait_ge(s_keys, 32)
            for i in range(2):
                ins = pe.transpose(ps[:, 6, i * P:(i + 1) * P], keys[:, i, :], ident)
            ins.then_inc(t_tr, 1)

            def route_pe(h):
                pe.wait_ge(s_wq, (h + 1) * 32)
                for i in range(2):
                    for k in range(KT):
                        ins = pe.matmul(ps[:, 4, i * T:(i + 1) * T], wq[:, i, k, :], h2T[:, k, :], start=(k == 0), stop=(k == KT - 1))
                ins.then_inc(done("p_q"), 1)
                on(pe, "p_q", h)
                pe.sem_inc(done("wq_used"), 1)
                on(pe, "p_qk", h)
                for c in range(NC):
                    for i in range(2):
                        ins = pe.matmul(ps[:, 5, (2 * c + i) * P:(2 * c + i + 1) * P], pq[:, i * T + c * P:i * T + (c + 1) * P],
                                        keysT[:, i * P:(i + 1) * P], start=True, stop=True)
                ins.then_inc(done("p_s"), 1)

            def chunk_pe(h, c, last=False):
                n = h * NC + c
                for k in range(TOPK):
                    if k % 2 == 0:
                        pe.wait_ge(s_v[k // 2], (n + 1) * 32)
                    on(pe, "diag", n * TOPK + k)
                    for half in range(2):
                        ins = pe.matmul(ps[:, 2 * c + half, :], diag[:, k % 8, :], ring[:, TOPK + k, half * 512:(half + 1) * 512],
                                        start=False, stop=last and k == TOPK - 1, skip_group_check=True)
                    ins.then_inc(done("vrow"), 1)

            pe.wait_ge(s_gate, 17)
            for b in range(4):
                ins = pe.matmul(ps[:, b, :], mask[:, P:T], h2[:, 0, 0:512], start=True, stop=False, skip_group_check=True)
            pe.sem_inc(done("vrow"), TOPK)
            route_pe(0)

            def head_pe(h, last=False):
                chunk_pe(h, 0, last)
                if not last:
                    route_pe(h + 1)
                chunk_pe(h, 1, last)

            with pe.Fori(0, PHEADS // 2 - 1) as pair:
                head_pe(pair * 2)
                head_pe(pair * 2 + 1)
            head_pe(PHEADS - 2)
            head_pe(PHEADS - 1, True)
            pe.wait_ge(done("vrow"), TOPK + PHEADS * NC * TOPK)
            pe.sem_inc(done("vmm_end"), 1)


_INS = ["x", "mem", "attn_norm_g", "mem_norm_g", "ffn_norm_g", "w_in", "moba_q_norm_g", "moba_k_norm_g", "dn_conv_w",
        "dn_a_log", "dn_dt_bias", "dn_out_norm_g", "w_mem_kv", "mem_q_norm_g", "mem_k_norm_g", "w_branch", "w_out",
        "peer_w_q", "peer_keys1", "peer_keys2", "peer_u", "peer_v"]


def kernel(**inputs):
    import concourse.bacc as bacc
    from concourse.bass_utils import run_bass_kernel_spmd

    nc = bacc.Bacc("TRN2", target_bir_lowering=False, num_devices=1)
    table, where = constants()
    arrays = {"constants_dram": table}
    d = {}
    for name in _INS:
        a = np.ascontiguousarray(inputs[name])
        arrays[f"in_{name}_dram"] = a
        d[name] = nc.dram_tensor(f"in_{name}_dram", a.shape, mybir.dt.from_np(a.dtype), kind="ExternalInput").ap()
    cst = nc.dram_tensor("constants_dram", table.shape, F32, kind="ExternalInput").ap()
    out = nc.dram_tensor("out_dram", (1, T, D), F32, kind="ExternalOutput").ap()

    def as_rows(name):
        return d[name].rearrange("o (r c) -> (o r) c", c=P)

    rows = [(R_CONV, d["dn_conv_w"].rearrange("o j (r c) -> (o j r) c", c=P)), (R_ATTN, as_rows("attn_norm_g")),
            (R_MEM, as_rows("mem_norm_g")), (R_MQ, as_rows("moba_q_norm_g")), (R_MK, as_rows("moba_k_norm_g")),
            (R_DN, as_rows("dn_out_norm_g")), (R_CQ, as_rows("mem_q_norm_g")), (R_CK, as_rows("mem_k_norm_g"))]
    hybrid_layer(nc, cst, where, d["x"][0], d["mem"][0], rows, d["w_in"][0], d["dn_a_log"][0], d["dn_dt_bias"][0],
                 d["ffn_norm_g"][0], d["w_mem_kv"][0], d["w_branch"][0], d["w_out"][0], d["peer_w_q"][0],
                 d["peer_keys1"][0], d["peer_keys2"][0], d["peer_u"][0], d["peer_v"][0], out[0])
    r = run_bass_kernel_spmd(nc, [arrays], core_ids=[0])
    return r.results[0]["out_dram"]
```

```python
from contextlib import ExitStack

import numpy as np

import concourse.bass as bass
from concourse import mybir

F32 = mybir.dt.float32
U32 = mybir.dt.uint32
ALU = mybir.AluOpType
ACT = mybir.ActivationFunctionType
AX = mybir.AxisListType

P = 128
T = 256
NC = T // P
D = 1024
KT = D // P
HEADS = 8
HD = 128
MEM_HEADS = 4
EPS = 1e-6
LEVELS = 7

C_MQ, C_MK, C_MV = 0, 1024, 2048
C_DQ, C_DK, C_DV = 3072, 4096, 5120
C_BA = 6144
C_Z = 6160
C_CQ = 7184
C_G = 8208
IN_W = 11280

NEXP = 16384
NKEY = 128
TOPK = 16
PHEADS = 8
UNITS = PHEADS * NC
RING = 8
QW = 2 * NKEY

R_CONV = 0
R_ATTN = 96
R_MEM = 104
R_MQ, R_MK, R_DN = 112, 113, 114
R_CQ, R_CK = 115, 117
NROWS = 119

NEG = -1.0e30


def constants():
    i = np.arange(P)
    ident = np.eye(P, dtype=np.float32)
    after = (i[:, None] > i[None, :]).astype(np.float32)
    upto = (i[:, None] <= i[None, :]).astype(np.float32)
    ones = np.ones((P, P), np.float32)
    causal = np.where(i[None, :] <= i[:, None], 0.0, NEG).astype(np.float32)
    zeros = np.zeros((P, P), np.float32)
    swap = np.zeros((P, P), np.float32)
    half = HD // 2
    for d in range(half):
        swap[d + half, d] = -1.0
        swap[d, d + half] = 1.0
    inv = (1.0 / (np.float32(10000.0) ** (np.arange(0, HD, 2, dtype=np.float32) / np.float32(HD)))).astype(np.float32)
    ang = (np.arange(T, dtype=np.float32)[:, None] * inv[None, :]).astype(np.float32)
    cos = np.cos(ang.astype(np.float64)).astype(np.float32).T
    sin = np.sin(ang.astype(np.float64)).astype(np.float32).T
    cos, sin = np.concatenate([cos, cos]), np.concatenate([sin, sin])
    levels = []
    for n in range(LEVELS):
        s = 1 << n
        same = i[:, None] // (2 * s) == i[None, :] // (2 * s)
        low = (i[None, :] % (2 * s) >= s) & (i[:, None] % (2 * s) < s)
        levels.append((same & low).astype(np.float32))
    eps = np.full((P, 1), EPS, np.float32)
    iota = np.tile(np.arange(TOPK, dtype=np.float32), (P, 1))
    parts = {
        "ident": ident, "after": after, "ones": ones, "swap": swap,
        "upto": np.concatenate([upto, ones, upto], 1),
        "mask": np.concatenate([causal, zeros, causal], 1),
        "cos": cos, "sin": sin, "levels": np.concatenate(levels, 1), "eps": eps, "iota": iota,
    }
    at, where = 0, {}
    for k, v in parts.items():
        where[k] = (at, v.shape[1])
        at += v.shape[1]
    return np.ascontiguousarray(np.concatenate(list(parts.values()), 1), dtype=np.float32), where


class Event:

    def __init__(self, sem, primed=0):
        self.sem, self.primed = sem, primed

    def now(self, it):
        return it + (1 + self.primed)

    def before(self, it):
        assert self.primed
        return it + 1


def hybrid_layer(nc, cst_d, where, x_d, mem_d, rows, w_in, a_log, dt_bias, ffn_g, w_kv, w_branch, w_out,
                 w_q, keys1, keys2, peer_u, peer_v, out_d):
    with ExitStack() as ctx:
        def sb(name, shape, dt=F32):
            return ctx.enter_context(nc.sbuf_tensor(name, shape, dt))

        def sem(name):
            return ctx.enter_context(nc.semaphore(name))

        PH1 = 41472
        arena = sb("arena", [P, PH1])
        cst = sb("cst", [P, cst_d.shape[1]])
        x1 = sb("x1", [P, NC, D])
        h2 = sb("h2", [P, NC, D])
        small = sb("small", [P, 512])
        ps = ctx.enter_context(nc.psum_tensor("ps", [P, 8, 512], F32))

        def const(name):
            a, n = where[name]
            return cst[:, a:a + n]

        ident, after, ones, swap = const("ident"), const("after"), const("ones"), const("swap")
        upto, mask, cos, sin = const("upto"), const("mask"), const("cos"), const("sin")
        levels = const("levels").rearrange("p (s j) -> p s j", s=LEVELS)
        eps, iota = const("eps"), const("iota")

        taken = [0]

        def carve(words):
            a = taken[0]
            taken[0] += words
            assert taken[0] <= PH1, taken[0]
            return arena[:, a:a + words]

        wq = arena[:, 0:16 * D].rearrange("p (k n) -> p k n", k=KT)
        ring = arena[:, 16 * D:32 * D].rearrange("p (s n) -> p s n", s=2 * RING)
        gates = carve(3 * KT * T).rearrange("p (k t) -> p k t", t=T)
        branch = carve(3 * KT * T).rearrange("p (k t) -> p k t", t=T)
        zT = carve(KT * T).rearrange("p (k t) -> p k t", t=T)
        WS = 9
        wring = carve(WS * D)
        wslot = [wring[:, D * s:D * (s + 1)].rearrange("p (k j) -> p k j", k=KT) for s in range(WS)]
        hT = carve(KT * T).rearrange("p (k t) -> p k t", t=T)
        memhT = carve(KT * T).rearrange("p (k t) -> p k t", t=T)
        stage0 = taken[0]

        cols = small[:, 0:NROWS]
        gtok = small[:, 120:136].rearrange("p (c h) -> p c h", c=NC)
        btok = small[:, 136:152].rearrange("p (c h) -> p c h", c=NC)
        ss4 = small[:, 152:156]
        rstd4 = small[:, 156:160]
        var4 = small[:, 160:164]
        arow = small[:, 164:172]
        dtrow = small[:, 172:180]
        ba = small[:, 180:212].rearrange("p (c n) -> p c n", c=NC)
        ya = small[:, 212:228].rearrange("p (c n) -> p c n", c=NC)
        yb = small[:, 228:244].rearrange("p (c n) -> p c n", c=NC)
        yc = small[:, 244:260].rearrange("p (c n) -> p c n", c=NC)
        gfull = sb("gfull", [P, D])
        keysT = sb("keysT", [P, 2 * P])
        sq2, std2, rstd2 = small[:, 260:262], small[:, 262:264], small[:, 264:266]
        wba_t = sb("wba", [P, KT, 16])

        xin = carve(2 * NC * D).rearrange("p (s n) -> p s n", s=2 * NC)
        junk = carve(D)
        rows_sb = carve(P)
        keys_in = carve(2 * P).rearrange("p (i d) -> p i d", i=2)
        taken[0] = stage0

        s_cst, s_rows, s_x, s_mem, s_ba, s_rowb = (sem(n) for n in ("s_cst", "s_rows", "s_x", "s_mem", "s_ba", "s_rowb"))
        a_sq, d_var, a_std, d_rstd, d_xn = (sem(n) for n in ("a_sq", "d_var", "a_std", "d_rstd", "d_xn"))
        p_keys, d_keys = sem("p_keys"), sem("d_keys")
        p_cols, d_cols, p_tr, d_hT, p_ba, s_gate = (sem(n) for n in ("p_cols", "d_cols", "p_tr", "d_hT", "p_ba", "s_gate"))

        HT = 2 * T
        qg = carve(HT)
        sqm = carve(HT)
        rp1 = carve(HT)
        rp2 = carve(HT)
        qk = carve(HT)
        sm = carve(384)
        pr = carve(384)
        pT = carve(384)
        vtok = carve(T)
        cv = carve(3 * T).rearrange("p (i t) -> p i t", i=3)
        sl = carve(3 * T).rearrange("p (i t) -> p i t", i=3)
        kq = carve(HT)
        Gm = carve(384)
        Dm = carve(384)
        LT = carve(384)
        AT = carve(384)
        BT = carve(LEVELS * T).rearrange("p (s n) -> p s n", s=LEVELS)
        X = carve(T)
        XT = carve(T)
        Y = carve(T)
        dv = carve(T)
        vp = carve(T)
        vn = carve(T)
        w1 = carve(P)
        mx = carve(8)
        sqd = carve(HT)
        mqk = carve(2 * HT)
        mqk4 = mqk.rearrange("p (a i t) -> p a i t", a=2, i=2)
        msq = carve(2 * HT)
        assert taken[0] <= PH1, taken[0]
        taken[0] = stage0

        mv = BT[:, 0:2, :].rearrange("p s n -> p (s n)")
        mstd = carve(HT)
        mpr = carve(HT)
        mpT = carve(HT)
        zs = carve(HT)
        dstd = carve(HT)
        taken[0] = stage0

        mixT = hT
        prod = memhT[:, 0:3, :]
        mixs = memhT[:, 3, :]
        wo_late = carve(5 * D).rearrange("p (k n) -> p k n", k=5)
        assert taken[0] == 32 * D

        h2T = carve(KT * T).rearrange("p (k t) -> p k t", t=T)
        qtok = carve(QW)
        qT = carve(QW)
        sc0 = carve(2 * NKEY).rearrange("p (r n) -> p r n", r=2)
        sc1 = carve(2 * NKEY).rearrange("p (r n) -> p r n", r=2)
        cd0 = carve(TOPK * TOPK)
        cd1 = carve(TOPK * TOPK)
        hot = carve(2 * TOPK * TOPK)
        rv = carve(2 * TOPK).rearrange("p (r k) -> p r k", r=2)
        ri = carve(2 * TOPK).bitcast(U32).rearrange("p (r k) -> p r k", r=2)
        rf = carve(2 * TOPK).rearrange("p (r k) -> p r k", r=2)
        sv = carve(TOPK)
        ci = carve(TOPK).bitcast(U32)
        ab = carve(2 * TOPK).bitcast(U32).rearrange("p (i k) -> p i k", i=2)
        ef = carve(2 * TOPK).rearrange("p (i k) -> p i k", i=2)
        idx_u = [carve(TOPK).bitcast(U32) for _ in range(NC)]
        idx_v = [carve(TOPK).bitcast(U32) for _ in range(NC)]
        ex = carve(TOPK)
        neg = carve(2)
        sums = carve(2)
        rsum = carve(2)
        wts2 = [carve(TOPK) for _ in range(NC)]
        acts = [carve(TOPK) for _ in range(NC)]
        gelu = carve(TOPK)
        coef2 = [carve(TOPK) for _ in range(NC)]
        diag = carve(8 * P).rearrange("p (s j) -> p s j", s=8)
        assert taken[0] <= PH1, taken[0]
        s_wo, s_wq, s_keys, s_x1, s_out = (sem(n) for n in ("s_wo", "s_wq", "s_keys", "s_x1", "s_out"))
        s_u = [sem(f"s_u{i}") for i in range(RING // 2)]
        s_v = [sem(f"s_v{i}") for i in range(RING // 2)]
        t_route = sem("t_route")
        t_sp = sem("t_sp")
        t_pool = sem("t_pool")
        r_step, t_tr, p_end = sem("r_step"), sem("t_tr"), sem("p_end")
        t_h2 = [sem(f"t_h2{c}") for c in range(NC)]
        EARLY = 6
        RSTEPS = 13
        FILLS = (8, 6, 8, 6, 3, 2, 2, 3)
        MFILLS = (14, 14, 12)

        s_w = [sem(f"s_w{i}") for i in range(WS)]
        names = {}

        def ev(name, primed=0):
            if name not in names:
                names[name] = Event(sem(name), primed)
            return names[name]

        def on(eng, name, it):
            e = names[name]
            eng.wait_ge(e.sem, e.now(it))

        def on_before(eng, name, it):
            e = names[name]
            eng.wait_ge(e.sem, e.before(it))

        for i in range(WS):
            ev(f"tile{i}")
        for n in ("att_sq", "att_gain", "att_ss", "att_rot", "att_std", "rope_cos", "rope_sin", "rope_sum",
                  "att_rstd", "att_qk", "scores", "masked", "maxes", "negmax", "probs", "psums", "z_silu", "dn_scaled", "br_sum", "br_mix", "sig", "x1_ready", "x1_done", "gdots",
                  "pnorm", "p_turned", "pT_ready",
                  "conv0", "conv0v", "mv_kept", "taps", "conv3", "silu", "dn_sq", "dn_ss", "dn_std", "dn_rstd", "dn_kq",
                  "Gm_ready", "gdiff", "decay", "decay_masked", "dv_turned", "kq_dots0", "kq_dots1",
                  "LT_ready", "AT_ready", "BT_ready", "B_first", "X_first", "lvlY", "lvlYc", "lvlZ", "lvlX",
                  "att_out", "dn_out", "dv_kept", "sol0", "vp0", "cross", "w1_ready", "sol1", "vp1", "vn_ready"):
            ev(n)
        for n in ("gate0", "gate1", "z_kept", "att_kept", "dn_kept"):
            ev(n, 1)
        ev("br_prod", 2)
        for n in ("p_q", "p_qk", "p_t", "p_tk", "p_s", "p_sk", "idx_ready", "idx_kept", "negs", "exps",
                  "acts", "gelu", "coef", "weighed", "vmm_end"):
            ev(n)
        ev("dot", RING)
        ev("vrow", RING)
        ev("diag")

        block = ctx.enter_context(nc.Block())

        def w_cols(src, col):
            return src[:, bass.ds(col, P)].rearrange("(k p) j -> p k j", p=P)

        @block.sync
        def _(sp):
            sp.dma_start(cst[:, :], cst_d).then_inc(s_cst, 16)
            for first, src in rows:
                sp.dma_start(rows_sb[first:first + src.shape[0], :], src).then_inc(s_rows, 16)
            for i, k in enumerate((keys1, keys2)):
                sp.dma_start(keys_in[:, i, :], k).then_inc(s_keys, 16)
            for c in range(NC):
                sp.dma_start(xin[:, c, :], x_d[c * P:(c + 1) * P, :]).then_inc(s_x, 16)
            for c in range(NC):
                sp.dma_start(xin[:, NC + c, :], mem_d[c * P:(c + 1) * P, :]).then_inc(s_mem, 16)
            sp.dma_start(wba_t[:, :, :], w_in[:, C_BA:C_BA + 16].rearrange("(k p) n -> p k n", p=P)).then_inc(s_ba, 16)
            sp.dma_start(gfull[:, :], ffn_g.partition_broadcast(P)).then_inc(s_x1, 16)
            for c in range(NC):
                sp.dma_start(x1[:, c, :], x_d[c * P:(c + 1) * P, :]).then_inc(s_x1, 16)
            sp.dma_start(arow, a_log.partition_broadcast(P)).then_inc(s_rowb, 16)
            sp.dma_start(dtrow, dt_bias.partition_broadcast(P)).then_inc(s_rowb, 16)

            def load(it, h, wait):
                starts = [C_MQ + h * P, C_MK + h * P, C_DK + h * P, C_DQ + h * P, C_DV + h * P, C_MV + h * P,
                          C_Z + h * P, C_G + h * (2 * P), C_G + h * (2 * P) + P]
                for i, at in enumerate(starts):
                    if wait:
                        sp.wait_ge(names[f"tile{i}"].sem, it)
                    sp.dma_start(wslot[i], w_cols(w_in, at)).then_inc(s_w[i], 16)

            load(0, 0, False)
            with sp.Fori(1, HEADS) as it:
                load(it, it, True)
            with sp.Fori(0, MEM_HEADS) as mh:
                sources = [(w_in, C_CQ), (w_in, C_CQ + P), (w_kv, 0), (w_kv, P), (w_kv, D), (w_kv, D + P),
                           (w_in, C_G + 16 * P), (w_in, C_G + 17 * P)]
                for i, (src, at) in enumerate(sources):
                    sp.wait_ge(names[f"tile{i}"].sem, mh + HEADS)
                    sp.sem_inc(t_sp, 1)
                    sp.dma_start(wslot[i], w_cols(src, mh * (2 * P) + at)).then_inc(s_w[i], 16)
            with sp.Fori(0, KT // 2) as m:
                for i in range(6):
                    sp.wait_ge(names[f"tile{i}"].sem, m + (HEADS + MEM_HEADS))
                    sp.sem_inc(t_sp, 1)
                    sp.dma_start(wslot[i], w_cols(w_branch[i % 3], m * (2 * P) + (i // 3) * P)).then_inc(s_w[i], 16)
                
            for i in (6, 7):
                sp.wait_ge(names[f"tile{i}"].sem, HEADS + MEM_HEADS)
            sp.wait_ge(names["tile8"].sem, HEADS)
            sp.wait_ge(names["att_kept"].sem, 1 + HEADS + MEM_HEADS)
            sp.wait_ge(names["dn_scaled"].sem, MEM_HEADS)
            sp.dma_start(wring[:, 6 * D:9 * D].rearrange("p (k n) -> p k n", k=3),
                         w_out[0:3 * P, :].rearrange("(k p) n -> p k n", p=P)).then_inc(s_wo, 16)
            sp.dma_start(wo_late, w_out[3 * P:D, :].rearrange("(k p) n -> p k n", p=P)).then_inc(s_wo, 16)
            for i in range(6):
                sp.wait_ge(names[f"tile{i}"].sem, HEADS + MEM_HEADS + KT // 2)
            sp.wait_ge(names["br_mix"].sem, KT)
            for k in range(0, KT, 2):
                sp.dma_start(wq[:, k:k + 2, :], w_q[k * P:(k + 2) * P, :].rearrange("(k p) n -> p k n", p=P)).then_inc(s_wq, 16)
            for c in range(NC):
                sp.wait_ge(p_end, c + 1)
                sp.dma_start(out_d[c * P:(c + 1) * P, :], x1[:, c, :]).then_inc(s_out, 16)
            sp.wait_ge(s_out, 16 * NC)

        @block.scalar
        def _(act):
            for s in range(2 * NC):
                act.wait_ge(s_x if s < NC else s_mem, 16 * NC)
                if s:
                    act.wait_ge(a_sq, s)
                act.activation(junk, xin[:, s, :], ACT.Square, accum_out=ss4[:, s:s + 1]).then_inc(a_sq, 1)
            act.wait_ge(d_var, 1)
            act.activation(var4, var4, ACT.Sqrt).then_inc(a_std, 1)
            act.wait_ge(p_ba, 1)
            act.activation(yb, ps[:, 0, 0:32].rearrange("p (c n) -> p c n", c=NC)[:, :, 0:8], ACT.Exp, scale=-1.0).then_inc(s_gate, 1)
            act.wait_ge(s_rowb, 32)
            act.activation(arow, arow, ACT.Exp).then_inc(s_gate, 1)
            act.wait_ge(s_gate, 6)
            act.activation(yc, ya, ACT.Abs).then_inc(s_gate, 1)
            act.wait_ge(s_gate, 7)
            act.activation(yc, yc, ACT.Exp, scale=-1.0).then_inc(s_gate, 1)
            act.wait_ge(s_gate, 8)
            act.activation(yc, yc, ACT.Ln, bias=1.0).then_inc(s_gate, 1)

            act.wait_ge(s_rows, 16 * len(rows))
            act.wait_ge(d_cols, 1)
            for n in ("gate0", "gate1", "z_kept", "att_kept", "dn_kept"):
                act.sem_inc(names[n].sem, 1)

            def copy(name, dst, src):
                act.activation(dst, src, ACT.Copy).then_inc(names[name].sem, 1)

            def evacuate(h):
                on(act, "tile1", h)
                act.activation(sqm, ps[:, 0, :], ACT.Square).then_inc(names["att_sq"].sem, 1)
                act.activation(qg[:, 0:T], ps[:, 0, 0:T], ACT.Copy, scale=cols[:, R_MQ:R_MQ + 1])
                act.activation(qg[:, T:HT], ps[:, 0, T:HT], ACT.Copy, scale=cols[:, R_MK:R_MK + 1]).then_inc(names["att_gain"].sem, 1)
                on(act, "tile3", h)
                for i, tile in ((0, 8), (1, 0)):
                    tap = small[:, bass.ds(h + (R_CONV + 3 * 24 + tile), 1)]
                    ins = act.activation(cv[:, i, :], ps[:, 1, i * T:(i + 1) * T], ACT.Copy, scale=tap)
                ins.then_inc(names["conv0"].sem, 1)

            def evacuate_v(h):
                on(act, "tile5", h)
                act.activation(vtok, ps[:, 2, T:HT], ACT.Copy)
                tap = small[:, bass.ds(h + (R_CONV + 3 * 24 + 16), 1)]
                act.activation(cv[:, 2, :], ps[:, 2, 0:T], ACT.Copy, scale=tap).then_inc(names["conv0v"].sem, 1)

            def evacuate_mem(it):
                for a, gain in ((0, R_CQ), (1, R_CK)):
                    on(act, f"tile{2 * a + 1}", it)
                    ins = act.activation(msq[:, a * HT:(a + 1) * HT], ps[:, a, :], ACT.Square)
                    if a:
                        ins.then_inc(names["att_sq"].sem, 1)
                    for i in range(2):
                        ins = act.activation(mqk4[:, a, i, :], ps[:, a, i * T:(i + 1) * T], ACT.Copy, scale=cols[:, gain + i:gain + i + 1])
                ins.then_inc(names["att_gain"].sem, 1)

            def evacuate_mem_v(it):
                on(act, "tile5", it)
                copy("mv_kept", mv, ps[:, 2, :])

            def head(h, then, then_v):
                on(act, "conv3", h)
                act.activation(sl[:, :, :], cv[:, :, :], ACT.Silu).then_inc(names["silu"].sem, 1)
                on(act, "silu", h)
                act.activation(sqd, sl[:, 0:2, :].rearrange("p i t -> p (i t)"), ACT.Square).then_inc(names["dn_sq"].sem, 1)
                on(act, "att_ss", h)
                act.activation(rp1, ps[:, 3, :], ACT.Sqrt, bias=eps, scale=1.0 / HD).then_inc(names["att_std"].sem, 1)
                on(act, "dn_ss", h)
                act.activation(kq, ps[:, 3, :], ACT.Sqrt, bias=eps, scale=1.0).then_inc(names["dn_std"].sem, 1)
                on(act, "gdiff", h)
                act.activation(Dm, ps[:, 5, 0:384], ACT.Exp).then_inc(names["decay"].sem, 1)
                on(act, "dv_turned", h)
                copy("dv_kept", dv, ps[:, 5, 0:T])
                on(act, "negmax", h)
                act.activation(pr[:, 0:P], sm[:, 0:P], ACT.Exp, bias=mx[:, 2:3], scale=float(HD) ** -0.5, accum_out=mx[:, 4:5])
                act.activation(pr[:, P:384], sm[:, P:384], ACT.Exp, bias=mx[:, 3:4], scale=float(HD) ** -0.5,
                               accum_out=mx[:, 5:6]).then_inc(names["probs"].sem, 1)
                on(act, "tile7", h)
                copy("z_kept", zT[:, bass.ds(h, 1), :], ps[:, 7, None, 0:T])
                copy("gate0", gates[:, bass.ds(h * 2, 1), :], ps[:, 7, None, T:HT])
                on(act, "p_turned", h)
                copy("pT_ready", pT, ps[:, 5, 0:384])
                on(act, "tile8", h)
                copy("gate1", gates[:, bass.ds(h * 2 + 1, 1), :], ps[:, 2, None, 0:T])
                on(act, "att_out", h)
                copy("att_kept", branch[:, bass.ds(h, 1), :], ps[:, 6, None, 0:T])
                then(h + 1)
                on(act, "dn_out", h)
                copy("dn_kept", branch[:, bass.ds(h + 8, 1), :], ps[:, 4, None, 0:T])
                then_v(h + 1)

            evacuate(0)
            evacuate_v(0)
            with act.Fori(0, HEADS - 1) as h:
                head(h, evacuate, evacuate_v)
            head(HEADS - 1, evacuate_mem, evacuate_mem_v)

            def mem_head(it, last=False):
                two = lambda a: a.rearrange("p (i t) -> p i t", i=2)
                heads = branch[:, bass.ds((it - HEADS) * 2 + 8, 2), :]
                act.activation(two(sqd), heads, ACT.Square).then_inc(names["dn_sq"].sem, 1)
                on(act, "att_ss", it)
                act.activation(mstd, ps[:, 3, :], ACT.Sqrt, bias=eps, scale=1.0 / (2 * HD)).then_inc(names["att_std"].sem, 1)
                on(act, "dn_ss", it)
                act.activation(dstd, ps[:, 6, :], ACT.Sqrt, bias=eps, scale=1.0 / HD).then_inc(names["dn_std"].sem, 1)
                act.activation(two(zs), zT[:, bass.ds((it - HEADS) * 2, 2), :], ACT.Silu).then_inc(names["z_silu"].sem, 1)
                on(act, "negmax", it)
                for c in range(NC):
                    ins = act.activation(mpr[:, c * T:(c + 1) * T], ps[:, 4, c * T:(c + 1) * T], ACT.Exp, bias=mx[:, 2 + c:3 + c],
                                         scale=float(2 * HD) ** -0.5, accum_out=mx[:, 4 + c:5 + c])
                ins.then_inc(names["probs"].sem, 1)
                on(act, "tile7", it)
                copy("gate0", gates[:, bass.ds((it - HEADS) * 2 + 16, 2), :], two(ps[:, 7, :]))
                on(act, "p_turned", it)
                copy("pT_ready", mpT, ps[:, 5, :])
                on(act, "att_out", it)
                copy("att_kept", branch[:, bass.ds((it - HEADS) * 2 + 16, 2), :], two(ps[:, 6, :]))
                if not last:
                    evacuate_mem(it + 1)
                    evacuate_mem_v(it + 1)

            with act.Fori(HEADS, HEADS + MEM_HEADS - 1) as it:
                mem_head(it)
            mem_head(HEADS + MEM_HEADS - 1, True)
            act.wait_ge(names["gate0"].sem, 1 + HEADS + MEM_HEADS)
            for n in range(3):
                act.activation(gates[:, 8 * n:8 * n + 8, :], gates[:, 8 * n:8 * n + 8, :], ACT.Sigmoid).then_inc(names["sig"].sem, 1)
            def route_act(n):
                on(act, "p_q", n)
                copy("p_qk", qtok, ps[:, 4, 0:QW])
                on(act, "p_t", n)
                copy("p_tk", qT, ps[:, 5, 0:QW])
                on(act, "p_s", n)
                copy("p_sk", sc0.rearrange("p r n -> p (r n)"), ps[:, 6, 0:2 * NKEY])

            def exps_act(n):
                on(act, "negs", n)
                act.activation(ex, sv, ACT.Exp, bias=neg[:, 0:1], accum_out=sums[:, 0:1]).then_inc(names["exps"].sem, 1)

            def gelu_act(n, c):
                on(act, "acts", n)
                act.activation(gelu, acts[c], ACT.Gelu_apprx_tanh).then_inc(names["gelu"].sem, 1)

            def diag_act(n, c):
                on(act, "coef", n)
                for k in range(TOPK):
                    act.wait_ge(names["vrow"].sem, n * TOPK + (k + 1))
                    act.activation(diag[:, k % 8, :], ident, ACT.Copy, scale=coef2[c][:, k:k + 1]).then_inc(names["diag"].sem, 1)

            def phase_act(n, c, route=True):
                gelu_act(n, c)
                if route:
                    route_act(n + 2)
                diag_act(n, c)
                if route:
                    exps_act(n + 2)

            def norm_act(c):
                act.wait_ge(names["x1_ready"].sem, 2 * (c + 1))
                act.activation(h2[:, c, :], x1[:, c, :], ACT.Square, accum_out=sq2[:, c:c + 1]).then_inc(names["x1_done"].sem, 1)
                act.wait_ge(t_h2[c], 1)
                act.activation(std2[:, c:c + 1], std2[:, c:c + 1], ACT.Sqrt).then_inc(t_h2[c], 1)

            norm_act(0)
            route_act(0)
            exps_act(0)
            norm_act(1)
            route_act(1)
            exps_act(1)
            with act.Fori(0, PHEADS - 1) as h:
                phase_act(h * NC, 0)
                phase_act(h * NC + 1, 1)
            phase_act(UNITS - 2, 0, False)
            phase_act(UNITS - 1, 1, False)

        @block.gpsimd
        def _(pool):
            with pool.Fori(0, HEADS) as h:
                on(pool, "decay", h)
                pool.tensor_tensor(Dm, Dm, upto, ALU.mult).then_inc(names["decay_masked"].sem, 1)
                on(pool, "LT_ready", h)
                for s in range(LEVELS):
                    for c in range(NC):
                        ins = pool.tensor_tensor(BT[:, s, c * P:(c + 1) * P], LT[:, c * T:c * T + P], levels[:, s, :], ALU.mult)
                    if s == 0:
                        ins.then_inc(names["B_first"].sem, 1)
                ins.then_inc(names["BT_ready"].sem, 1)

            def gather(table, used, landed, first, idx, n, k):
                pool.wait_ge(names[used].sem, n * TOPK + (k + 1))
                pool.sem_inc(t_pool, 1)
                pool.indirect_dma_start(ring[:, first + k % RING, :], None, table,
                                        bass.IndirectOffsetOnAxis(ap=idx[:, k:k + 1], axis=0)).then_inc(landed[k % RING // 2], 16)

            def phase_pool(n, c, more=True):
                if more:
                    on(pool, "idx_ready", n + 1)
                    pool.sem_inc(t_pool, 1)
                on(pool, "idx_kept", n)
                pool.sem_inc(t_pool, 1)
                for k in range(TOPK):
                    if more:
                        gather(peer_u, "dot", s_u, 0, idx_u[1 - c], n + 1, k)
                    gather(peer_v, "vrow", s_v, RING, idx_v[c], n, k)

            pool.sem_inc(names["dot"].sem, RING)
            on(pool, "idx_ready", 0)
            for k in range(RING):
                gather(peer_u, "dot", s_u, 0, idx_u[0], 0, k)
            on(pool, "idx_kept", 0)
            for k in range(RING):
                gather(peer_v, "vrow", s_v, RING, idx_v[0], 0, k)
            for k in range(RING, TOPK):
                gather(peer_u, "dot", s_u, 0, idx_u[0], 0, k)
            on(pool, "idx_ready", 1)
            for k in range(TOPK):
                gather(peer_u, "dot", s_u, 0, idx_u[1], 1, k)
                if k >= RING:
                    gather(peer_v, "vrow", s_v, RING, idx_v[0], 0, k)
            with pool.Fori(0, PHEADS - 1) as h:
                phase_pool(h * NC + 1, 1)
                phase_pool(h * NC + 2, 0)
            phase_pool(UNITS - 1, 1, False)

        @block.vector
        def _(dve):
            def done(name):
                return names[name].sem

            dve.wait_ge(p_cols, 1)
            dve.tensor_copy(cols, ps[:, 7, 0:NROWS]).then_inc(d_cols, 1)
            dve.wait_ge(a_sq, 2 * NC)
            dve.tensor_scalar(var4, ss4, 1.0 / D, EPS, ALU.mult, ALU.add).then_inc(d_var, 1)
            dve.wait_ge(a_std, 1)
            dve.reciprocal(rstd4, var4).then_inc(d_rstd, 1)
            dve.wait_ge(d_rstd, 1)
            for s in range(2 * NC):
                dve.tensor_scalar(xin[:, s, :], xin[:, s, :], rstd4[:, s:s + 1], None, ALU.mult).then_inc(d_xn, 1)
            dve.wait_ge(p_keys, 1)
            dve.tensor_copy(keysT[:, :], ps[:, 6, 0:2 * P]).then_inc(d_keys, 1)
            dve.wait_ge(d_cols, 1)
            for b in range(8):
                s, half = b // 2, b % 2
                c = s % NC
                gain = (R_ATTN if s < NC else R_MEM) + 4 * half
                dst = (hT if s < NC else memhT)[:, 4 * half:4 * half + 4, c * P:(c + 1) * P]
                dve.wait_ge(p_tr, b + 1)
                dve.tensor_tensor(dst, ps[:, b, :].rearrange("p (k t) -> p k t", k=4),
                                  cols[:, gain:gain + 4, None].to_broadcast([P, 4, P]), ALU.mult).then_inc(d_hT, 1)
            dve.wait_ge(s_gate, 2)
            dve.tensor_scalar(yb, yb, 1.0, None, ALU.add).then_inc(s_gate, 1)
            dve.wait_ge(s_gate, 3)
            dve.reciprocal(btok, yb).then_inc(s_gate, 1)
            dve.tensor_tensor(ya, ps[:, 0, 0:32].rearrange("p (c n) -> p c n", c=NC)[:, :, 8:16],
                              dtrow[:, None, :].to_broadcast([P, NC, 8]), ALU.add).then_inc(s_gate, 1)
            dve.wait_ge(s_gate, 5)
            dve.tensor_scalar(yb, ya, 0.0, None, ALU.max).then_inc(s_gate, 1)
            dve.wait_ge(s_gate, 9)
            dve.tensor_tensor(yb, yb, yc, ALU.add).then_inc(s_gate, 1)
            dve.wait_ge(s_gate, 10)
            dve.scalar_tensor_tensor(out=gtok, in0=yb, scalar=-1.0, in1=arow[:, None, :].to_broadcast([P, NC, 8]),
                                     op0=ALU.mult, op1=ALU.mult).then_inc(s_gate, 1)
            dve.wait_ge(s_gate, 11)
            dve.wait_ge(s_cst, 16)


            def convolve(h):
                g0, g1 = (small[:, bass.ds(h + (120 + 8 * c), 1)] for c in range(NC))
                dve.tensor_scalar(Gm[:, 0:T], upto[:, 0:T], g0, None, ALU.mult)
                dve.tensor_scalar(Gm[:, T:384], upto[:, T:384], g1, None, ALU.mult).then_inc(done("Gm_ready"), 1)
                for part, tiles in (("conv0", ((0, 8), (1, 0))), ("conv0v", ((2, 16),))):
                    on(dve, part, h)
                    for back in (1, 2, 3):
                        if back > 1:
                            dve.wait_ge(done("taps"), h * 6 + (back - 1 if part == "conv0" else back + 2))
                        for i, tile in tiles:
                            src = ps[:, 1, i * T:(i + 1) * T] if i < 2 else ps[:, 2, 0:T]
                            tap = small[:, bass.ds(h + (R_CONV + (3 - back) * 24 + tile), 1)]
                            ins = dve.scalar_tensor_tensor(out=cv[:, i, back:T], in0=src[:, 0:T - back], scalar=tap,
                                                           in1=cv[:, i, back:T], op0=ALU.mult, op1=ALU.add)
                        ins.then_inc(done("taps"), 1)
                dve.wait_ge(done("taps"), h * 6 + 6)
                dve.sem_inc(done("conv3"), 1)

            def head(h, last=False):
                b0, b1 = (small[:, bass.ds(h + (136 + 8 * c), 1)] for c in range(NC))
                both = lambda a: a.rearrange("p (i t) -> p i t", i=2)
                on(dve, "att_gain", h)
                dve.tensor_tensor(both(qk), both(qg), cos[:, None, :].to_broadcast([P, 2, T]), ALU.mult).then_inc(done("rope_cos"), 1)
                on(dve, "att_rot", h)
                dve.tensor_tensor(both(rp2), both(ps[:, 4, :]), sin[:, None, :].to_broadcast([P, 2, T]), ALU.mult).then_inc(done("rope_sin"), 1)
                on(dve, "rope_sin", h)
                dve.tensor_tensor(qk, qk, rp2, ALU.add).then_inc(done("rope_sum"), 1)
                on(dve, "att_std", h)
                dve.reciprocal(rp1, rp1).then_inc(done("att_rstd"), 1)
                on(dve, "att_rstd", h)
                dve.tensor_tensor(qk, qk, rp1, ALU.mult).then_inc(done("att_qk"), 1)
                on(dve, "dn_std", h)
                dve.reciprocal(kq, kq).then_inc(done("dn_rstd"), 1)
                on(dve, "dn_rstd", h)
                dve.tensor_tensor(kq, kq, sl[:, 0:2, :].rearrange("p i t -> p (i t)"), ALU.mult).then_inc(done("dn_kq"), 1)
                on(dve, "decay_masked", h)
                on(dve, "kq_dots0", h)
                dve.scalar_tensor_tensor(out=LT[:, 0:T], in0=ps[:, 4, 0:T], scalar=b0, in1=Dm[:, 0:T], op0=ALU.mult, op1=ALU.mult)
                on(dve, "kq_dots1", h)
                dve.scalar_tensor_tensor(out=LT[:, T:384], in0=ps[:, 5, 0:P], scalar=b1, in1=Dm[:, T:384],
                                         op0=ALU.mult, op1=ALU.mult).then_inc(done("LT_ready"), 1)
                on(dve, "scores", h)
                dve.tensor_tensor(sm, ps[:, 6, 0:384], mask, ALU.add).then_inc(done("masked"), 1)
                on(dve, "masked", h)
                dve.tensor_reduce(mx[:, 0:1], sm[:, 0:P], AX.X, ALU.max)
                dve.tensor_reduce(mx[:, 1:2], sm[:, P:384], AX.X, ALU.max).then_inc(done("maxes"), 1)
                dve.scalar_tensor_tensor(out=AT[:, 0:T], in0=ps[:, 4, T:HT], scalar=float(HD) ** -0.5, in1=Dm[:, 0:T],
                                         op0=ALU.mult, op1=ALU.mult)
                dve.scalar_tensor_tensor(out=AT[:, T:384], in0=ps[:, 5, P:T], scalar=float(HD) ** -0.5, in1=Dm[:, T:384],
                                         op0=ALU.mult, op1=ALU.mult).then_inc(done("AT_ready"), 1)
                on(dve, "maxes", h)
                dve.tensor_scalar(mx[:, 2:4], mx[:, 0:2], -float(HD) ** -0.5, None, ALU.mult).then_inc(done("negmax"), 1)
                two = lambda a: a.rearrange("p (c j) -> p c j", c=NC)
                idb = ident[:, None, :].to_broadcast([P, NC, P])
                on(dve, "B_first", h)
                dve.tensor_tensor(two(XT), idb, two(BT[:, 0, :]), ALU.subtract)
                on(dve, "lvlZ", h * LEVELS)
                dve.tensor_tensor(two(X), idb, two(ps[:, 3, 0:T]), ALU.subtract).then_inc(done("lvlX"), 1)
                for s in range(1, LEVELS):
                    on(dve, "lvlY", h * (LEVELS - 1) + (s - 1))
                    dve.tensor_copy(Y, ps[:, 4, 0:T]).then_inc(done("lvlYc"), 1)
                    if s == 1:
                        on(dve, "probs", h)
                        dve.reciprocal(mx[:, 6:8], mx[:, 4:6]).then_inc(done("psums"), 1)
                        on(dve, "psums", h)
                        dve.tensor_scalar(pr[:, 0:P], pr[:, 0:P], mx[:, 6:7], None, ALU.mult)
                        dve.tensor_scalar(pr[:, P:384], pr[:, P:384], mx[:, 7:8], None, ALU.mult).then_inc(done("pnorm"), 1)
                    on(dve, "lvlZ", h * LEVELS + s)
                    if s < LEVELS - 1:
                        dve.tensor_tensor(X, X, ps[:, 3, 0:T], ALU.subtract)
                    dve.tensor_tensor(XT, XT, ps[:, 3, T:HT], ALU.subtract).then_inc(done("lvlX"), 1)
                on(dve, "sol0", h)
                dve.tensor_copy(vp[:, 0:P], ps[:, 4, 0:P]).then_inc(done("vp0"), 1)
                on(dve, "cross", h)
                dve.tensor_tensor(w1, dv[:, P:T], ps[:, 3, 0:P], ALU.subtract).then_inc(done("w1_ready"), 1)
                dve.tensor_scalar(vn[:, 0:P], vp[:, 0:P], b0, None, ALU.mult)
                on(dve, "sol1", h)
                dve.tensor_scalar(vn[:, P:T], ps[:, 4, 0:P], b1, None, ALU.mult).then_inc(done("vn_ready"), 1)
                if not last:
                    convolve(h + 1)

            convolve(0)
            with dve.Fori(0, HEADS - 1) as h:
                head(h)
            head(HEADS - 1, True)

            with dve.Fori(HEADS, HEADS + MEM_HEADS) as it:
                two = lambda a: a.rearrange("p (i t) -> p i t", i=2)
                heads = branch[:, bass.ds((it - HEADS) * 2 + 8, 2), :]
                on(dve, "att_std", it)
                dve.reciprocal(mstd, mstd).then_inc(done("att_rstd"), 1)
                on(dve, "att_rstd", it)
                on(dve, "att_gain", it)
                dve.tensor_tensor(mqk4, mqk4, two(mstd)[:, :, None, :].to_broadcast([P, 2, 2, T]), ALU.mult).then_inc(done("att_qk"), 1)
                on(dve, "dn_std", it)
                dve.reciprocal(dstd, dstd).then_inc(done("dn_rstd"), 1)
                on(dve, "dn_rstd", it)
                on(dve, "z_silu", it - HEADS)
                dve.scalar_tensor_tensor(out=dstd, in0=dstd, scalar=cols[:, R_DN:R_DN + 1], in1=zs, op0=ALU.mult,
                                         op1=ALU.mult).then_inc(done("dn_kq"), 1)
                on(dve, "dn_kq", it)
                dve.tensor_tensor(heads, heads, two(dstd), ALU.mult).then_inc(done("dn_scaled"), 1)
                on(dve, "scores", it)
                dve.tensor_reduce(mx[:, 0:2], two(ps[:, 4, :]), AX.X, ALU.max).then_inc(done("maxes"), 1)
                on(dve, "maxes", it)
                dve.tensor_scalar(mx[:, 2:4], mx[:, 0:2], -float(2 * HD) ** -0.5, None, ALU.mult).then_inc(done("negmax"), 1)
                on(dve, "probs", it)
                dve.reciprocal(mx[:, 6:8], mx[:, 4:6]).then_inc(done("psums"), 1)
                on(dve, "psums", it)
                dve.tensor_tensor(two(mpr), two(mpr), mx[:, 6:8, None].to_broadcast([P, 2, T]), ALU.mult).then_inc(done("pnorm"), 1)
            dve.wait_ge(done("sig"), 3)
            g4 = gates.rearrange("p (n m) t -> p n m t", n=3)
            with dve.Fori(0, KT // 2) as mp:
                for j in range(2):
                    m = mp * 2 + j
                    on(dve, f"tile{3 * j + 2}", mp + (HEADS + MEM_HEADS))
                    dve.tensor_tensor(prod, ps[:, 3 * j:3 * j + 3, 0:T], g4[:, :, bass.ds(m, 1), :].rearrange("p n o t -> p n (o t)"),
                                      ALU.mult).then_inc(done("br_prod"), 1)
                    on(dve, "br_prod", m)
                    dve.tensor_tensor(mixs, prod[:, 0, :], prod[:, 1, :], ALU.add).then_inc(done("br_sum"), 1)
                    on(dve, "br_sum", m)
                    dve.tensor_tensor(mixT[:, bass.ds(m, 1), :], mixs[:, None, :], prod[:, 2:3, :], ALU.add).then_inc(done("br_mix"), 1)
                    on(dve, "br_mix", m)
            def route_dve(n, c):
                step = [0]

                def link(ins):
                    ins.then_inc(r_step, 1)
                    step[0] += 1
                    dve.wait_ge(r_step, n * RSTEPS + step[0])
                    dve.sem_inc(t_route, 1)

                def best(values, where_, rows_, scratch):
                    link([dve.max(v[:, 0:8], a) for v, a in zip(values, rows_)][-1])
                    for v, i, a, b in zip(values, where_, rows_, scratch):
                        dve.max_index(i[:, 0:8], v[:, 0:8], a)
                        ins = dve.match_replace(b, v[:, 0:8], a, -3.0e38)
                    link(ins)
                    link([dve.max(v[:, 8:16], b) for v, b in zip(values, scratch)][-1])
                    link([dve.max_index(i[:, 8:16], v[:, 8:16], b) for v, i, b in zip(values, where_, scratch)][-1])

                on(dve, "p_sk", n)
                dve.sem_inc(t_route, 1)
                best([rv[:, r, :] for r in range(2)], [ri[:, r, :] for r in range(2)],
                     [sc0[:, r, :] for r in range(2)], [sc1[:, r, :] for r in range(2)])
                dve.tensor_copy(rf, ri)
                link(dve.tensor_tensor(cd0.rearrange("p (a b) -> p a b", a=TOPK), rv[:, 0, :, None].to_broadcast([P, TOPK, TOPK]),
                                       rv[:, 1, None, :].to_broadcast([P, TOPK, TOPK]), ALU.add))
                best([sv], [ci], [cd0], [cd1])
                dve.tensor_scalar(neg[:, 0:1], sv[:, 0:1], -1.0, None, ALU.mult).then_inc(done("negs"), 1)
                dve.tensor_scalar(ab[:, 0, :], ci, 4, None, ALU.logical_shift_right)
                link(dve.tensor_scalar(ab[:, 1, :], ci, 15, None, ALU.bitwise_and))
                h3 = hot.rearrange("p (r a) -> p r a", a=TOPK)
                link(dve.tensor_tensor(h3, ab.rearrange("p i k -> p (i k)")[:, :, None].to_broadcast([P, 2 * TOPK, TOPK]),
                                       iota[:, None, :].to_broadcast([P, 2 * TOPK, TOPK]), ALU.is_equal))
                h4 = hot.rearrange("p (r k a) -> p r k a", r=2, k=TOPK)
                link(dve.tensor_tensor(h4, h4, rf[:, :, None, :].to_broadcast([P, 2, TOPK, TOPK]), ALU.mult))
                link(dve.tensor_reduce(ef.rearrange("p i k -> p (i k)"), h3, AX.X, ALU.add))
                dve.scalar_tensor_tensor(out=idx_u[c], in0=ef[:, 0, :], scalar=float(NKEY), in1=ef[:, 1, :],
                                         op0=ALU.mult, op1=ALU.add).then_inc(done("idx_ready"), 1)
                assert step[0] == RSTEPS

            def keep_idx(n, c):
                dve.wait_ge(done("idx_ready"), n + 1)
                dve.sem_inc(t_route, 1)
                dve.wait_ge(done("vrow"), RING if isinstance(n, int) and n < 2 else (n - 1) * TOPK + RING)
                dve.tensor_copy(idx_v[c], idx_u[c]).then_inc(done("idx_kept"), 1)

            def weigh(n, c):
                on(dve, "exps", n)
                dve.reciprocal(rsum[:, 0:1], sums[:, 0:1]).then_inc(done("weighed"), 1)
                dve.wait_ge(done("weighed"), n * 2 + 1)
                dve.tensor_scalar(wts2[c], ex, rsum[:, 0:1], None, ALU.mult).then_inc(done("weighed"), 1)

            def dots(n, c, rows_):
                for k in rows_:
                    if k % 2 == 0:
                        dve.wait_ge(s_u[k % RING // 2], (n * 2 + (k // RING + 1)) * 32)
                    row = ring[:, k % RING, :]
                    dve.tensor_tensor_reduce(out=row, in0=row, in1=h2[:, c, :], scale=1.0, scalar=0.0,
                                             op0=ALU.mult, op1=ALU.add, accum_out=acts[c][:, k:k + 1]).then_inc(done("dot"), 1)

            def dots_done(n):
                dve.wait_ge(done("dot"), n * TOPK + (TOPK + RING))
                dve.sem_inc(done("acts"), 1)

            def coefficients(n, c):
                dve.wait_ge(done("weighed"), n * 2 + 2)
                on(dve, "gelu", n)
                dve.tensor_tensor(coef2[c], gelu, wts2[c], ALU.mult).then_inc(done("coef"), 1)

            def phase_dve(n, c, route=True):
                dots(n + 1, 1 - c, range(0, EARLY))
                if route:
                    route_dve(n + 2, c)
                keep_idx(n + 1, 1 - c)
                dots(n + 1, 1 - c, range(EARLY, TOPK))
                dots_done(n + 1)
                if route:
                    weigh(n + 2, c)
                coefficients(n + 1, 1 - c)

            def norm_dve(c):
                for n in range(2):
                    b = 2 * c + n
                    dve.wait_ge(done("gdots"), b + 1)
                    dve.tensor_tensor(x1[:, c, n * 512:(n + 1) * 512], x1[:, c, n * 512:(n + 1) * 512], ps[:, b, :],
                                      ALU.add).then_inc(done("x1_ready"), 1)
                dve.wait_ge(done("x1_done"), c + 1)
                dve.tensor_scalar(std2[:, c:c + 1], sq2[:, c:c + 1], 1.0 / D, EPS, ALU.mult, ALU.add).then_inc(t_h2[c], 1)
                dve.wait_ge(t_h2[c], 2)
                dve.reciprocal(rstd2[:, c:c + 1], std2[:, c:c + 1]).then_inc(t_h2[c], 1)
                dve.wait_ge(t_h2[c], 3)
                dve.scalar_tensor_tensor(out=h2[:, c, :], in0=x1[:, c, :], scalar=rstd2[:, c:c + 1], in1=gfull[:, :],
                                         op0=ALU.mult, op1=ALU.mult).then_inc(t_h2[c], 1)
                for half in range(2):
                    dve.wait_ge(t_tr, 1 + 2 * c + half)
                    dve.tensor_copy(h2T[:, 4 * half:4 * half + 4, c * P:(c + 1) * P],
                                    ps[:, 2 * c + half, :].rearrange("p (k t) -> p k t", k=4)).then_inc(t_h2[c], 1)

            dve.wait_ge(s_x1, 16 * (NC + 1))
            norm_dve(0)
            route_dve(0, 0)
            keep_idx(0, 0)
            norm_dve(1)
            weigh(0, 0)
            route_dve(1, 1)
            dots(0, 0, range(TOPK))
            dots_done(0)
            weigh(1, 1)
            coefficients(0, 0)
            with dve.Fori(0, PHEADS - 1) as h:
                phase_dve(h * NC, 0)
                phase_dve(h * NC + 1, 1)
            phase_dve(UNITS - 2, 0, False)
            dve.wait_ge(done("vmm_end"), 1)
            for c in range(NC):
                dve.tensor_tensor(x1[:, c, :], x1[:, c, :], ps[:, 2 * c:2 * c + 2, :].rearrange("p b n -> p (b n)"),
                                  ALU.add).then_inc(p_end, 1)

        @block.tensor
        def _(pe):
            def done(name):
                return names[name].sem

            pe.wait_ge(s_cst, 16)
            pe.wait_ge(s_rows, 16 * len(rows))
            pe.transpose(ps[:, 7, 0:NROWS], rows_sb[0:NROWS, :], ident[0:NROWS, 0:NROWS]).then_inc(p_cols, 1)
            pe.wait_ge(s_keys, 32)
            for i in range(2):
                ins = pe.transpose(ps[:, 6, i * P:(i + 1) * P], keys_in[:, i, :], ident)
            ins.then_inc(p_keys, 1)
            for b in range(8):
                s, half = b // 2, b % 2
                pe.wait_ge(d_xn, s + 1)
                if b == 7:
                    pe.wait_ge(d_cols, 1)
                if b == 6:
                    pe.wait_ge(d_keys, 1)
                for k in range(4):
                    at = (4 * half + k) * P
                    ins = pe.transpose(ps[:, b, k * P:(k + 1) * P], xin[:, s, at:at + P], ident)
                ins.then_inc(p_tr, 1)
            pe.wait_ge(d_hT, 4)
            pe.wait_ge(s_ba, 16)
            for c in range(NC):
                for k in range(KT):
                    ins = pe.matmul(ps[:, 0, 16 * c:16 * c + 16], hT[:, k, c * P:(c + 1) * P], wba_t[:, k, :],
                                    start=(k == 0), stop=(k == KT - 1))
            ins.then_inc(p_ba, 1)
            pe.wait_ge(d_hT, 8)
            pe.sem_inc(done("br_prod"), 2)
            pe.wait_ge(s_gate, 5)

            def whole(steps):
                for _ in steps:
                    pass


            def tile(it, i, dst, rhs):
                pe.wait_ge(s_w[i], (it + 1) * 16)
                for k in range(KT):
                    ins = pe.matmul(dst, wslot[i][:, k, :], rhs[:, k, :], start=(k == 0), stop=(k == KT - 1))
                    if k == KT - 1:
                        ins.then_inc(done(f"tile{i}"), 1)
                    yield

            def by_token(it, i, dst, lhs):
                pe.wait_ge(s_w[i], (it + 1) * 16)
                for c in range(NC):
                    for k in range(KT):
                        ins = pe.matmul(dst(c), lhs[:, k, c * P:(c + 1) * P], wslot[i][:, k, :], start=(k == 0), stop=(k == KT - 1))
                        if c == NC - 1 and k == KT - 1:
                            ins.then_inc(done(f"tile{i}"), 1)
                        if k % 2:
                            yield

            def tiles(h):
                yield from tile(h, 0, ps[:, 0, 0:T], hT)
                yield from tile(h, 1, ps[:, 0, T:HT], hT)
                yield from tile(h, 2, ps[:, 1, 0:T], hT)
                yield from tile(h, 3, ps[:, 1, T:HT], hT)
                on_before(pe, "gate1", h)
                yield from tile(h, 4, ps[:, 2, 0:T], hT)
                yield from by_token(h, 5, lambda c: ps[:, 2, T + c * P:T + (c + 1) * P], hT)

            def mem_tiles(it):
                yield from tile(it, 0, ps[:, 0, 0:T], hT)
                yield from tile(it, 1, ps[:, 0, T:HT], hT)
                yield from tile(it, 2, ps[:, 1, 0:T], memhT)
                yield from tile(it, 3, ps[:, 1, T:HT], memhT)
                on_before(pe, "gate1", HEADS)
                for i in range(2):
                    yield from by_token(it, 4 + i, lambda c, i=i: ps[:, 2, c * T + i * P:c * T + (i + 1) * P], memhT)

            def gate_tiles(h):
                on_before(pe, "z_kept", h)
                on_before(pe, "gate0", h)
                yield from tile(h, 6, ps[:, 7, 0:T], hT)
                yield from tile(h, 7, ps[:, 7, T:HT], hT)
                yield from tile(h, 8, ps[:, 2, 0:T], hT)

            def mem_gate_tiles(it):
                on_before(pe, "gate0", it)
                yield from tile(it, 6, ps[:, 7, 0:T], hT)
                yield from tile(it, 7, ps[:, 7, T:HT], hT)

            def filling(*parts):
                def chained():
                    for part in parts:
                        yield from part
                rest = chained()

                def fill(n):
                    for _ in range(n):
                        next(rest, None)
                return fill

            def head(h, following):
                fill = filling(gate_tiles(h), following)
                on(pe, "att_sq", h)
                pe.matmul(ps[:, 3, :], ones, sqm, start=True, stop=True).then_inc(done("att_ss"), 1)
                on_before(pe, "dn_kept", h)
                on(pe, "att_gain", h)
                pe.matmul(ps[:, 4, :], swap, qg, start=True, stop=True).then_inc(done("att_rot"), 1)
                on(pe, "Gm_ready", h)
                pe.matmul(ps[:, 5, 0:T], after, Gm[:, 0:T], start=True, stop=False, skip_group_check=True)
                pe.matmul(ps[:, 5, P:T], ones, Gm[:, T:384], start=False, stop=True, skip_group_check=True)
                pe.matmul(ps[:, 5, T:384], after, Gm[:, T:384], start=True, stop=True, skip_group_check=True).then_inc(done("gdiff"), 1)
                fill(FILLS[0])
                on(pe, "dn_sq", h)
                on(pe, "att_std", h)
                pe.matmul(ps[:, 3, :], ones, sqd, start=True, stop=True).then_inc(done("dn_ss"), 1)
                fill(FILLS[1])
                on(pe, "att_qk", h)
                on_before(pe, "att_kept", h)
                pe.matmul(ps[:, 6, 0:P], qk[:, 0:P], qk[:, T:T + P], start=True, stop=True)
                pe.matmul(ps[:, 6, P:384], qk[:, P:T], qk[:, T:HT], start=True, stop=True).then_inc(done("scores"), 1)
                on(pe, "silu", h)
                on(pe, "decay", h)
                for c in range(NC):
                    ins = pe.transpose(ps[:, 5, c * P:(c + 1) * P], sl[:, 2, c * P:(c + 1) * P], ident)
                ins.then_inc(done("dv_turned"), 1)
                fill(FILLS[2])
                on(pe, "dn_kq", h)
                pe.matmul(ps[:, 4, :], kq[:, 0:P], kq, start=True, stop=True).then_inc(done("kq_dots0"), 1)
                on(pe, "dv_kept", h)
                pe.matmul(ps[:, 5, 0:T].rearrange("p (i j) -> p i j", i=2), kq[:, P:T],
                          kq.rearrange("p (i t) -> p i t", i=2)[:, :, P:T], start=True, stop=True).then_inc(done("kq_dots1"), 1)
                fill(FILLS[3])
                on(pe, "B_first", h)
                for c in range(NC):
                    ins = pe.transpose(ps[:, 3, c * P:(c + 1) * P], BT[:, 0, c * P:(c + 1) * P], ident)
                ins.then_inc(done("lvlZ"), 1)
                fill(FILLS[4])
                on(pe, "BT_ready", h)
                on(pe, "AT_ready", h)
                for s in range(1, LEVELS):
                    on(pe, "lvlX", h * LEVELS + (s - 1))
                    for c in range(NC):
                        a, b = c * P, (c + 1) * P
                        ins = pe.matmul(ps[:, 4, a:b], BT[:, s, a:b], X[:, a:b], start=True, stop=True)
                    ins.then_inc(done("lvlY"), 1)
                    if s == 2:
                        on(pe, "pnorm", h)
                        pe.transpose(ps[:, 5, 0:P], pr[:, 0:P], ident)
                        pe.transpose(ps[:, 5, P:T], pr[:, P:T], ident)
                        pe.transpose(ps[:, 5, T:384], pr[:, T:384], ident).then_inc(done("p_turned"), 1)
                    if s == 4:
                        on(pe, "pT_ready", h)
                        pe.matmul(ps[:, 6, 0:T], vtok[:, 0:P], pT[:, 0:T], start=True, stop=False, skip_group_check=True)
                        pe.matmul(ps[:, 6, P:T], vtok[:, P:T], pT[:, T:384], start=False, stop=True,
                                  skip_group_check=True).then_inc(done("att_out"), 1)
                    fill(FILLS[5])
                    on(pe, "lvlYc", h * (LEVELS - 1) + (s - 1))
                    for c in range(NC):
                        a, b = c * P, (c + 1) * P
                        if s < LEVELS - 1:
                            pe.matmul(ps[:, 3, a:b], XT[:, a:b], Y[:, a:b], start=True, stop=True)
                        ins = pe.matmul(ps[:, 3, T + a:T + b], Y[:, a:b], XT[:, a:b], start=True, stop=True)
                    ins.then_inc(done("lvlZ"), 1)
                    fill(FILLS[6])
                on(pe, "lvlX", h * LEVELS + (LEVELS - 1))
                pe.matmul(ps[:, 4, 0:P], XT[:, 0:P], dv[:, 0:P], start=True, stop=True).then_inc(done("sol0"), 1)
                fill(FILLS[7])
                on(pe, "vp0", h)
                pe.matmul(ps[:, 3, 0:P], LT[:, P:T], vp[:, 0:P], start=True, stop=True).then_inc(done("cross"), 1)
                fill(FILLS[7])
                on(pe, "w1_ready", h)
                pe.matmul(ps[:, 4, 0:P], XT[:, P:T], w1, start=True, stop=True).then_inc(done("sol1"), 1)
                fill(FILLS[7])
                on(pe, "vn_ready", h)
                pe.matmul(ps[:, 4, 0:T], vn[:, 0:P], AT[:, 0:T], start=True, stop=False, skip_group_check=True)
                pe.matmul(ps[:, 4, P:T], vn[:, P:T], AT[:, T:384], start=False, stop=True,
                          skip_group_check=True).then_inc(done("dn_out"), 1)
                fill(200)

            whole(tiles(0))
            with pe.Fori(0, HEADS - 1) as h:
                head(h, tiles(h + 1))
            head(HEADS - 1, mem_tiles(HEADS))

            def mem_head(it, following):
                fill = filling(mem_gate_tiles(it), following)
                on(pe, "att_sq", it)
                for a in range(2):
                    for i in range(2):
                        ins = pe.matmul(ps[:, 3, a * T:(a + 1) * T], ones, msq[:, (2 * a + i) * T:(2 * a + i + 1) * T],
                                        start=(i == 0), stop=(i == 1))
                ins.then_inc(done("att_ss"), 1)
                on(pe, "dn_sq", it)
                on_before(pe, "att_kept", it)
                pe.matmul(ps[:, 6, :], ones, sqd, start=True, stop=True).then_inc(done("dn_ss"), 1)
                fill(MFILLS[0])
                on(pe, "att_qk", it)
                on(pe, "att_gain", it)
                for c in range(NC):
                    for i in range(2):
                        ins = pe.matmul(ps[:, 4, c * T:(c + 1) * T], mqk4[:, 0, i, c * P:(c + 1) * P], mqk4[:, 1, i, :],
                                        start=(i == 0), stop=(i == 1))
                ins.then_inc(done("scores"), 1)
                fill(MFILLS[1])
                on(pe, "pnorm", it)
                for m in range(NC):
                    for c in range(NC):
                        ins = pe.transpose(ps[:, 5, m * T + c * P:m * T + (c + 1) * P], mpr[:, c * T + m * P:c * T + (m + 1) * P], ident)
                ins.then_inc(done("p_turned"), 1)
                fill(MFILLS[2])
                on(pe, "pT_ready", it)
                on(pe, "mv_kept", it - HEADS)
                on(pe, "dn_std", it)
                for i in range(2):
                    for m in range(NC):
                        ins = pe.matmul(ps[:, 6, i * T:(i + 1) * T], mv[:, m * T + i * P:m * T + (i + 1) * P],
                                        mpT[:, m * T:(m + 1) * T], start=(m == 0), stop=(m == NC - 1))
                ins.then_inc(done("att_out"), 1)
                fill(200)

            with pe.Fori(HEADS, HEADS + MEM_HEADS - 1) as it:
                mem_head(it, mem_tiles(it + 1))
            mem_head(HEADS + MEM_HEADS - 1, ())

            pe.wait_ge(done("att_kept"), 1 + HEADS + MEM_HEADS)
            pe.wait_ge(done("dn_scaled"), MEM_HEADS)
            with pe.Fori(0, KT // 2) as mp:
                for j in range(2):
                    m = mp * 2 + j
                    pe.wait_ge(done("br_prod"), m + 1)
                    for n in range(3):
                        i = 3 * j + n
                        pe.wait_ge(s_w[i], (mp + (HEADS + MEM_HEADS + 1)) * 16)
                        for k in range(KT):
                            ins = pe.matmul(ps[:, i, 0:T], wslot[i][:, k, :], branch[:, 8 * n + k, :], start=(k == 0), stop=(k == KT - 1))
                        ins.then_inc(done(f"tile{i}"), 1)
            pe.wait_ge(done("br_mix"), KT)
            pe.wait_ge(s_wo, 32)
            for c in range(NC):
                for n in range(2):
                    for k in range(KT):
                        w = wring[:, (6 + k) * D:(7 + k) * D] if k < 3 else wo_late[:, k - 3, :]
                        ins = pe.matmul(ps[:, 2 * c + n, :], mixT[:, k, c * P:(c + 1) * P], w[:, n * 512:(n + 1) * 512],
                                        start=(k == 0), stop=(k == KT - 1))
                    ins.then_inc(done("gdots"), 1)
            def turn_h2(c):
                pe.wait_ge(t_h2[c], 4)
                for half in range(2):
                    for k in range(4):
                        at = (4 * half + k) * P
                        ins = pe.transpose(ps[:, 2 * c + half, k * P:(k + 1) * P], h2[:, c, at:at + P], ident)
                    ins.then_inc(t_tr, 1)

            def route_pe(n, h, c):
                for k in range(KT):
                    ins = pe.matmul(ps[:, 4, 0:QW], h2T[:, k, c * P:(c + 1) * P], wq[:, k, bass.ds(h * QW, QW)], start=(k == 0), stop=(k == KT - 1))
                ins.then_inc(done("p_q"), 1)
                on(pe, "p_qk", n)
                for i in range(2):
                    ins = pe.transpose(ps[:, 5, i * P:(i + 1) * P], qtok[:, i * P:(i + 1) * P], ident)
                ins.then_inc(done("p_t"), 1)
                on(pe, "p_tk", n)
                for i in range(2):
                    ins = pe.matmul(ps[:, 6, i * NKEY:(i + 1) * NKEY], qT[:, i * P:(i + 1) * P], keysT[:, i * P:(i + 1) * P], start=True, stop=True)
                ins.then_inc(done("p_s"), 1)

            def rows_pe(n, c, last=False):
                for k in range(TOPK):
                    if k % 2 == 0:
                        pe.wait_ge(s_v[k % RING // 2], (n * 2 + (k // RING + 1)) * 32)
                    on(pe, "diag", n * TOPK + k)
                    for half in range(2):
                        ins = pe.matmul(ps[:, 2 * c + half, :], diag[:, k % 8, :], ring[:, RING + k % RING, half * 512:(half + 1) * 512],
                                        start=False, stop=last and k == TOPK - 1, skip_group_check=True)
                    ins.then_inc(done("vrow"), 1)

            def open_sums(c):
                pe.wait_ge(t_h2[c], 6)
                for half in range(2):
                    pe.matmul(ps[:, 2 * c + half, :], mask[:, P:T], h2[:, c, 0:512], start=True, stop=False, skip_group_check=True)

            turn_h2(0)
            pe.wait_ge(s_wq, 16 * (KT // 2))
            pe.wait_ge(t_h2[0], 6)
            route_pe(0, 0, 0)
            pe.sem_inc(done("vrow"), RING)
            turn_h2(1)
            open_sums(0)
            open_sums(1)
            route_pe(1, 0, 1)
            with pe.Fori(0, PHEADS - 1) as h:
                route_pe(h * NC + 2, h + 1, 0)
                rows_pe(h * NC, 0)
                route_pe(h * NC + 3, h + 1, 1)
                rows_pe(h * NC + 1, 1)
            rows_pe(UNITS - 2, 0, True)
            rows_pe(UNITS - 1, 1, True)
            pe.wait_ge(done("vrow"), RING + UNITS * TOPK)
            pe.sem_inc(done("vmm_end"), 1)


_INS = ["x", "mem", "attn_norm_g", "mem_norm_g", "ffn_norm_g", "w_in", "moba_q_norm_g", "moba_k_norm_g", "dn_conv_w",
        "dn_a_log", "dn_dt_bias", "dn_out_norm_g", "w_mem_kv", "mem_q_norm_g", "mem_k_norm_g", "w_branch", "w_out",
        "peer_w_q", "peer_keys1", "peer_keys2", "peer_u", "peer_v"]


def kernel(**inputs):
    import concourse.bacc as bacc
    from concourse.bass_utils import run_bass_kernel_spmd

    nc = bacc.Bacc("TRN2", target_bir_lowering=False, num_devices=1)
    table, where = constants()
    arrays = {"constants_dram": table}
    d = {}
    for name in _INS:
        a = np.ascontiguousarray(inputs[name])
        arrays[f"in_{name}_dram"] = a
        d[name] = nc.dram_tensor(f"in_{name}_dram", a.shape, mybir.dt.from_np(a.dtype), kind="ExternalInput").ap()
    cst = nc.dram_tensor("constants_dram", table.shape, F32, kind="ExternalInput").ap()
    out = nc.dram_tensor("out_dram", (1, T, D), F32, kind="ExternalOutput").ap()

    def as_rows(name):
        return d[name].rearrange("o (r c) -> (o r) c", c=P)

    rows = [(R_CONV, d["dn_conv_w"].rearrange("o j (r c) -> (o j r) c", c=P)), (R_ATTN, as_rows("attn_norm_g")),
            (R_MEM, as_rows("mem_norm_g")), (R_MQ, as_rows("moba_q_norm_g")), (R_MK, as_rows("moba_k_norm_g")),
            (R_DN, as_rows("dn_out_norm_g")), (R_CQ, as_rows("mem_q_norm_g")), (R_CK, as_rows("mem_k_norm_g"))]
    hybrid_layer(nc, cst, where, d["x"][0], d["mem"][0], rows, d["w_in"][0], d["dn_a_log"][0], d["dn_dt_bias"][0],
                 d["ffn_norm_g"][0], d["w_mem_kv"][0], d["w_branch"][0], d["w_out"][0], d["peer_w_q"][0],
                 d["peer_keys1"][0], d["peer_keys2"][0], d["peer_u"][0], d["peer_v"][0], out[0])
    r = run_bass_kernel_spmd(nc, [arrays], core_ids=[0])
    return r.results[0]["out_dram"]
```

```python
from contextlib import ExitStack

import numpy as np

import concourse.bass as bass
from concourse import mybir

F32 = mybir.dt.float32
F32R = mybir.dt.float32r
U32 = mybir.dt.uint32
ALU = mybir.AluOpType
ACT = mybir.ActivationFunctionType
AX = mybir.AxisListType

P = 128
T = 256
NC = T // P
D = 1024
KT = D // P
HEADS = 8
HD = 128
MEM_HEADS = 4
EPS = 1e-6
LEVELS = 7

C_MQ, C_MK, C_MV = 0, 1024, 2048
C_DQ, C_DK, C_DV = 3072, 4096, 5120
C_BA = 6144
C_Z = 6160
C_CQ = 7184
C_G = 8208
IN_W = 11280

NEXP = 16384
NKEY = 128
TOPK = 16
PHEADS = 8
UNITS = PHEADS * NC
RING = 8
SLOTS = 3
QW = 2 * NKEY

R_CONV = 0
R_ATTN = 96
R_MEM = 104
R_MQ, R_MK, R_DN = 112, 113, 114
R_CQ, R_CK = 115, 117
NROWS = 119

NEG = -1.0e30


def constants():
    i = np.arange(P)
    ident = np.eye(P, dtype=np.float32)
    after = (i[:, None] > i[None, :]).astype(np.float32)
    upto = (i[:, None] <= i[None, :]).astype(np.float32)
    ones = np.ones((P, P), np.float32)
    causal = np.where(i[None, :] <= i[:, None], 0.0, NEG).astype(np.float32)
    zeros = np.zeros((P, P), np.float32)
    swap = np.zeros((P, P), np.float32)
    half = HD // 2
    for d in range(half):
        swap[d + half, d] = -1.0
        swap[d, d + half] = 1.0
    inv = (1.0 / (np.float32(10000.0) ** (np.arange(0, HD, 2, dtype=np.float32) / np.float32(HD)))).astype(np.float32)
    ang = (np.arange(T, dtype=np.float32)[:, None] * inv[None, :]).astype(np.float32)
    cos = np.cos(ang.astype(np.float64)).astype(np.float32).T
    sin = np.sin(ang.astype(np.float64)).astype(np.float32).T
    cos, sin = np.concatenate([cos, cos]), np.concatenate([sin, sin])
    levels = []
    for n in range(LEVELS):
        s = 1 << n
        same = i[:, None] // (2 * s) == i[None, :] // (2 * s)
        low = (i[None, :] % (2 * s) >= s) & (i[:, None] % (2 * s) < s)
        levels.append((same & low).astype(np.float32))
    eps = np.full((P, 1), EPS, np.float32)
    iota = np.tile(np.arange(TOPK, dtype=np.float32), (P, 1))
    parts = {
        "ident": ident, "after": after, "ones": ones, "swap": swap,
        "upto": np.concatenate([upto, ones, upto], 1),
        "mask": np.concatenate([causal, zeros, causal], 1),
        "cos": cos, "sin": sin, "levels": np.concatenate(levels, 1), "eps": eps, "iota": iota,
    }
    at, where = 0, {}
    for k, v in parts.items():
        where[k] = (at, v.shape[1])
        at += v.shape[1]
    return np.ascontiguousarray(np.concatenate(list(parts.values()), 1), dtype=np.float32), where


class Event:

    def __init__(self, sem, primed=0):
        self.sem, self.primed = sem, primed

    def now(self, it):
        return it + (1 + self.primed)

    def before(self, it):
        assert self.primed
        return it + 1


def hybrid_layer(nc, cst_d, where, x_d, mem_d, rows, w_in, a_log, dt_bias, ffn_g, w_kv, w_branch, w_out,
                 w_q, keys1, keys2, peer_u, peer_v, out_d):
    with ExitStack() as ctx:
        def sb(name, shape, dt=F32):
            return ctx.enter_context(nc.sbuf_tensor(name, shape, dt))

        def sem(name):
            return ctx.enter_context(nc.semaphore(name))

        ARENA = 46592
        AT_RAW, AT_SCRATCH, AT_SPLIT = 14336, 17408, 31232
        front = sb("front", [P, AT_SCRATCH])
        with nc.sbuf_tensor("branch_split", [P, 2 * 3 * KT * T], F32R) as branch_split:
            pass
        scratch = sb("scratch", [P, AT_SPLIT - AT_SCRATCH])
        with nc.sbuf_tensor("split", [P, 4 * KT * T + SLOTS * 2 * D], F32R) as split:
            pass
        top = sb("top", [P, ARENA - AT_SPLIT])

        def words(a, n):
            for first, part in ((AT_SPLIT, top), (AT_SCRATCH, scratch), (0, front)):
                if a >= first:
                    assert a + n <= first + part.shape[1]
                    return part[:, a - first:a - first + n]

        cst = sb("cst", [P, cst_d.shape[1]])
        small = sb("small", [P, 512])
        ps = ctx.enter_context(nc.psum_tensor("ps", [P, 8, 512], F32))

        def const(name):
            a, n = where[name]
            return cst[:, a:a + n]

        ident, after, ones, swap = const("ident"), const("after"), const("ones"), const("swap")
        upto, mask, cos, sin = const("upto"), const("mask"), const("cos"), const("sin")
        levels = const("levels").rearrange("p (s j) -> p s j", s=LEVELS)
        eps, iota = const("eps"), const("iota")

        taken = [0]

        def carve(n):
            a = taken[0]
            taken[0] += n
            assert taken[0] <= ARENA, taken[0]
            return words(a, n)

        gates = carve(3 * KT * T).rearrange("p (k t) -> p k t", t=T)
        branch = carve(3 * KT * T).rearrange("p (k t) -> p k t", t=T)
        zT = carve(KT * T).rearrange("p (k t) -> p k t", t=T)
        assert taken[0] == AT_RAW
        raw = [carve(D).rearrange("p (k j) -> p k j", k=KT) for _ in range(SLOTS)]
        stage0 = taken[0]
        assert stage0 == AT_SCRATCH
        hT, memhT = (split[:, i * 2 * KT * T:(i + 1) * 2 * KT * T].rearrange("p (f k t) -> p f k t", f=2, k=KT) for i in range(2))
        halves = [split[:, 4 * KT * T + i * 2 * D:4 * KT * T + (i + 1) * 2 * D].rearrange("p (f k j) -> p f k j", f=2, k=KT)
                  for i in range(SLOTS)]
        branch2 = branch_split[:, :].rearrange("p (f k t) -> p f k t", f=2, k=3 * KT)

        cols = small[:, 0:NROWS]
        gtok = small[:, 120:136].rearrange("p (c h) -> p c h", c=NC)
        btok = small[:, 136:152].rearrange("p (c h) -> p c h", c=NC)
        ss4 = small[:, 152:156]
        rstd4 = small[:, 156:160]
        var4 = small[:, 160:164]
        arow = small[:, 164:172]
        dtrow = small[:, 172:180]
        ya = small[:, 212:228].rearrange("p (c n) -> p c n", c=NC)
        yb = small[:, 228:244].rearrange("p (c n) -> p c n", c=NC)
        yc = small[:, 244:260].rearrange("p (c n) -> p c n", c=NC)
        keysT = sb("keysT", [P, 2 * P])
        sq2, std2, rstd2 = small[:, 260:262], small[:, 262:264], small[:, 264:266]
        wba_t = sb("wba", [P, KT, 16])

        xin = carve(2 * NC * D).rearrange("p (s n) -> p s n", s=2 * NC)
        junk = carve(D)
        rows_sb = carve(P)
        keys_in = carve(2 * P).rearrange("p (i d) -> p i d", i=2)
        hraw, memraw = (carve(KT * T).rearrange("p (k t) -> p k t", t=T) for _ in range(2))
        assert taken[0] <= AT_SPLIT
        taken[0] = stage0

        s_cst, s_rows, s_x, s_mem, s_ba, s_rowb = (sem(n) for n in ("s_cst", "s_rows", "s_x", "s_mem", "s_ba", "s_rowb"))
        a_sq, d_var, a_std, d_rstd, d_xn = (sem(n) for n in ("a_sq", "d_var", "a_std", "d_rstd", "d_xn"))
        p_keys, d_keys = sem("p_keys"), sem("d_keys")
        p_cols, d_cols, p_tr, d_hT, p_ba, s_gate = (sem(n) for n in ("p_cols", "d_cols", "p_tr", "d_hT", "p_ba", "s_gate"))

        HT = 2 * T
        qg = carve(HT)
        sqm = carve(HT)
        rp1 = carve(HT)
        rp2 = carve(HT)
        qk = carve(HT)
        sm = carve(384)
        pr = carve(384)
        pT = carve(384)
        vtok = carve(T)
        cv = carve(3 * T).rearrange("p (i t) -> p i t", i=3)
        sl = carve(3 * T).rearrange("p (i t) -> p i t", i=3)
        kq = carve(HT)
        Gm = carve(384)
        Dm = carve(384)
        LT = carve(384)
        AT = carve(384)
        BT = carve(LEVELS * T).rearrange("p (s n) -> p s n", s=LEVELS)
        X = carve(T)
        XT = carve(T)
        Y = carve(T)
        dv = carve(T)
        vp = carve(T)
        vn = carve(T)
        w1 = carve(P)
        mx = carve(8)
        sqd = carve(HT)
        mqk = carve(2 * HT)
        mqk4 = mqk.rearrange("p (a i t) -> p a i t", a=2, i=2)
        msq = carve(2 * HT)
        assert taken[0] <= AT_SPLIT, taken[0]
        taken[0] = stage0

        mv = BT[:, 0:2, :].rearrange("p s n -> p (s n)")
        mstd = carve(HT)
        mpr = carve(HT)
        mpT = carve(HT)
        zs = carve(HT)
        dstd = carve(HT)
        taken[0] = stage0

        mixT = zT
        taken[0] = AT_SCRATCH + 2 * 3 * KT * T
        prod = carve(3 * T).rearrange("p (n t) -> p n t", n=3)
        mixs = carve(T)
        assert taken[0] <= AT_SPLIT
        wo = words(AT_SPLIT, 4 * KT * T).rearrange("p (k n) -> p k n", k=KT)
        taken[0] = AT_SCRATCH
        x1 = carve(NC * D).rearrange("p (c n) -> p c n", c=NC)
        h2 = carve(NC * D).rearrange("p (c n) -> p c n", c=NC)
        gfull = carve(D)

        wq = [words(a, 2 * D) for a in [2 * D * k for k in range(6)] + [39424, 39424 + 2 * D]]
        u_rows = [words(a, D) for a in [AT_RAW + D * k for k in range(3)] + [43520 + D * k for k in range(3)] + [AT_SPLIT + D * k for k in range(2)]]
        v_rows = [words(a, D) for a in [AT_RAW - 2 * D, AT_RAW - D] + [AT_SPLIT + D * k for k in range(2, 8)]]
        h2T = carve(KT * T).rearrange("p (k t) -> p k t", t=T)
        qtok = carve(QW)
        qT = carve(QW)
        sc0 = carve(2 * NKEY).rearrange("p (r n) -> p r n", r=2)
        sc1 = carve(2 * NKEY).rearrange("p (r n) -> p r n", r=2)
        cd0 = carve(TOPK * TOPK)
        cd1 = carve(TOPK * TOPK)
        hot = carve(2 * TOPK * TOPK)
        rv = carve(2 * TOPK).rearrange("p (r k) -> p r k", r=2)
        ri = carve(2 * TOPK).bitcast(U32).rearrange("p (r k) -> p r k", r=2)
        rf = carve(2 * TOPK).rearrange("p (r k) -> p r k", r=2)
        sv = carve(TOPK)
        ci = carve(TOPK).bitcast(U32)
        ab = carve(2 * TOPK).bitcast(U32).rearrange("p (i k) -> p i k", i=2)
        ef = carve(2 * TOPK).rearrange("p (i k) -> p i k", i=2)
        idx_u = [carve(TOPK).bitcast(U32) for _ in range(NC)]
        idx_v = [carve(TOPK).bitcast(U32) for _ in range(NC)]
        ex = carve(TOPK)
        neg = carve(2)
        sums = carve(2)
        rsum = carve(2)
        wts2 = [carve(TOPK) for _ in range(NC)]
        acts = [carve(TOPK) for _ in range(NC)]
        gelu = carve(TOPK)
        coef2 = [carve(TOPK) for _ in range(NC)]
        diag = carve(8 * P).rearrange("p (s j) -> p s j", s=8)
        assert taken[0] <= AT_SPLIT, taken[0]
        s_wo, s_keys, s_x1, s_out = (sem(n) for n in ("s_wo", "s_keys", "s_x1", "s_out"))
        s_wq = [sem(f"s_wq{i}") for i in range(2)]
        WQ_PARTS = ((0, QW), (QW, PHEADS * QW))
        s_u = [sem(f"s_u{i}") for i in range(RING // 2)]
        s_v = [sem(f"s_v{i}") for i in range(RING // 2)]
        t_route = sem("t_route")
        t_sp = sem("t_sp")
        t_pool = sem("t_pool")
        r_step, t_tr, p_end = sem("r_step"), sem("t_tr"), sem("p_end")
        t_h2 = [sem(f"t_h2{c}") for c in range(NC)]
        EARLY = 6
        RSTEPS = 13
        FILLS = (8, 10, 7, 5, 3, 2, 3, 2)
        MFILLS = (18, 16, 16)

        s_w = [sem(f"s_w{i}") for i in range(SLOTS)]
        hi_ready, lo_ready, tiles_done = sem("hi_ready"), sem("lo_ready"), sem("tiles_done")
        s_hhi, s_hlo, s_bhi, s_blo = sem("s_hhi"), sem("s_hlo"), sem("s_bhi"), sem("s_blo")

        def made(kind, it, i):
            if kind == "head":
                return it * 9 + (i + 1)
            if kind == "mem":
                return it * 8 + (9 * HEADS - 8 * HEADS + i + 1)
            return it * 6 + (9 * HEADS + 8 * MEM_HEADS + i + 1)

        def landed(kind, it, i):
            c = (3, 3, 2)[i % 3]
            if kind == "head":
                return (it * 3 + (i // 3 + 1)) * 16
            if kind == "mem":
                return (it * c + ((3 - c) * HEADS + i // 3 + 1)) * 16
            return (it * 2 + (3 * HEADS + MEM_HEADS * c + i // 3 + 1)) * 16

        def before(kind, it, i):
            first_branch = kind == "branch" and isinstance(it, int) and it == 0
            if i < 3 and (first_branch or kind == "mem" and not (isinstance(it, int) and it == HEADS)):
                return made(kind, it, i) - (2, 2, 5)[i]
            if kind == "head" and isinstance(it, int) and it == 0 and i < 3:
                return None
            return made(kind, it, i - 3)
        names = {}

        def ev(name, primed=0):
            if name not in names:
                names[name] = Event(sem(name), primed)
            return names[name]

        def on(eng, name, it):
            e = names[name]
            eng.wait_ge(e.sem, e.now(it))

        def on_before(eng, name, it):
            e = names[name]
            eng.wait_ge(e.sem, e.before(it))

        for n in ("att_sq", "att_gain", "att_ss", "att_rot", "att_std", "rope_cos", "rope_sin", "rope_sum",
                  "att_rstd", "att_qk", "scores", "masked", "maxes", "negmax", "probs", "psums", "z_silu", "dn_scaled", "br_sum", "br_mix", "sig", "x1_ready", "x1_done", "gdots",
                  "pnorm", "vtok_kept", "p_turned", "pT_ready",
                  "conv0", "conv0v", "mv_kept", "taps", "conv3", "silu", "dn_sq", "dn_ss", "dn_std", "dn_rstd", "dn_kq",
                  "Gm_ready", "gdiff", "decay", "decay_masked", "dv_turned", "kq_dots0", "kq_dots1",
                  "LT_ready", "AT_ready", "B_made", "lvlY", "lvlYc", "lvlZ", "lvlX",
                  "att_out", "dn_out", "dv_kept", "sol0", "vp0", "cross", "w1_ready", "sol1", "vn_ready"):
            ev(n)
        for n in ("gate0", "gate1", "z_kept", "att_kept", "dn_kept"):
            ev(n, 1)
        ev("br_prod", 2)
        for n in ("p_q", "p_qk", "p_t", "p_tk", "p_s", "p_sk", "idx_ready", "idx_kept", "negs", "exps",
                  "acts", "gelu", "coef", "weighed", "vmm_end"):
            ev(n)
        ev("dot", RING)
        ev("vrow", RING)
        ev("diag")

        block = ctx.enter_context(nc.Block())

        def w_cols(src, col):
            return src[:, bass.ds(col, P)].rearrange("(k p) j -> p k j", p=P)

        @block.sync
        def _(sp):
            for c in range(NC):
                sp.dma_start(xin[:, c, :], x_d[c * P:(c + 1) * P, :]).then_inc(s_x, 16)
            sp.dma_start(cst[:, :], cst_d).then_inc(s_cst, 16)
            for first, src in rows:
                sp.dma_start(rows_sb[first:first + src.shape[0], :], src).then_inc(s_rows, 16)
            sp.dma_start(wba_t[:, :, :], w_in[:, C_BA:C_BA + 16].rearrange("(k p) n -> p k n", p=P)).then_inc(s_ba, 16)

            def load_rest():
                for c in range(NC):
                    sp.dma_start(xin[:, NC + c, :], mem_d[c * P:(c + 1) * P, :]).then_inc(s_mem, 16)
                for i, k in enumerate((keys1, keys2)):
                    sp.dma_start(keys_in[:, i, :], k).then_inc(s_keys, 16)
                sp.dma_start(arow, a_log.partition_broadcast(P)).then_inc(s_rowb, 16)
                sp.dma_start(dtrow, dt_bias.partition_broadcast(P)).then_inc(s_rowb, 16)

            def load(kind, it, i, src, col):
                free = before(kind, it, i)
                if free is not None:
                    sp.wait_ge(lo_ready, free)
                sp.sem_inc(t_sp, 1)
                sp.dma_start(raw[i % 3], w_cols(src, col)).then_inc(s_w[i % 3], 16)

            def load_head(h, tiles_=range(9)):
                starts = (C_DK + h * P, C_DQ + h * P, C_DV + h * P, C_MV + h * P, C_MQ + h * P, C_MK + h * P,
                                        C_Z + h * P, C_G + h * (2 * P), C_G + h * (2 * P) + P)
                for i in tiles_:
                    load("head", h, i, w_in, starts[i])

            def load_mem(it):
                for i, (src, at) in enumerate(((w_in, C_CQ), (w_in, C_CQ + P), (w_kv, 0), (w_kv, P), (w_kv, D), (w_kv, D + P),
                                               (w_in, C_G + 16 * P), (w_in, C_G + 17 * P))):
                    load("mem", it, i, src, (it - HEADS) * (2 * P) + at)

            def load_branch(m, tiles_):
                for i in tiles_:
                    load("branch", m, i, w_branch[i % 3], m * (2 * P) + (i // 3) * P)

            def load_wo(m):
                for j in range(2):
                    sp.dma_start(wo[:, bass.ds(m * 2 + j, 1), :],
                                 w_out[bass.ds((m * 2 + j) * P, P), :].rearrange("(k p) n -> p k n", k=1)).then_inc(s_wo, 16)

            load_head(0, range(3))
            load_rest()
            load_head(0, range(3, 9))
            with sp.Fori(1, HEADS) as h:
                load_head(h)
            load_mem(HEADS)
            with sp.Fori(HEADS + 1, HEADS + MEM_HEADS) as it:
                load_mem(it)
            load_branch(0, range(3))
            sp.wait_ge(tiles_done, made("mem", HEADS + MEM_HEADS - 1, 7))
            with sp.Fori(0, KT // 2 - 1) as m:
                load_branch(m, range(3, 6))
                load_branch(m + 1, range(3))
                load_wo(m)
            load_branch(KT // 2 - 1, range(3, 6))
            load_wo(KT // 2 - 1)
            sp.wait_ge(tiles_done, made("branch", KT // 2 - 1, 5))
            sp.wait_ge(names["br_mix"].sem, KT)
            for c in range(NC):
                sp.dma_start(x1[:, c, :], x_d[c * P:(c + 1) * P, :]).then_inc(s_x1, 16)
            sp.dma_start(gfull, ffn_g.partition_broadcast(P)).then_inc(s_x1, 16)
            for (a, b), here in zip(WQ_PARTS, s_wq):
                for k in range(KT):
                    sp.dma_start(wq[k][:, a:b], w_q[k * P:(k + 1) * P, a:b]).then_inc(here, 16)
            for c in range(NC):
                sp.wait_ge(p_end, c + 1)
                sp.dma_start(out_d[c * P:(c + 1) * P, :], x1[:, c, :]).then_inc(s_out, 16)
            sp.wait_ge(s_out, 16 * NC)

        @block.scalar
        def _(act):
            def norm_in(g):
                act.wait_ge((s_x, s_mem)[g], 16 * NC)
                for s in range(g * NC, (g + 1) * NC):
                    if s:
                        act.wait_ge(a_sq, s)
                    act.activation(junk, xin[:, s, :], ACT.Square, accum_out=ss4[:, s:s + 1]).then_inc(a_sq, 1)
                act.wait_ge(d_var, g + 1)
                act.activation(var4[:, g * NC:(g + 1) * NC], var4[:, g * NC:(g + 1) * NC], ACT.Sqrt).then_inc(a_std, 1)

            for n in ("gate0", "gate1", "z_kept", "att_kept", "dn_kept"):
                act.sem_inc(names[n].sem, 1)
            norm_in(0)

            def high(kind, it, i):
                free = before(kind, it, i)
                if free is not None:
                    act.wait_ge(tiles_done, free)
                act.wait_ge(s_w[i % 3], landed(kind, it, i))
                act.activation(halves[i % 3][:, 0], raw[i % 3], ACT.Copy).then_inc(hi_ready, 1)

            act.wait_ge(d_hT, 4)
            act.activation(hT[:, 0], hraw, ACT.Copy).then_inc(s_hhi, 1)
            for i in range(3):
                high("head", 0, i)
            norm_in(1)
            high("head", 0, 3)
            act.wait_ge(p_ba, 1)
            act.activation(yb, ps[:, 0, 0:32].rearrange("p (c n) -> p c n", c=NC)[:, :, 0:8], ACT.Exp, scale=-1.0).then_inc(s_gate, 1)
            act.wait_ge(s_rowb, 32)
            act.activation(arow, arow, ACT.Exp).then_inc(s_gate, 1)
            high("head", 0, 4)
            act.wait_ge(s_gate, 6)
            act.activation(yc, ya, ACT.Abs).then_inc(s_gate, 1)
            act.wait_ge(s_gate, 7)
            act.activation(yc, yc, ACT.Exp, scale=-1.0).then_inc(s_gate, 1)
            act.wait_ge(s_gate, 8)
            act.activation(yc, yc, ACT.Ln, bias=1.0).then_inc(s_gate, 1)

            act.wait_ge(s_rows, 16 * len(rows))
            act.wait_ge(d_cols, 1)

            def copy(name, dst, src):
                act.activation(dst, src, ACT.Copy).then_inc(names[name].sem, 1)

            def evacuate_conv(h):
                act.wait_ge(tiles_done, made("head", h, 1))
                for i, tile in ((0, 8), (1, 0)):
                    tap = small[:, bass.ds(h + (R_CONV + 3 * 24 + tile), 1)]
                    ins = act.activation(cv[:, i, :], ps[:, 1, i * T:(i + 1) * T], ACT.Copy, scale=tap)
                ins.then_inc(names["conv0"].sem, 1)

            def evacuate_v(h):
                act.wait_ge(tiles_done, made("head", h, 3))
                tap = small[:, bass.ds(h + (R_CONV + 3 * 24 + 16), 1)]
                act.activation(vtok, ps[:, 2, T:HT], ACT.Copy).then_inc(names["vtok_kept"].sem, 1)
                act.activation(cv[:, 2, :], ps[:, 2, 0:T], ACT.Copy, scale=tap).then_inc(names["conv0v"].sem, 1)

            def silu(h):
                on(act, "conv3", h)
                act.activation(sl[:, :, :], cv[:, :, :], ACT.Silu).then_inc(names["silu"].sem, 1)
                on(act, "silu", h)
                act.activation(sqd, sl[:, 0:2, :].rearrange("p i t -> p (i t)"), ACT.Square).then_inc(names["dn_sq"].sem, 1)

            def evacuate_att(h):
                act.wait_ge(tiles_done, made("head", h, 5))
                act.activation(sqm, ps[:, 0, :], ACT.Square).then_inc(names["att_sq"].sem, 1)
                act.activation(qg[:, 0:T], ps[:, 0, 0:T], ACT.Copy, scale=cols[:, R_MQ:R_MQ + 1])
                act.activation(qg[:, T:HT], ps[:, 0, T:HT], ACT.Copy, scale=cols[:, R_MK:R_MK + 1]).then_inc(names["att_gain"].sem, 1)

            def evacuate_mem(it, a):
                gain = (R_CQ, R_CK)[a]
                act.wait_ge(tiles_done, made("mem", it, 2 * a + 1))
                ins = act.activation(msq[:, a * HT:(a + 1) * HT], ps[:, a, :], ACT.Square)
                if a:
                    ins.then_inc(names["att_sq"].sem, 1)
                for i in range(2):
                    ins = act.activation(mqk4[:, a, i, :], ps[:, a, i * T:(i + 1) * T], ACT.Copy, scale=cols[:, gain + i:gain + i + 1])
                if a:
                    ins.then_inc(names["att_gain"].sem, 1)

            def evacuate_mem_v(it):
                act.wait_ge(tiles_done, made("mem", it, 5))
                copy("mv_kept", mv, ps[:, 2, :])

            def head(h, last=False):
                def split(i):
                    if not last:
                        high("head", h + 1, i)
                    elif i < 8:
                        high("mem", h + 1, i)

                on(act, "att_ss", h)
                act.activation(rp1, ps[:, 3, :], ACT.Sqrt, bias=eps, scale=1.0 / HD).then_inc(names["att_std"].sem, 1)
                on(act, "dn_ss", h)
                act.activation(kq, ps[:, 3, :], ACT.Sqrt, bias=eps, scale=1.0).then_inc(names["dn_std"].sem, 1)
                split(0)
                on(act, "gdiff", h)
                act.activation(Dm, ps[:, 5, 0:384], ACT.Exp).then_inc(names["decay"].sem, 1)
                on(act, "dv_turned", h)
                copy("dv_kept", dv, ps[:, 5, 0:T])
                split(1)
                on(act, "negmax", h)
                act.activation(pr[:, 0:P], sm[:, 0:P], ACT.Exp, bias=mx[:, 2:3], scale=float(HD) ** -0.5, accum_out=mx[:, 4:5])
                act.activation(pr[:, P:384], sm[:, P:384], ACT.Exp, bias=mx[:, 3:4], scale=float(HD) ** -0.5,
                               accum_out=mx[:, 5:6]).then_inc(names["probs"].sem, 1)
                act.wait_ge(tiles_done, made("head", h, 7))
                copy("z_kept", zT[:, bass.ds(h, 1), :], ps[:, 7, None, 0:T])
                copy("gate0", gates[:, bass.ds(h * 2, 1), :], ps[:, 7, None, T:HT])
                split(2)
                act.wait_ge(tiles_done, made("head", h, 8))
                copy("gate1", gates[:, bass.ds(h * 2 + 1, 1), :], ps[:, 2, None, 0:T])
                split(3)
                on(act, "p_turned", h)
                copy("pT_ready", pT, ps[:, 5, 0:384])
                split(4)
                on(act, "att_out", h)
                copy("att_kept", branch[:, bass.ds(h, 1), :], ps[:, 6, None, 0:T])
                if last:
                    evacuate_mem(h + 1, 0)
                else:
                    evacuate_conv(h + 1)
                split(5)
                if last:
                    evacuate_mem(h + 1, 1)
                else:
                    evacuate_v(h + 1)
                split(6)
                on(act, "dn_out", h)
                copy("dn_kept", branch[:, bass.ds(h + 8, 1), :], ps[:, 4, None, 0:T])
                split(7)
                if last:
                    evacuate_mem_v(h + 1)
                else:
                    evacuate_att(h + 1)
                    silu(h + 1)
                split(8)

            act.wait_ge(d_hT, 8)
            act.activation(memhT[:, 0], memraw, ACT.Copy).then_inc(s_hhi, 1)
            high("head", 0, 5)
            evacuate_conv(0)
            high("head", 0, 6)
            evacuate_v(0)
            for i in range(7, 9):
                high("head", 0, i)
            evacuate_att(0)
            silu(0)
            with act.Fori(0, HEADS - 1) as h:
                head(h)
            head(HEADS - 1, True)

            def mem_head(it, last=False):
                split = lambda i: high("mem", it + 1, i) if not last else high("branch", 0, i) if i < 3 else None
                """Memory attention, and the norm of the delta rule's outputs (heads 2 mh, 2 mh + 1)."""
                two = lambda a: a.rearrange("p (i t) -> p i t", i=2)
                heads = branch[:, bass.ds((it - HEADS) * 2 + 8, 2), :]
                act.activation(two(sqd), heads, ACT.Square).then_inc(names["dn_sq"].sem, 1)
                on(act, "att_ss", it)
                act.activation(mstd, ps[:, 3, :], ACT.Sqrt, bias=eps, scale=1.0 / (2 * HD)).then_inc(names["att_std"].sem, 1)
                on(act, "dn_ss", it)
                act.activation(dstd, ps[:, 6, :], ACT.Sqrt, bias=eps, scale=1.0 / HD).then_inc(names["dn_std"].sem, 1)
                act.activation(two(zs), zT[:, bass.ds((it - HEADS) * 2, 2), :], ACT.Silu).then_inc(names["z_silu"].sem, 1)
                split(0)
                split(1)
                split(2)
                on(act, "negmax", it)
                for c in range(NC):
                    ins = act.activation(mpr[:, c * T:(c + 1) * T], ps[:, 4, c * T:(c + 1) * T], ACT.Exp, bias=mx[:, 2 + c:3 + c],
                                         scale=float(2 * HD) ** -0.5, accum_out=mx[:, 4 + c:5 + c])
                ins.then_inc(names["probs"].sem, 1)
                act.wait_ge(tiles_done, made("mem", it, 7))
                copy("gate0", gates[:, bass.ds((it - HEADS) * 2 + 16, 2), :], two(ps[:, 7, :]))
                split(3)
                on(act, "p_turned", it)
                copy("pT_ready", mpT, ps[:, 5, :])
                split(4)
                on(act, "att_out", it)
                copy("att_kept", branch[:, bass.ds((it - HEADS) * 2 + 16, 2), :], two(ps[:, 6, :]))
                if not last:
                    evacuate_mem(it + 1, 0)
                    split(5)
                    evacuate_mem(it + 1, 1)
                    split(6)
                    split(7)
                    evacuate_mem_v(it + 1)

            with act.Fori(HEADS, HEADS + MEM_HEADS - 1) as it:
                mem_head(it)
            mem_head(HEADS + MEM_HEADS - 1, True)
            act.wait_ge(names["dn_scaled"].sem, MEM_HEADS)
            act.wait_ge(names["att_kept"].sem, 1 + HEADS + MEM_HEADS)
            for n in range(3):
                act.activation(branch2[:, 0, 8 * n:8 * n + 8, :], branch[:, 8 * n:8 * n + 8, :], ACT.Copy).then_inc(s_bhi, 1)
            act.wait_ge(names["gate0"].sem, 1 + HEADS + MEM_HEADS)
            for n in range(3):
                act.activation(gates[:, 8 * n:8 * n + 8, :], gates[:, 8 * n:8 * n + 8, :], ACT.Sigmoid).then_inc(names["sig"].sem, 1)
                high("branch", 0, 3 + n)
            for i in range(3):
                high("branch", 1, i)
            with act.Fori(1, KT // 2 - 1) as m:
                for i in range(3, 6):
                    high("branch", m, i)
                for i in range(3):
                    high("branch", m + 1, i)
            for i in range(3, 6):
                high("branch", KT // 2 - 1, i)

            def route_act(n):
                on(act, "p_q", n)
                copy("p_qk", qtok, ps[:, 4, 0:QW])
                on(act, "p_t", n)
                copy("p_tk", qT, ps[:, 5, 0:QW])
                on(act, "p_s", n)
                copy("p_sk", sc0.rearrange("p r n -> p (r n)"), ps[:, 6, 0:2 * NKEY])

            def exps_act(n):
                on(act, "negs", n)
                act.activation(ex, sv, ACT.Exp, bias=neg[:, 0:1], accum_out=sums[:, 0:1]).then_inc(names["exps"].sem, 1)

            def gelu_act(n, c):
                on(act, "acts", n)
                act.activation(gelu, acts[c], ACT.Gelu_apprx_tanh).then_inc(names["gelu"].sem, 1)

            def diag_act(n, c):
                on(act, "coef", n)
                for k in range(TOPK):
                    act.wait_ge(names["vrow"].sem, n * TOPK + (k + 1))
                    act.activation(diag[:, k % 8, :], ident, ACT.Copy, scale=coef2[c][:, k:k + 1]).then_inc(names["diag"].sem, 1)

            def phase_act(n, c, route=True):
                gelu_act(n, c)
                if route:
                    route_act(n + 2)
                diag_act(n, c)
                if route:
                    exps_act(n + 2)

            def norm_act(c):
                act.wait_ge(names["x1_ready"].sem, 2 * (c + 1))
                act.activation(h2[:, c, :], x1[:, c, :], ACT.Square, accum_out=sq2[:, c:c + 1]).then_inc(names["x1_done"].sem, 1)
                act.wait_ge(t_h2[c], 1)
                act.activation(std2[:, c:c + 1], std2[:, c:c + 1], ACT.Sqrt).then_inc(t_h2[c], 1)

            norm_act(0)
            route_act(0)
            exps_act(0)
            norm_act(1)
            route_act(1)
            exps_act(1)
            with act.Fori(0, PHEADS - 1) as h:
                phase_act(h * NC, 0)
                phase_act(h * NC + 1, 1)
            phase_act(UNITS - 2, 0, False)
            phase_act(UNITS - 1, 1, False)

        @block.gpsimd
        def _(pool):
            def low(kind, it, i):
                pool.wait_ge(hi_ready, made(kind, it, i))
                pool.tensor_tensor(halves[i % 3][:, 1], raw[i % 3], halves[i % 3][:, 0], ALU.subtract).then_inc(lo_ready, 1)

            def head(h, last=False):
                def split(i):
                    if not last:
                        low("head", h + 1, i)
                    elif i < 8:
                        low("mem", h + 1, i)

                split(0)
                on(pool, "decay", h)
                pool.tensor_tensor(Dm, Dm, upto, ALU.mult).then_inc(names["decay_masked"].sem, 1)
                split(1)
                on(pool, "LT_ready", h)
                lt2 = LT.rearrange("p (t j) -> p t j", j=P)[:, 0:3:2, :]
                for s in range(LEVELS):
                    pool.tensor_tensor(BT[:, s, :].rearrange("p (c j) -> p c j", c=NC), lt2,
                                       levels[:, s, None, :].to_broadcast([P, NC, P]), ALU.mult).then_inc(names["B_made"].sem, 1)
                for i in range(2, 9):
                    split(i)

            for i in range(9):
                low("head", 0, i)
            with pool.Fori(0, HEADS - 1) as h:
                head(h)
            head(HEADS - 1, True)

            def gather(table, used, here, rows_, idx, n, k):
                pool.wait_ge(names[used].sem, n * TOPK + (k + 1))
                pool.sem_inc(t_pool, 1)
                pool.indirect_dma_start(rows_[k % RING], None, table,
                                        bass.IndirectOffsetOnAxis(ap=idx[:, k:k + 1], axis=0)).then_inc(here[k % RING // 2], 16)

            def phase_pool(n, c, more=True):
                if more:
                    on(pool, "idx_ready", n + 1)
                    pool.sem_inc(t_pool, 1)
                on(pool, "idx_kept", n)
                pool.sem_inc(t_pool, 1)
                for k in range(TOPK):
                    if more:
                        gather(peer_u, "dot", s_u, u_rows, idx_u[1 - c], n + 1, k)
                    gather(peer_v, "vrow", s_v, v_rows, idx_v[c], n, k)

            pool.sem_inc(names["dot"].sem, RING)
            on(pool, "idx_ready", 0)
            for k in range(RING):
                if k == 6:
                    pool.wait_ge(names["gdots"].sem, 2 * NC)
                    pool.sem_inc(t_pool, 1)
                gather(peer_u, "dot", s_u, u_rows, idx_u[0], 0, k)
            on(pool, "idx_kept", 0)
            for k in range(RING):
                gather(peer_v, "vrow", s_v, v_rows, idx_v[0], 0, k)
            for k in range(RING, TOPK):
                gather(peer_u, "dot", s_u, u_rows, idx_u[0], 0, k)
            on(pool, "idx_ready", 1)
            for k in range(TOPK):
                gather(peer_u, "dot", s_u, u_rows, idx_u[1], 1, k)
                if k >= RING:
                    gather(peer_v, "vrow", s_v, v_rows, idx_v[0], 0, k)
            with pool.Fori(0, PHEADS - 1) as h:
                phase_pool(h * NC + 1, 1)
                phase_pool(h * NC + 2, 0)
            phase_pool(UNITS - 1, 1, False)

        @block.vector
        def _(dve):
            def done(name):
                return names[name].sem

            dve.wait_ge(p_cols, 1)
            dve.tensor_copy(cols, ps[:, 7, 0:NROWS]).then_inc(d_cols, 1)
            for g in range(2):
                half2 = slice(g * NC, (g + 1) * NC)
                dve.wait_ge(a_sq, (g + 1) * NC)
                dve.tensor_scalar(var4[:, half2], ss4[:, half2], 1.0 / D, EPS, ALU.mult, ALU.add).then_inc(d_var, 1)
                dve.wait_ge(a_std, g + 1)
                dve.reciprocal(rstd4[:, half2], var4[:, half2]).then_inc(d_rstd, 1)
                dve.wait_ge(d_rstd, g + 1)
                for s in range(g * NC, (g + 1) * NC):
                    dve.tensor_scalar(xin[:, s, :], xin[:, s, :], rstd4[:, s:s + 1], None, ALU.mult).then_inc(d_xn, 1)
                if g == 1:
                    dve.wait_ge(p_keys, 1)
                    dve.tensor_copy(keysT[:, :], ps[:, 6, 0:2 * P]).then_inc(d_keys, 1)
                dve.wait_ge(d_cols, 1)
                for b in range(4 * g, 4 * g + 4):
                    s, half = b // 2, b % 2
                    c = s % NC
                    gain = (R_ATTN, R_MEM)[g] + 4 * half
                    dve.wait_ge(p_tr, b + 1)
                    dve.tensor_tensor((hraw, memraw)[g][:, 4 * half:4 * half + 4, c * P:(c + 1) * P],
                                      ps[:, b, :].rearrange("p (k t) -> p k t", k=4),
                                      cols[:, gain:gain + 4, None].to_broadcast([P, 4, P]), ALU.mult).then_inc(d_hT, 1)
                if g == 0:
                    dve.wait_ge(s_hhi, 1)
                    dve.tensor_tensor(hT[:, 1], hraw, hT[:, 0], ALU.subtract).then_inc(s_hlo, 1)
            dve.wait_ge(s_gate, 2)
            dve.tensor_scalar(yb, yb, 1.0, None, ALU.add).then_inc(s_gate, 1)
            dve.wait_ge(s_gate, 3)
            dve.reciprocal(btok, yb).then_inc(s_gate, 1)
            dve.tensor_tensor(ya, ps[:, 0, 0:32].rearrange("p (c n) -> p c n", c=NC)[:, :, 8:16],
                              dtrow[:, None, :].to_broadcast([P, NC, 8]), ALU.add).then_inc(s_gate, 1)
            dve.wait_ge(s_gate, 5)
            dve.tensor_scalar(yb, ya, 0.0, None, ALU.max).then_inc(s_gate, 1)
            dve.wait_ge(s_gate, 9)
            dve.tensor_tensor(yb, yb, yc, ALU.add).then_inc(s_gate, 1)
            dve.wait_ge(s_gate, 10)
            dve.scalar_tensor_tensor(out=gtok, in0=yb, scalar=-1.0, in1=arow[:, None, :].to_broadcast([P, NC, 8]),
                                     op0=ALU.mult, op1=ALU.mult).then_inc(s_gate, 1)
            dve.wait_ge(s_gate, 11)
            dve.wait_ge(s_cst, 16)
            dve.wait_ge(s_hhi, 2)
            dve.tensor_tensor(memhT[:, 1], memraw, memhT[:, 0], ALU.subtract).then_inc(s_hlo, 1)

            def low(kind, it, i):
                dve.wait_ge(hi_ready, made(kind, it, i))
                dve.tensor_tensor(halves[i % 3][:, 1], raw[i % 3], halves[i % 3][:, 0], ALU.subtract).then_inc(lo_ready, 1)

            def log_decays(h):
                g0, g1 = (small[:, bass.ds(h + (120 + 8 * c), 1)] for c in range(NC))
                dve.tensor_scalar(Gm[:, 0:T], upto[:, 0:T], g0, None, ALU.mult)
                dve.tensor_scalar(Gm[:, T:384], upto[:, T:384], g1, None, ALU.mult).then_inc(done("Gm_ready"), 1)

            def convolve(h, part, back):
                if back == 1:
                    on(dve, part, h)
                else:
                    dve.wait_ge(done("taps"), h * 6 + (back - 1 if part == "conv0" else back + 2))
                for i, tile in ((0, 8), (1, 0)) if part == "conv0" else ((2, 16),):
                    src = ps[:, 1, i * T:(i + 1) * T] if i < 2 else ps[:, 2, 0:T]
                    tap = small[:, bass.ds(h + (R_CONV + (3 - back) * 24 + tile), 1)]
                    ins = dve.scalar_tensor_tensor(out=cv[:, i, back:T], in0=src[:, 0:T - back], scalar=tap,
                                                   in1=cv[:, i, back:T], op0=ALU.mult, op1=ALU.add)
                ins.then_inc(done("taps"), 1)

            def convolved(h):
                dve.wait_ge(done("taps"), h * 6 + 6)
                dve.sem_inc(done("conv3"), 1)

            def head(h, last=False):
                b0, b1 = (small[:, bass.ds(h + (136 + 8 * c), 1)] for c in range(NC))
                both = lambda a: a.rearrange("p (i t) -> p i t", i=2)
                on(dve, "att_gain", h)
                dve.tensor_tensor(both(qk), both(qg), cos[:, None, :].to_broadcast([P, 2, T]), ALU.mult).then_inc(done("rope_cos"), 1)
                on(dve, "att_rot", h)
                dve.tensor_tensor(both(rp2), both(ps[:, 4, :]), sin[:, None, :].to_broadcast([P, 2, T]), ALU.mult).then_inc(done("rope_sin"), 1)
                on(dve, "rope_sin", h)
                dve.tensor_tensor(qk, qk, rp2, ALU.add).then_inc(done("rope_sum"), 1)
                on(dve, "att_std", h)
                dve.reciprocal(rp1, rp1).then_inc(done("att_rstd"), 1)
                on(dve, "att_rstd", h)
                dve.tensor_tensor(qk, qk, rp1, ALU.mult).then_inc(done("att_qk"), 1)
                on(dve, "dn_std", h)
                dve.reciprocal(kq, kq).then_inc(done("dn_rstd"), 1)
                on(dve, "dn_rstd", h)
                dve.tensor_tensor(kq, kq, sl[:, 0:2, :].rearrange("p i t -> p (i t)"), ALU.mult).then_inc(done("dn_kq"), 1)
                on(dve, "decay_masked", h)
                on(dve, "kq_dots0", h)
                dve.scalar_tensor_tensor(out=LT[:, 0:T], in0=ps[:, 4, 0:T], scalar=b0, in1=Dm[:, 0:T], op0=ALU.mult, op1=ALU.mult)
                on(dve, "kq_dots1", h)
                dve.scalar_tensor_tensor(out=LT[:, T:384], in0=ps[:, 5, 0:P], scalar=b1, in1=Dm[:, T:384],
                                         op0=ALU.mult, op1=ALU.mult).then_inc(done("LT_ready"), 1)
                on(dve, "scores", h)
                dve.tensor_tensor(sm, ps[:, 6, 0:384], mask, ALU.add).then_inc(done("masked"), 1)
                on(dve, "masked", h)
                dve.tensor_reduce(mx[:, 0:1], sm[:, 0:P], AX.X, ALU.max)
                dve.tensor_reduce(mx[:, 1:2], sm[:, P:384], AX.X, ALU.max).then_inc(done("maxes"), 1)
                dve.scalar_tensor_tensor(out=AT[:, 0:T], in0=ps[:, 4, T:HT], scalar=float(HD) ** -0.5, in1=Dm[:, 0:T],
                                         op0=ALU.mult, op1=ALU.mult)
                dve.scalar_tensor_tensor(out=AT[:, T:384], in0=ps[:, 5, P:T], scalar=float(HD) ** -0.5, in1=Dm[:, T:384],
                                         op0=ALU.mult, op1=ALU.mult).then_inc(done("AT_ready"), 1)
                on(dve, "maxes", h)
                dve.tensor_scalar(mx[:, 2:4], mx[:, 0:2], -float(HD) ** -0.5, None, ALU.mult).then_inc(done("negmax"), 1)
                two = lambda a: a.rearrange("p (c j) -> p c j", c=NC)
                idb = ident[:, None, :].to_broadcast([P, NC, P])
                on(dve, "B_made", h * LEVELS)
                dve.tensor_tensor(two(XT), idb, two(BT[:, 0, :]), ALU.subtract)
                on(dve, "lvlZ", h * LEVELS)
                dve.tensor_tensor(two(X), idb, two(ps[:, 3, 0:T]), ALU.subtract).then_inc(done("lvlX"), 1)
                for s in range(1, LEVELS):
                    on(dve, "lvlY", h * (LEVELS - 1) + (s - 1))
                    dve.tensor_copy(Y, ps[:, 4, 0:T]).then_inc(done("lvlYc"), 1)
                    if s >= 5 and not last:
                        convolve(h + 1, "conv0", s - 4)
                    if s == 1:
                        on(dve, "probs", h)
                        dve.reciprocal(mx[:, 6:8], mx[:, 4:6]).then_inc(done("psums"), 1)
                        on(dve, "psums", h)
                        dve.tensor_scalar(pr[:, 0:P], pr[:, 0:P], mx[:, 6:7], None, ALU.mult)
                        dve.tensor_scalar(pr[:, P:384], pr[:, P:384], mx[:, 7:8], None, ALU.mult).then_inc(done("pnorm"), 1)
                    on(dve, "lvlZ", h * LEVELS + s)
                    if s < LEVELS - 1:
                        dve.tensor_tensor(X, X, ps[:, 3, 0:T], ALU.subtract)
                    dve.tensor_tensor(XT, XT, ps[:, 3, T:HT], ALU.subtract).then_inc(done("lvlX"), 1)
                on(dve, "sol0", h)
                dve.tensor_copy(vp[:, 0:P], ps[:, 4, 0:P]).then_inc(done("vp0"), 1)
                if not last:
                    convolve(h + 1, "conv0", 3)
                on(dve, "cross", h)
                dve.tensor_tensor(w1, dv[:, P:T], ps[:, 3, 0:P], ALU.subtract).then_inc(done("w1_ready"), 1)
                dve.tensor_scalar(vn[:, 0:P], vp[:, 0:P], b0, None, ALU.mult)
                on(dve, "sol1", h)
                dve.tensor_scalar(vn[:, P:T], ps[:, 4, 0:P], b1, None, ALU.mult).then_inc(done("vn_ready"), 1)
                if not last:
                    log_decays(h + 1)
                    for back in (1, 2, 3):
                        convolve(h + 1, "conv0v", back)
                    convolved(h + 1)

            log_decays(0)
            for part in ("conv0", "conv0v"):
                for back in (1, 2, 3):
                    convolve(0, part, back)
            convolved(0)
            with dve.Fori(0, HEADS - 1) as h:
                head(h)
            head(HEADS - 1, True)
            dve.wait_ge(lo_ready, made("mem", HEADS, 7))

            def mem_head(it, last=False):
                split = lambda i: low("mem", it + 1, i) if not last else low("branch", 0, i) if i < 3 else None
                two = lambda a: a.rearrange("p (i t) -> p i t", i=2)
                heads = branch[:, bass.ds((it - HEADS) * 2 + 8, 2), :]
                on(dve, "att_std", it)
                dve.reciprocal(mstd, mstd).then_inc(done("att_rstd"), 1)
                on(dve, "att_rstd", it)
                on(dve, "att_gain", it)
                dve.tensor_tensor(mqk4, mqk4, two(mstd)[:, :, None, :].to_broadcast([P, 2, 2, T]), ALU.mult).then_inc(done("att_qk"), 1)
                split(0)
                on(dve, "dn_std", it)
                dve.reciprocal(dstd, dstd).then_inc(done("dn_rstd"), 1)
                split(1)
                on(dve, "dn_rstd", it)
                on(dve, "z_silu", it - HEADS)
                dve.scalar_tensor_tensor(out=dstd, in0=dstd, scalar=cols[:, R_DN:R_DN + 1], in1=zs, op0=ALU.mult,
                                         op1=ALU.mult).then_inc(done("dn_kq"), 1)
                on(dve, "dn_kq", it)
                dve.tensor_tensor(heads, heads, two(dstd), ALU.mult).then_inc(done("dn_scaled"), 1)
                on(dve, "scores", it)
                dve.tensor_reduce(mx[:, 0:2], two(ps[:, 4, :]), AX.X, ALU.max).then_inc(done("maxes"), 1)
                on(dve, "maxes", it)
                dve.tensor_scalar(mx[:, 2:4], mx[:, 0:2], -float(2 * HD) ** -0.5, None, ALU.mult).then_inc(done("negmax"), 1)
                split(2)
                on(dve, "probs", it)
                dve.reciprocal(mx[:, 6:8], mx[:, 4:6]).then_inc(done("psums"), 1)
                on(dve, "psums", it)
                dve.tensor_tensor(two(mpr), two(mpr), mx[:, 6:8, None].to_broadcast([P, 2, T]), ALU.mult).then_inc(done("pnorm"), 1)
                for i in range(3, 8):
                    split(i)

            with dve.Fori(HEADS, HEADS + MEM_HEADS - 1) as it:
                mem_head(it)
            mem_head(HEADS + MEM_HEADS - 1, True)
            for n in range(3):
                dve.wait_ge(s_bhi, n + 1)
                dve.tensor_tensor(branch2[:, 1, 8 * n:8 * n + 8, :], branch[:, 8 * n:8 * n + 8, :], branch2[:, 0, 8 * n:8 * n + 8, :],
                                  ALU.subtract).then_inc(s_blo, 1)
            dve.wait_ge(done("sig"), 3)
            g4 = gates.rearrange("p (n m) t -> p n m t", n=3)

            def mix(mp, last=False):
                for j in range(2):
                    m = mp * 2 + j
                    for i in range(3):
                        if j == 0:
                            low("branch", mp, 3 + i)
                        elif not last:
                            low("branch", mp + 1, i)
                    dve.wait_ge(tiles_done, made("branch", mp, 3 * j + 2))
                    dve.tensor_tensor(prod, ps[:, 3 * j:3 * j + 3, 0:T], g4[:, :, bass.ds(m, 1), :].rearrange("p n o t -> p n (o t)"),
                                      ALU.mult).then_inc(done("br_prod"), 1)
                    on(dve, "br_prod", m)
                    dve.tensor_tensor(mixs, prod[:, 0, :], prod[:, 1, :], ALU.add).then_inc(done("br_sum"), 1)
                    on(dve, "br_sum", m)
                    dve.tensor_tensor(mixT[:, bass.ds(m, 1), :], mixs[:, None, :], prod[:, 2:3, :], ALU.add).then_inc(done("br_mix"), 1)
                    on(dve, "br_mix", m)

            with dve.Fori(0, KT // 2 - 1) as mp:
                mix(mp)
            mix(KT // 2 - 1, True)

            def route_dve(n, c):
                step = [0]

                def link(ins):
                    ins.then_inc(r_step, 1)
                    step[0] += 1
                    dve.wait_ge(r_step, n * RSTEPS + step[0])
                    dve.sem_inc(t_route, 1)

                def best(values, where_, rows_, scratch):
                    link([dve.max(v[:, 0:8], a) for v, a in zip(values, rows_)][-1])
                    for v, i, a, b in zip(values, where_, rows_, scratch):
                        dve.max_index(i[:, 0:8], v[:, 0:8], a)
                        ins = dve.match_replace(b, v[:, 0:8], a, -3.0e38)
                    link(ins)
                    link([dve.max(v[:, 8:16], b) for v, b in zip(values, scratch)][-1])
                    link([dve.max_index(i[:, 8:16], v[:, 8:16], b) for v, i, b in zip(values, where_, scratch)][-1])

                on(dve, "p_sk", n)
                dve.sem_inc(t_route, 1)
                best([rv[:, r, :] for r in range(2)], [ri[:, r, :] for r in range(2)],
                     [sc0[:, r, :] for r in range(2)], [sc1[:, r, :] for r in range(2)])
                dve.tensor_copy(rf, ri)
                link(dve.tensor_tensor(cd0.rearrange("p (a b) -> p a b", a=TOPK), rv[:, 0, :, None].to_broadcast([P, TOPK, TOPK]),
                                       rv[:, 1, None, :].to_broadcast([P, TOPK, TOPK]), ALU.add))
                best([sv], [ci], [cd0], [cd1])
                dve.tensor_scalar(neg[:, 0:1], sv[:, 0:1], -1.0, None, ALU.mult).then_inc(done("negs"), 1)
                dve.tensor_scalar(ab[:, 0, :], ci, 4, None, ALU.logical_shift_right)
                link(dve.tensor_scalar(ab[:, 1, :], ci, 15, None, ALU.bitwise_and))
                h3 = hot.rearrange("p (r a) -> p r a", a=TOPK)
                link(dve.tensor_tensor(h3, ab.rearrange("p i k -> p (i k)")[:, :, None].to_broadcast([P, 2 * TOPK, TOPK]),
                                       iota[:, None, :].to_broadcast([P, 2 * TOPK, TOPK]), ALU.is_equal))
                h4 = hot.rearrange("p (r k a) -> p r k a", r=2, k=TOPK)
                link(dve.tensor_tensor(h4, h4, rf[:, :, None, :].to_broadcast([P, 2, TOPK, TOPK]), ALU.mult))
                link(dve.tensor_reduce(ef.rearrange("p i k -> p (i k)"), h3, AX.X, ALU.add))
                dve.scalar_tensor_tensor(out=idx_u[c], in0=ef[:, 0, :], scalar=float(NKEY), in1=ef[:, 1, :],
                                         op0=ALU.mult, op1=ALU.add).then_inc(done("idx_ready"), 1)
                assert step[0] == RSTEPS

            def keep_idx(n, c):
                dve.wait_ge(done("idx_ready"), n + 1)
                dve.sem_inc(t_route, 1)
                dve.wait_ge(done("vrow"), RING if isinstance(n, int) and n < 2 else (n - 1) * TOPK + RING)
                dve.tensor_copy(idx_v[c], idx_u[c]).then_inc(done("idx_kept"), 1)

            def weigh(n, c):
                on(dve, "exps", n)
                dve.reciprocal(rsum[:, 0:1], sums[:, 0:1]).then_inc(done("weighed"), 1)
                dve.wait_ge(done("weighed"), n * 2 + 1)
                dve.tensor_scalar(wts2[c], ex, rsum[:, 0:1], None, ALU.mult).then_inc(done("weighed"), 1)

            def dots(n, c, rows_):
                for k in rows_:
                    if k % 2 == 0:
                        dve.wait_ge(s_u[k % RING // 2], (n * 2 + (k // RING + 1)) * 32)
                    row = u_rows[k % RING]
                    dve.tensor_tensor_reduce(out=row, in0=row, in1=h2[:, c, :], scale=1.0, scalar=0.0,
                                             op0=ALU.mult, op1=ALU.add, accum_out=acts[c][:, k:k + 1]).then_inc(done("dot"), 1)

            def dots_done(n):
                dve.wait_ge(done("dot"), n * TOPK + (TOPK + RING))
                dve.sem_inc(done("acts"), 1)

            def coefficients(n, c):
                dve.wait_ge(done("weighed"), n * 2 + 2)
                on(dve, "gelu", n)
                dve.tensor_tensor(coef2[c], gelu, wts2[c], ALU.mult).then_inc(done("coef"), 1)

            def phase_dve(n, c, route=True):
                dots(n + 1, 1 - c, range(0, EARLY))
                if route:
                    route_dve(n + 2, c)
                keep_idx(n + 1, 1 - c)
                dots(n + 1, 1 - c, range(EARLY, TOPK))
                dots_done(n + 1)
                if route:
                    weigh(n + 2, c)
                coefficients(n + 1, 1 - c)

            def norm_dve(c):
                for n in range(2):
                    b = 2 * c + n
                    dve.wait_ge(done("gdots"), b + 1)
                    dve.tensor_tensor(x1[:, c, n * 512:(n + 1) * 512], x1[:, c, n * 512:(n + 1) * 512], ps[:, b, :],
                                      ALU.add).then_inc(done("x1_ready"), 1)
                dve.wait_ge(done("x1_done"), c + 1)
                dve.tensor_scalar(std2[:, c:c + 1], sq2[:, c:c + 1], 1.0 / D, EPS, ALU.mult, ALU.add).then_inc(t_h2[c], 1)
                dve.wait_ge(t_h2[c], 2)
                dve.reciprocal(rstd2[:, c:c + 1], std2[:, c:c + 1]).then_inc(t_h2[c], 1)
                dve.wait_ge(t_h2[c], 3)
                dve.scalar_tensor_tensor(out=h2[:, c, :], in0=x1[:, c, :], scalar=rstd2[:, c:c + 1], in1=gfull[:, :],
                                         op0=ALU.mult, op1=ALU.mult).then_inc(t_h2[c], 1)
                for half in range(2):
                    dve.wait_ge(t_tr, 1 + 2 * c + half)
                    dve.tensor_copy(h2T[:, 4 * half:4 * half + 4, c * P:(c + 1) * P],
                                    ps[:, 2 * c + half, :].rearrange("p (k t) -> p k t", k=4)).then_inc(t_h2[c], 1)

            dve.wait_ge(s_x1, 16 * (NC + 1))
            norm_dve(0)
            route_dve(0, 0)
            keep_idx(0, 0)
            norm_dve(1)
            weigh(0, 0)
            route_dve(1, 1)
            dots(0, 0, range(TOPK))
            dots_done(0)
            weigh(1, 1)
            coefficients(0, 0)
            with dve.Fori(0, PHEADS - 1) as h:
                phase_dve(h * NC, 0)
                phase_dve(h * NC + 1, 1)
            phase_dve(UNITS - 2, 0, False)
            dve.wait_ge(done("vmm_end"), 1)
            for c in range(NC):
                dve.tensor_tensor(x1[:, c, :], x1[:, c, :], ps[:, 2 * c:2 * c + 2, :].rearrange("p b n -> p (b n)"),
                                  ALU.add).then_inc(p_end, 1)

        @block.tensor
        def _(pe):
            def done(name):
                return names[name].sem

            pe.wait_ge(s_cst, 16)
            pe.wait_ge(s_rows, 16 * len(rows))
            pe.transpose(ps[:, 7, 0:NROWS], rows_sb[0:NROWS, :], ident[0:NROWS, 0:NROWS]).then_inc(p_cols, 1)

            def turn_in(b):
                s, half = b // 2, b % 2
                pe.wait_ge(d_xn, s + 1)
                if b == 7:
                    pe.wait_ge(d_cols, 1)
                if b == 6:
                    pe.wait_ge(d_keys, 1)
                for k in range(4):
                    at = (4 * half + k) * P
                    ins = pe.transpose(ps[:, b, k * P:(k + 1) * P], xin[:, s, at:at + P], ident)
                ins.then_inc(p_tr, 1)

            for b in range(4):
                turn_in(b)
            pe.wait_ge(d_hT, 4)
            pe.wait_ge(s_ba, 16)
            for c in range(NC):
                for k in range(KT):
                    ins = pe.matmul(ps[:, 0, 16 * c:16 * c + 16], hraw[:, k, c * P:(c + 1) * P], wba_t[:, k, :],
                                    start=(k == 0), stop=(k == KT - 1))
            ins.then_inc(p_ba, 1)
            pe.sem_inc(done("br_prod"), 2)

            def whole(steps):
                for _ in steps:
                    pass

            def product(dst, lhs, rhs, first, last):
                pe.matmul(dst, lhs[0], rhs[0], start=first, stop=False)
                pe.matmul(dst, lhs[0], rhs[1], start=False, stop=False)
                return pe.matmul(dst, lhs[1], rhs[0], start=False, stop=last)

            def tile(kind, it, i, dst, rhs):
                pe.wait_ge(lo_ready, made(kind, it, i))
                w = halves[i % 3]
                for k in range(KT):
                    ins = product(dst, [w[:, f, k, :] for f in range(2)], [rhs[:, f, k, :] for f in range(2)], k == 0, k == KT - 1)
                    if k == KT - 1:
                        ins.then_inc(tiles_done, 1)
                    yield

            def by_token(kind, it, i, dst, lhs):
                pe.wait_ge(lo_ready, made(kind, it, i))
                w = halves[i % 3]
                for c in range(NC):
                    for k in range(KT):
                        ins = product(dst(c), [lhs[:, f, k, c * P:(c + 1) * P] for f in range(2)], [w[:, f, k, :] for f in range(2)],
                                      k == 0, k == KT - 1)
                        if c == NC - 1 and k == KT - 1:
                            ins.then_inc(tiles_done, 1)
                        if k % 2:
                            yield

            def tiles(h):
                yield from tile("head", h, 0, ps[:, 1, 0:T], hT)
                yield from tile("head", h, 1, ps[:, 1, T:HT], hT)
                on_before(pe, "gate1", h)
                yield from tile("head", h, 2, ps[:, 2, 0:T], hT)
                yield from by_token("head", h, 3, lambda c: ps[:, 2, T + c * P:T + (c + 1) * P], hT)
                yield from tile("head", h, 4, ps[:, 0, 0:T], hT)
                yield from tile("head", h, 5, ps[:, 0, T:HT], hT)

            def mem_tiles(it):
                yield from tile("mem", it, 0, ps[:, 0, 0:T], hT)
                yield from tile("mem", it, 1, ps[:, 0, T:HT], hT)
                yield from tile("mem", it, 2, ps[:, 1, 0:T], memhT)
                yield from tile("mem", it, 3, ps[:, 1, T:HT], memhT)
                on_before(pe, "gate1", HEADS)
                for i in range(2):
                    yield from by_token("mem", it, 4 + i, lambda c, i=i: ps[:, 2, c * T + i * P:c * T + (i + 1) * P], memhT)

            def gate_tiles(h):
                on_before(pe, "z_kept", h)
                on_before(pe, "gate0", h)
                yield from tile("head", h, 6, ps[:, 7, 0:T], hT)
                yield from tile("head", h, 7, ps[:, 7, T:HT], hT)
                yield from tile("head", h, 8, ps[:, 2, 0:T], hT)

            def mem_gate_tiles(it):
                on_before(pe, "gate0", it)
                yield from tile("mem", it, 6, ps[:, 7, 0:T], hT)
                yield from tile("mem", it, 7, ps[:, 7, T:HT], hT)

            def filling(*parts):
                def chained():
                    for part in parts:
                        yield from part
                rest = chained()

                def fill(n):
                    for _ in range(n):
                        next(rest, None)
                return fill

            def head(h, following):
                fill = filling(gate_tiles(h), following)
                on(pe, "att_sq", h)
                pe.matmul(ps[:, 3, :], ones, sqm, start=True, stop=True).then_inc(done("att_ss"), 1)
                on_before(pe, "dn_kept", h)
                on(pe, "att_gain", h)
                pe.matmul(ps[:, 4, :], swap, qg, start=True, stop=True).then_inc(done("att_rot"), 1)
                on(pe, "Gm_ready", h)
                pe.matmul(ps[:, 5, 0:T], after, Gm[:, 0:T], start=True, stop=False, skip_group_check=True)
                pe.matmul(ps[:, 5, P:T], ones, Gm[:, T:384], start=False, stop=True, skip_group_check=True)
                pe.matmul(ps[:, 5, T:384], after, Gm[:, T:384], start=True, stop=True, skip_group_check=True).then_inc(done("gdiff"), 1)
                fill(FILLS[0])
                on(pe, "dn_sq", h)
                on(pe, "att_std", h)
                pe.matmul(ps[:, 3, :], ones, sqd, start=True, stop=True).then_inc(done("dn_ss"), 1)
                fill(FILLS[1])
                on(pe, "att_qk", h)
                on_before(pe, "att_kept", h)
                pe.matmul(ps[:, 6, 0:P], qk[:, 0:P], qk[:, T:T + P], start=True, stop=True)
                pe.matmul(ps[:, 6, P:384], qk[:, P:T], qk[:, T:HT], start=True, stop=True).then_inc(done("scores"), 1)
                on(pe, "silu", h)
                on(pe, "decay", h)
                for c in range(NC):
                    ins = pe.transpose(ps[:, 5, c * P:(c + 1) * P], sl[:, 2, c * P:(c + 1) * P], ident)
                ins.then_inc(done("dv_turned"), 1)
                fill(FILLS[2])
                on(pe, "dn_kq", h)
                pe.matmul(ps[:, 4, :], kq[:, 0:P], kq, start=True, stop=True).then_inc(done("kq_dots0"), 1)
                on(pe, "dv_kept", h)
                pe.matmul(ps[:, 5, 0:T].rearrange("p (i j) -> p i j", i=2), kq[:, P:T],
                          kq.rearrange("p (i t) -> p i t", i=2)[:, :, P:T], start=True, stop=True).then_inc(done("kq_dots1"), 1)
                fill(FILLS[3])
                on(pe, "B_made", h * LEVELS)
                for c in range(NC):
                    ins = pe.transpose(ps[:, 3, c * P:(c + 1) * P], BT[:, 0, c * P:(c + 1) * P], ident)
                ins.then_inc(done("lvlZ"), 1)
                fill(FILLS[4])
                on(pe, "AT_ready", h)
                for s in range(1, LEVELS):
                    on(pe, "B_made", h * LEVELS + s)
                    on(pe, "lvlX", h * LEVELS + (s - 1))
                    for c in range(NC):
                        a, b = c * P, (c + 1) * P
                        ins = pe.matmul(ps[:, 4, a:b], BT[:, s, a:b], X[:, a:b], start=True, stop=True)
                    ins.then_inc(done("lvlY"), 1)
                    if s == 2:
                        on(pe, "pnorm", h)
                        pe.transpose(ps[:, 5, 0:P], pr[:, 0:P], ident)
                        pe.transpose(ps[:, 5, P:T], pr[:, P:T], ident)
                        pe.transpose(ps[:, 5, T:384], pr[:, T:384], ident).then_inc(done("p_turned"), 1)
                    if s == 4:
                        on(pe, "pT_ready", h)
                        on(pe, "vtok_kept", h)
                        pe.matmul(ps[:, 6, 0:T], vtok[:, 0:P], pT[:, 0:T], start=True, stop=False, skip_group_check=True)
                        pe.matmul(ps[:, 6, P:T], vtok[:, P:T], pT[:, T:384], start=False, stop=True,
                                  skip_group_check=True).then_inc(done("att_out"), 1)
                    fill(FILLS[5])
                    on(pe, "lvlYc", h * (LEVELS - 1) + (s - 1))
                    for c in range(NC):
                        a, b = c * P, (c + 1) * P
                        if s < LEVELS - 1:
                            pe.matmul(ps[:, 3, a:b], XT[:, a:b], Y[:, a:b], start=True, stop=True)
                        ins = pe.matmul(ps[:, 3, T + a:T + b], Y[:, a:b], XT[:, a:b], start=True, stop=True)
                    ins.then_inc(done("lvlZ"), 1)
                    fill(FILLS[6])
                on(pe, "lvlX", h * LEVELS + (LEVELS - 1))
                pe.matmul(ps[:, 4, 0:P], XT[:, 0:P], dv[:, 0:P], start=True, stop=True).then_inc(done("sol0"), 1)
                fill(FILLS[7])
                on(pe, "vp0", h)
                pe.matmul(ps[:, 3, 0:P], LT[:, P:T], vp[:, 0:P], start=True, stop=True).then_inc(done("cross"), 1)
                fill(FILLS[7])
                on(pe, "w1_ready", h)
                pe.matmul(ps[:, 4, 0:P], XT[:, P:T], w1, start=True, stop=True).then_inc(done("sol1"), 1)
                fill(FILLS[7])
                on(pe, "vn_ready", h)
                pe.matmul(ps[:, 4, 0:T], vn[:, 0:P], AT[:, 0:T], start=True, stop=False, skip_group_check=True)
                pe.matmul(ps[:, 4, P:T], vn[:, P:T], AT[:, T:384], start=False, stop=True,
                          skip_group_check=True).then_inc(done("dn_out"), 1)
                fill(200)

            pe.wait_ge(s_hlo, 1)
            first = filling(tiles(0))
            first(KT)
            pe.wait_ge(s_keys, 32)
            for i in range(2):
                ins = pe.transpose(ps[:, 6, i * P:(i + 1) * P], keys_in[:, i, :], ident)
            ins.then_inc(p_keys, 1)
            for b in range(4, 8):
                turn_in(b)
            first(2 * KT)
            pe.wait_ge(d_hT, 8)
            pe.wait_ge(s_gate, 5)
            first(3 * KT)
            pe.wait_ge(s_hlo, 2)
            with pe.Fori(0, HEADS - 1) as h:
                head(h, tiles(h + 1))
            head(HEADS - 1, mem_tiles(HEADS))

            def mem_head(it, following):
                fill = filling(mem_gate_tiles(it), following)
                on(pe, "att_sq", it)
                for a in range(2):
                    for i in range(2):
                        ins = pe.matmul(ps[:, 3, a * T:(a + 1) * T], ones, msq[:, (2 * a + i) * T:(2 * a + i + 1) * T],
                                        start=(i == 0), stop=(i == 1))
                ins.then_inc(done("att_ss"), 1)
                on(pe, "dn_sq", it)
                on_before(pe, "att_kept", it)
                pe.matmul(ps[:, 6, :], ones, sqd, start=True, stop=True).then_inc(done("dn_ss"), 1)
                fill(MFILLS[0])
                on(pe, "att_qk", it)
                on(pe, "att_gain", it)
                for c in range(NC):
                    for i in range(2):
                        ins = pe.matmul(ps[:, 4, c * T:(c + 1) * T], mqk4[:, 0, i, c * P:(c + 1) * P], mqk4[:, 1, i, :],
                                        start=(i == 0), stop=(i == 1))
                ins.then_inc(done("scores"), 1)
                fill(MFILLS[1])
                on(pe, "pnorm", it)
                for m in range(NC):
                    for c in range(NC):
                        ins = pe.transpose(ps[:, 5, m * T + c * P:m * T + (c + 1) * P], mpr[:, c * T + m * P:c * T + (m + 1) * P], ident)
                ins.then_inc(done("p_turned"), 1)
                fill(MFILLS[2])
                on(pe, "pT_ready", it)
                on(pe, "mv_kept", it - HEADS)
                on(pe, "dn_std", it)
                for i in range(2):
                    for m in range(NC):
                        ins = pe.matmul(ps[:, 6, i * T:(i + 1) * T], mv[:, m * T + i * P:m * T + (i + 1) * P],
                                        mpT[:, m * T:(m + 1) * T], start=(m == 0), stop=(m == NC - 1))
                ins.then_inc(done("att_out"), 1)
                fill(200)

            with pe.Fori(HEADS, HEADS + MEM_HEADS - 1) as it:
                mem_head(it, mem_tiles(it + 1))
            mem_head(HEADS + MEM_HEADS - 1, ())

            pe.wait_ge(done("att_kept"), 1 + HEADS + MEM_HEADS)
            pe.wait_ge(done("dn_scaled"), MEM_HEADS)
            with pe.Fori(0, KT // 2) as mp:
                for j in range(2):
                    m = mp * 2 + j
                    pe.wait_ge(done("br_prod"), m + 1)
                    for n in range(3):
                        i = 3 * j + n
                        pe.wait_ge(s_blo, n + 1)
                        whole(tile("branch", mp, i, ps[:, i, 0:T], branch2[:, :, 8 * n:8 * n + 8, :]))
            pe.wait_ge(done("br_mix"), KT)
            pe.wait_ge(s_wo, 16 * KT)

            def output(c, n):
                for k in range(KT):
                    ins = pe.matmul(ps[:, 2 * c + n, :], mixT[:, k, c * P:(c + 1) * P], wo[:, k, n * 512:(n + 1) * 512],
                                    start=(k == 0), stop=(k == KT - 1))
                ins.then_inc(done("gdots"), 1)

            def turn_h2(c):
                pe.wait_ge(t_h2[c], 4)
                for half in range(2):
                    for k in range(4):
                        at = (4 * half + k) * P
                        ins = pe.transpose(ps[:, 2 * c + half, k * P:(k + 1) * P], h2[:, c, at:at + P], ident)
                    ins.then_inc(t_tr, 1)

            def route_pe(n, h, c):
                for k in range(KT):
                    ins = pe.matmul(ps[:, 4, 0:QW], h2T[:, k, c * P:(c + 1) * P], wq[k][:, bass.ds(h * QW, QW)], start=(k == 0), stop=(k == KT - 1))
                ins.then_inc(done("p_q"), 1)
                on(pe, "p_qk", n)
                for i in range(2):
                    ins = pe.transpose(ps[:, 5, i * P:(i + 1) * P], qtok[:, i * P:(i + 1) * P], ident)
                ins.then_inc(done("p_t"), 1)
                on(pe, "p_tk", n)
                for i in range(2):
                    ins = pe.matmul(ps[:, 6, i * NKEY:(i + 1) * NKEY], qT[:, i * P:(i + 1) * P], keysT[:, i * P:(i + 1) * P], start=True, stop=True)
                ins.then_inc(done("p_s"), 1)

            def rows_pe(n, c, last=False):
                for k in range(TOPK):
                    if k % 2 == 0:
                        pe.wait_ge(s_v[k % RING // 2], (n * 2 + (k // RING + 1)) * 32)
                    on(pe, "diag", n * TOPK + k)
                    for half in range(2):
                        ins = pe.matmul(ps[:, 2 * c + half, :], diag[:, k % 8, :], v_rows[k % RING][:, half * 512:(half + 1) * 512],
                                        start=False, stop=last and k == TOPK - 1, skip_group_check=True)
                    ins.then_inc(done("vrow"), 1)

            def open_sums(c):
                pe.wait_ge(t_h2[c], 6)
                for half in range(2):
                    pe.matmul(ps[:, 2 * c + half, :], mask[:, P:T], h2[:, c, 0:512], start=True, stop=False, skip_group_check=True)

            output(0, 0)
            output(0, 1)
            output(1, 0)
            turn_h2(0)
            pe.wait_ge(s_wq[0], 16 * KT)
            pe.wait_ge(t_h2[0], 6)
            route_pe(0, 0, 0)
            output(1, 1)
            pe.sem_inc(done("vrow"), RING)
            turn_h2(1)
            pe.wait_ge(t_h2[1], 6)
            route_pe(1, 0, 1)
            open_sums(0)
            open_sums(1)
            pe.wait_ge(s_wq[1], 16 * KT)
            with pe.Fori(0, PHEADS - 1) as h:
                route_pe(h * NC + 2, h + 1, 0)
                rows_pe(h * NC, 0)
                route_pe(h * NC + 3, h + 1, 1)
                rows_pe(h * NC + 1, 1)
            rows_pe(UNITS - 2, 0, True)
            rows_pe(UNITS - 1, 1, True)
            pe.wait_ge(done("vrow"), RING + UNITS * TOPK)
            pe.sem_inc(done("vmm_end"), 1)


_INS = ["x", "mem", "attn_norm_g", "mem_norm_g", "ffn_norm_g", "w_in", "moba_q_norm_g", "moba_k_norm_g", "dn_conv_w",
        "dn_a_log", "dn_dt_bias", "dn_out_norm_g", "w_mem_kv", "mem_q_norm_g", "mem_k_norm_g", "w_branch", "w_out",
        "peer_w_q", "peer_keys1", "peer_keys2", "peer_u", "peer_v"]


def kernel(**inputs):
    import concourse.bacc as bacc
    from concourse.bass_utils import run_bass_kernel_spmd

    nc = bacc.Bacc("TRN2", target_bir_lowering=False, num_devices=1)
    table, where = constants()
    arrays = {"constants_dram": table}
    d = {}
    for name in _INS:
        a = np.ascontiguousarray(inputs[name])
        arrays[f"in_{name}_dram"] = a
        d[name] = nc.dram_tensor(f"in_{name}_dram", a.shape, mybir.dt.from_np(a.dtype), kind="ExternalInput").ap()
    cst = nc.dram_tensor("constants_dram", table.shape, F32, kind="ExternalInput").ap()
    out = nc.dram_tensor("out_dram", (1, T, D), F32, kind="ExternalOutput").ap()

    def as_rows(name):
        return d[name].rearrange("o (r c) -> (o r) c", c=P)

    rows = [(R_CONV, d["dn_conv_w"].rearrange("o j (r c) -> (o j r) c", c=P)), (R_ATTN, as_rows("attn_norm_g")),
            (R_MEM, as_rows("mem_norm_g")), (R_MQ, as_rows("moba_q_norm_g")), (R_MK, as_rows("moba_k_norm_g")),
            (R_DN, as_rows("dn_out_norm_g")), (R_CQ, as_rows("mem_q_norm_g")), (R_CK, as_rows("mem_k_norm_g"))]
    hybrid_layer(nc, cst, where, d["x"][0], d["mem"][0], rows, d["w_in"][0], d["dn_a_log"][0], d["dn_dt_bias"][0],
                 d["ffn_norm_g"][0], d["w_mem_kv"][0], d["w_branch"][0], d["w_out"][0], d["peer_w_q"][0],
                 d["peer_keys1"][0], d["peer_keys2"][0], d["peer_u"][0], d["peer_v"][0], out[0])
    r = run_bass_kernel_spmd(nc, [arrays], core_ids=[0])
    return r.results[0]["out_dram"]
```
